# Optimizing a Trainium2 kernel written in Bass

```python
import math
import jax, jax.numpy as jnp
from jax import lax
import numpy as np

D_MODEL = 1024
BATCH = 1
SEQ = 512
DEPTH = 2

D_FF = 2816
MLSTM_HEADS = 4
MLSTM_HEAD_DIM = 64
MLSTM_WIDTH = MLSTM_HEADS * MLSTM_HEAD_DIM
MLSTM_CHUNK = 64
SSM_HEADS = 8
SSM_HEAD_DIM = 64
SSM_WIDTH = SSM_HEADS * SSM_HEAD_DIM
SSM_STATE = 128
SSM_GROUPS = 2
SSM_CONV = 4
SSM_CONV_DIM = SSM_WIDTH + 2 * SSM_GROUPS * SSM_STATE
SSM_CHUNK = 128
DIFF_HEADS = 4
DIFF_QK_DIM = 32
DIFF_V_DIM = 64
DIFF_WIDTH = DIFF_HEADS * DIFF_V_DIM
Q_BLOCK = 128
REL_BUCKETS = 32
REL_MAX_DIST = 128
D_MIX = MLSTM_WIDTH + SSM_WIDTH + DIFF_WIDTH
IN_SPLIT_SIZES = (MLSTM_WIDTH, MLSTM_WIDTH, MLSTM_WIDTH, MLSTM_WIDTH, MLSTM_HEADS, MLSTM_HEADS,
                  SSM_WIDTH, SSM_CONV_DIM, SSM_HEADS,
                  2 * DIFF_HEADS * DIFF_QK_DIM, 2 * DIFF_HEADS * DIFF_QK_DIM, DIFF_WIDTH)
D_IN = sum(IN_SPLIT_SIZES)
NORM_EPS = 1e-6


def rms_norm(x, w):
    xf = x.astype(jnp.float32)
    y = xf * lax.rsqrt(jnp.mean(xf * xf, axis=-1, keepdims=True) + NORM_EPS)
    return (y * w.astype(jnp.float32)).astype(x.dtype)

def swiglu_ffn(x, w_gate, w_up, w_down):
    return (jax.nn.silu(x @ w_gate) * (x @ w_up)) @ w_down

def t5_bucket(rel):
    n = jnp.maximum(rel, 0)
    max_exact = REL_BUCKETS // 2
    nf = jnp.maximum(n, 1).astype(jnp.float32)
    large = max_exact + (jnp.log(nf / max_exact) / math.log(REL_MAX_DIST / max_exact)
                         * (REL_BUCKETS - max_exact)).astype(jnp.int32)
    large = jnp.minimum(large, REL_BUCKETS - 1)
    return jnp.where(n < max_exact, n, large)

def causal_dwconv(x, w, b):
    K, C = w.shape
    y = lax.conv_general_dilated(x, w[:, None, :], window_strides=(1,), padding=((K - 1, 0),),
                                 dimension_numbers=('NWC', 'WIO', 'NWC'), feature_group_count=C)
    return y + b

def mlstm_chunkwise(q, k, v, i_pre, log_f):
    Bsz, H, S, DK = q.shape
    DV = v.shape[-1]
    L = MLSTM_CHUNK
    nc = S // L

    def to_chunks(a):
        return jnp.moveaxis(a.reshape(a.shape[:2] + (nc, L) + a.shape[3:]), 2, 0)

    causal = jnp.tril(jnp.ones((L, L), dtype=bool))

    def step(carry, inp):
        C, n, m = carry
        qc, kc, vc, ic, fc = inp
        b = jnp.cumsum(fc, axis=-1)
        log_d = jnp.where(causal, b[..., :, None] - b[..., None, :] + ic[..., None, :], -jnp.inf)
        m_inter = b + m[..., None]
        m_t = jnp.maximum(m_inter, jnp.max(log_d, axis=-1))
        d = jnp.exp(log_d - m_t[..., None])
        inter = jnp.exp(m_inter - m_t)
        s = jnp.einsum('bhtd,bhsd->bhts', qc, kc) * d
        num = jnp.einsum('bhts,bhsv->bhtv', s, vc) + inter[..., None] * jnp.einsum('bhtd,bhdv->bhtv', qc, C)
        den = jnp.sum(s, axis=-1) + inter * jnp.einsum('bhtd,bhd->bht', qc, n)
        h = num / jnp.maximum(jnp.abs(den), jnp.exp(-m_t))[..., None]
        b_last = b[..., -1]
        log_w = b_last[..., None] - b + ic
        m_new = jnp.maximum(b_last + m, jnp.max(log_w, axis=-1))
        w = jnp.exp(log_w - m_new[..., None])
        decay = jnp.exp(b_last + m - m_new)
        C_new = decay[..., None, None] * C + jnp.einsum('bhs,bhsd,bhsv->bhdv', w, kc, vc)
        n_new = decay[..., None] * n + jnp.einsum('bhs,bhsd->bhd', w, kc)
        return (C_new, n_new, m_new), h

    init = (jnp.zeros((Bsz, H, DK, DV), jnp.float32), jnp.zeros((Bsz, H, DK), jnp.float32),
            jnp.zeros((Bsz, H), jnp.float32))
    xs = (to_chunks(q), to_chunks(k), to_chunks(v), to_chunks(i_pre), to_chunks(log_f))
    _, h = lax.scan(step, init, xs)
    return jnp.moveaxis(h, 0, 2).reshape(Bsz, H, S, DV)

def ssd_chunked(x, dt, A, Bm, Cm):
    Bsz, S, H, P = x.shape
    N = Bm.shape[-1]
    L = SSM_CHUNK
    nc = S // L
    xc = (x * dt[..., None]).reshape(Bsz, nc, L, H, P)
    Bc = Bm.reshape(Bsz, nc, L, H, N)
    Cc = Cm.reshape(Bsz, nc, L, H, N)
    a_cs = jnp.cumsum((dt * A).reshape(Bsz, nc, L, H).transpose(0, 3, 1, 2), axis=-1)
    causal = jnp.tril(jnp.ones((L, L), dtype=bool))
    seg = jnp.exp(jnp.where(causal, a_cs[..., :, None] - a_cs[..., None, :], -jnp.inf))
    scores = jnp.einsum('bclhn,bcshn->bhcls', Cc, Bc) * seg
    y_diag = jnp.einsum('bhcls,bcshp->bclhp', scores, xc)
    decay_in = jnp.exp(a_cs[..., -1:] - a_cs)
    states = jnp.einsum('bcshn,bhcs,bcshp->bchpn', Bc, decay_in, xc)
    chunk_decay = jnp.exp(a_cs[..., -1])

    def step(s, inp):
        st, dec = inp
        return dec[..., None, None] * s + st, s

    _, prev = lax.scan(step, jnp.zeros((Bsz, H, P, N), jnp.float32),
                       (jnp.moveaxis(states, 1, 0), jnp.moveaxis(chunk_decay, 2, 0)))
    prev = jnp.moveaxis(prev, 0, 1)
    y_off = jnp.einsum('bclhn,bchpn,bhcl->bclhp', Cc, prev, jnp.exp(a_cs))
    return (y_diag + y_off).reshape(Bsz, S, H, P)

def diff_attention(q, k, v, rel_bias, lam):
    Bsz, H, S = q.shape[:3]
    DV = v.shape[-1]
    nb = S // Q_BLOCK
    scale = DIFF_QK_DIM ** -0.5
    k1 = k[..., 0, :]
    k2 = k[..., 1, :]
    qb = jnp.moveaxis(q.reshape(Bsz, H, nb, Q_BLOCK, 2, DIFF_QK_DIM), 2, 0)
    k_pos = jnp.arange(S)

    def block(args):
        qblk, bi = args
        q_pos = bi * Q_BLOCK + jnp.arange(Q_BLOCK)
        rel = q_pos[:, None] - k_pos[None, :]
        mask = rel >= 0
        bias = jnp.moveaxis(rel_bias[t5_bucket(rel)], -1, 0).astype(jnp.float32)

        def probs(qi, ki):
            logits = jnp.einsum('bhqd,bhkd->bhqk', qi, ki).astype(jnp.float32) * scale + bias
            return jax.nn.softmax(jnp.where(mask, logits, -jnp.inf), axis=-1)

        a = probs(qblk[..., 0, :], k1) - lam * probs(qblk[..., 1, :], k2)
        return jnp.einsum('bhqk,bhkv->bhqv', a.astype(v.dtype), v)

    out = lax.map(block, (qb, jnp.arange(nb)))
    return jnp.moveaxis(out, 0, 2).reshape(Bsz, H, S, DV)

def hybrid_mixer(h, layer_idx, w_in, w_out, mlstm_gate_bias, mlstm_norm_w, conv_w, conv_b,
                 dt_bias, A_log, D_skip, ssm_norm_w, q_norm_w, k_norm_w, lambdas, subln_w, rel_bias):
    Bsz, S, _ = h.shape
    f32 = jnp.float32
    proj = h @ w_in
    split_idx = np.cumsum(IN_SPLIT_SIZES)[:-1].tolist()
    mq, mk, mv, mo, mi, mf, z, xbc, dt_raw, dq, dk, dv = jnp.split(proj, split_idx, axis=-1)

    def heads(a, nh):
        return a.reshape(Bsz, S, nh, -1).transpose(0, 2, 1, 3)

    i_pre = (mi + mlstm_gate_bias[0]).astype(f32).transpose(0, 2, 1)
    log_f = jax.nn.log_sigmoid((mf + mlstm_gate_bias[1]).astype(f32)).transpose(0, 2, 1)
    hm = mlstm_chunkwise(heads(mq, MLSTM_HEADS).astype(f32),
                         heads(mk, MLSTM_HEADS).astype(f32) * (MLSTM_HEAD_DIM ** -0.5),
                         heads(mv, MLSTM_HEADS).astype(f32), i_pre, log_f)
    hm = rms_norm(hm.transpose(0, 2, 1, 3), mlstm_norm_w.reshape(MLSTM_HEADS, MLSTM_HEAD_DIM))
    y_mlstm = jax.nn.sigmoid(mo) * hm.reshape(Bsz, S, MLSTM_WIDTH).astype(h.dtype)

    xbc = jax.nn.silu(causal_dwconv(xbc, conv_w, conv_b))
    xs, Bm, Cm = jnp.split(xbc, [SSM_WIDTH, SSM_WIDTH + SSM_GROUPS * SSM_STATE], axis=-1)
    xs = xs.reshape(Bsz, S, SSM_HEADS, SSM_HEAD_DIM).astype(f32)
    rep = SSM_HEADS // SSM_GROUPS
    Bm = jnp.repeat(Bm.reshape(Bsz, S, SSM_GROUPS, SSM_STATE), rep, axis=2).astype(f32)
    Cm = jnp.repeat(Cm.reshape(Bsz, S, SSM_GROUPS, SSM_STATE), rep, axis=2).astype(f32)
    dt = jax.nn.softplus((dt_raw + dt_bias).astype(f32))
    A = -jnp.exp(A_log.astype(f32))
    y = ssd_chunked(xs, dt, A, Bm, Cm) + D_skip.astype(f32)[:, None] * xs
    y = y.reshape(Bsz, S, SSM_WIDTH).astype(h.dtype) * jax.nn.silu(z)
    y_ssm = rms_norm(y.reshape(Bsz, S, SSM_GROUPS, -1),
                     ssm_norm_w.reshape(SSM_GROUPS, -1)).reshape(Bsz, S, SSM_WIDTH)

    dq = rms_norm(dq.reshape(Bsz, S, DIFF_HEADS, 2, DIFF_QK_DIM), q_norm_w).transpose(0, 2, 1, 3, 4)
    dk = rms_norm(dk.reshape(Bsz, S, DIFF_HEADS, 2, DIFF_QK_DIM), k_norm_w).transpose(0, 2, 1, 3, 4)
    dv = heads(dv, DIFF_HEADS)
    lam_init = 0.8 - 0.6 * math.exp(-0.3 * layer_idx)
    lf = lambdas.astype(f32)
    lam = jnp.exp(jnp.sum(lf[0] * lf[1])) - jnp.exp(jnp.sum(lf[2] * lf[3])) + lam_init
    o = diff_attention(dq, dk, dv, rel_bias, lam)
    o = rms_norm(o.transpose(0, 2, 1, 3), subln_w) * (1.0 - lam_init)
    y_diff = o.reshape(Bsz, S, DIFF_WIDTH)

    return jnp.concatenate([y_mlstm, y_ssm, y_diff], axis=-1) @ w_out

def first_inputs(seed: int = 0) -> dict:
    key = jax.random.key(seed)
    ks = jax.random.split(key, 32)
    L = DEPTH
    f32 = jnp.float32

    def nrm(i, shape, scale):
        return scale * jax.random.normal(ks[i], shape, f32)

    def gain(i, shape):
        return 1.0 + 0.1 * jax.random.normal(ks[i], shape, f32)

    x = jax.random.normal(ks[0], (BATCH, SEQ, D_MODEL), f32)
    ffn1_norm_w = gain(1, (L, D_MODEL))
    ffn1_w_gate = nrm(2, (L, D_MODEL, D_FF), D_MODEL ** -0.5)
    ffn1_w_up = nrm(3, (L, D_MODEL, D_FF), D_MODEL ** -0.5)
    ffn1_w_down = nrm(4, (L, D_FF, D_MODEL), D_FF ** -0.5)
    mix_norm_w = gain(5, (L, D_MODEL))
    w_in = nrm(6, (L, D_MODEL, D_IN), D_MODEL ** -0.5)
    mlstm_gate_bias = jnp.stack([nrm(7, (L, MLSTM_HEADS), 0.1),
                                 jnp.linspace(3.0, 6.0, MLSTM_HEADS)[None, :] + nrm(8, (L, MLSTM_HEADS), 0.1)],
                                axis=1)
    mlstm_norm_w = gain(9, (L, MLSTM_WIDTH))
    ssm_conv_w = nrm(10, (L, SSM_CONV, SSM_CONV_DIM), SSM_CONV ** -0.5)
    ssm_conv_b = nrm(11, (L, SSM_CONV_DIM), 0.01)
    dt0 = jnp.exp(jax.random.uniform(ks[12], (L, SSM_HEADS), f32, math.log(1e-3), math.log(1e-1)))
    ssm_dt_bias = dt0 + jnp.log(-jnp.expm1(-dt0))
    ssm_A_log = jnp.log(jax.random.uniform(ks[13], (L, SSM_HEADS), f32, 1.0, 16.0))
    ssm_D = gain(14, (L, SSM_HEADS))
    ssm_norm_w = gain(15, (L, SSM_WIDTH))
    diff_q_norm_w = gain(16, (L, 2, DIFF_QK_DIM))
    diff_k_norm_w = gain(17, (L, 2, DIFF_QK_DIM))
    diff_lambda = nrm(18, (L, 4, DIFF_QK_DIM), 0.1)
    diff_subln_w = gain(19, (L, DIFF_V_DIM))
    rel_bias = nrm(20, (REL_BUCKETS, DIFF_HEADS), 0.5)
    w_out = nrm(21, (L, D_MIX, D_MODEL), D_MIX ** -0.5)
    ffn2_norm_w = gain(22, (L, D_MODEL))
    ffn2_w_gate = nrm(23, (L, D_MODEL, D_FF), D_MODEL ** -0.5)
    ffn2_w_up = nrm(24, (L, D_MODEL, D_FF), D_MODEL ** -0.5)
    ffn2_w_down = nrm(25, (L, D_FF, D_MODEL), D_FF ** -0.5)
    return {'x': x, 'ffn1_norm_w': ffn1_norm_w, 'ffn1_w_gate': ffn1_w_gate, 'ffn1_w_up': ffn1_w_up,
            'ffn1_w_down': ffn1_w_down, 'mix_norm_w': mix_norm_w, 'w_in': w_in,
            'mlstm_gate_bias': mlstm_gate_bias, 'mlstm_norm_w': mlstm_norm_w,
            'ssm_conv_w': ssm_conv_w, 'ssm_conv_b': ssm_conv_b, 'ssm_dt_bias': ssm_dt_bias,
            'ssm_A_log': ssm_A_log, 'ssm_D': ssm_D, 'ssm_norm_w': ssm_norm_w,
            'diff_q_norm_w': diff_q_norm_w, 'diff_k_norm_w': diff_k_norm_w, 'diff_lambda': diff_lambda,
            'diff_subln_w': diff_subln_w, 'rel_bias': rel_bias, 'w_out': w_out,
            'ffn2_norm_w': ffn2_norm_w, 'ffn2_w_gate': ffn2_w_gate, 'ffn2_w_up': ffn2_w_up,
            'ffn2_w_down': ffn2_w_down}

def first_block(x, ffn1_norm_w, ffn1_w_gate, ffn1_w_up, ffn1_w_down, mix_norm_w, w_in,
              mlstm_gate_bias, mlstm_norm_w, ssm_conv_w, ssm_conv_b, ssm_dt_bias, ssm_A_log, ssm_D,
              ssm_norm_w, diff_q_norm_w, diff_k_norm_w, diff_lambda, diff_subln_w, rel_bias, w_out,
              ffn2_norm_w, ffn2_w_gate, ffn2_w_up, ffn2_w_down):
    for l in range(DEPTH):
        x = x + 0.5 * swiglu_ffn(rms_norm(x, ffn1_norm_w[l]), ffn1_w_gate[l], ffn1_w_up[l], ffn1_w_down[l])
        x = x + hybrid_mixer(rms_norm(x, mix_norm_w[l]), l, w_in[l], w_out[l],
                             mlstm_gate_bias[l], mlstm_norm_w[l], ssm_conv_w[l], ssm_conv_b[l],
                             ssm_dt_bias[l], ssm_A_log[l], ssm_D[l], ssm_norm_w[l],
                             diff_q_norm_w[l], diff_k_norm_w[l], diff_lambda[l], diff_subln_w[l],
                             rel_bias)
        x = x + 0.5 * swiglu_ffn(rms_norm(x, ffn2_norm_w[l]), ffn2_w_gate[l], ffn2_w_up[l], ffn2_w_down[l])
    return x


DEPTH_2 = 1

BRANCH_WIDTH = D_MODEL
N_BRANCH = 3
EPS = 1e-6
NEG_INF = -1e30
FORCED = 1e4

LRU_WIDTH = BRANCH_WIDTH
LRU_BLOCKS = 8
LRU_BLOCK = LRU_WIDTH // LRU_BLOCKS
CONV_WIDTH = 4
LRU_C = 8.0

NSA_HEADS = 16
NSA_KV_HEADS = 4
NSA_GROUP = NSA_HEADS // NSA_KV_HEADS
NSA_HEAD_DIM = BRANCH_WIDTH // NSA_HEADS
NSA_WIDTH = NSA_HEADS * NSA_HEAD_DIM
CMP_BLOCK = 32
CMP_STRIDE = 16
CMP_HIDDEN = 256
SLC_BLOCK = 64
SLC_TOP_N = 8
SLC_Q_BLOCK = 64
WINDOW = 256

GLA_HEADS = 4
GLA_KEY_WIDTH = D_MODEL // 2
GLA_VALUE_WIDTH = BRANCH_WIDTH
GLA_DK = GLA_KEY_WIDTH // GLA_HEADS
GLA_DV = GLA_VALUE_WIDTH // GLA_HEADS
GLA_GATE_RANK = 16
GLA_TAU = 16.0
GLA_CHUNK = 32

REL_MAX_EXACT = 16

D_FF_2 = -(-8 * D_MODEL // (3 * 256)) * 256

IN_SIZES = (
    LRU_WIDTH,
    LRU_WIDTH,
    NSA_WIDTH,
    6 * NSA_KV_HEADS * NSA_HEAD_DIM,
    3 * NSA_HEADS,
    GLA_KEY_WIDTH,
    GLA_KEY_WIDTH,
    GLA_VALUE_WIDTH,
    GLA_VALUE_WIDTH,
    GLA_GATE_RANK,
    N_BRANCH * D_MODEL,
)
IN_WIDTH = sum(IN_SIZES)


def rms_norm_2(x, g):
    xf = x.astype(jnp.float32)
    y = xf * lax.rsqrt(jnp.mean(xf * xf, axis=-1, keepdims=True) + EPS)
    return (y * g.astype(jnp.float32)).astype(x.dtype)

def rel_bucket(dist):
    n = jnp.maximum(dist, 0)
    nf = jnp.maximum(n, REL_MAX_EXACT).astype(jnp.float32)
    large = REL_MAX_EXACT + (jnp.log(nf / REL_MAX_EXACT) / math.log(REL_MAX_DIST / REL_MAX_EXACT)
                             * (REL_BUCKETS - REL_MAX_EXACT)).astype(jnp.int32)
    large = jnp.minimum(large, REL_BUCKETS - 1)
    return jnp.where(n < REL_MAX_EXACT, n, large)

def rglru_mixer(xa, ga, conv_w, conv_b, w_gates, b_gates, lam):
    B_, S_, _ = xa.shape
    f32 = jnp.float32
    xc = lax.conv_general_dilated(
        xa, conv_w[:, None, :].astype(xa.dtype), window_strides=(1,),
        padding=[(CONV_WIDTH - 1, 0)], dimension_numbers=("NWC", "WIO", "NWC"),
        feature_group_count=LRU_WIDTH) + conv_b
    xb = xc.reshape(B_, S_, LRU_BLOCKS, LRU_BLOCK)
    gates = jnp.einsum("bsnc,knce->kbsne", xb, w_gates).reshape(2, B_, S_, LRU_WIDTH) + b_gates[:, None, None, :]
    r = jax.nn.sigmoid(gates[0].astype(f32))
    i = jax.nn.sigmoid(gates[1].astype(f32))
    log_a = -LRU_C * r * jax.nn.softplus(-lam.astype(f32))
    a = jnp.exp(log_a)
    u = jnp.sqrt(-jnp.expm1(2.0 * log_a)) * (i * xc.astype(f32))

    def combine(left, right):
        a1, b1 = left
        a2, b2 = right
        return a1 * a2, a2 * b1 + b2

    _, h = lax.associative_scan(combine, (a, u), axis=1)
    return h.astype(xa.dtype) * jax.nn.gelu(ga)

def compress_blocks(t, pos_emb, w1, w2):
    B_, G_, S_, hd = t.shape
    r = CMP_BLOCK // CMP_STRIDE
    n_cmp = S_ // CMP_STRIDE - r + 1
    ch = t.reshape(B_, G_, S_ // CMP_STRIDE, CMP_STRIDE, hd)
    blocks = jnp.concatenate([ch[:, :, j:j + n_cmp] for j in range(r)], axis=3) + pos_emb
    return jax.nn.gelu(blocks.reshape(B_, G_, n_cmp, CMP_BLOCK * hd) @ w1) @ w2

def nsa_mixer(q, kv, gate, rel_table, cmp_pos, cmp_w1, cmp_w2):
    B_, S_, _ = q.shape
    G, R, hd = NSA_KV_HEADS, NSA_GROUP, NSA_HEAD_DIM
    f32 = jnp.float32
    q = q.reshape(B_, S_, G, R, hd).transpose(0, 2, 3, 1, 4) * (hd ** -0.5)
    kv = kv.reshape(B_, S_, 6, G, hd).transpose(2, 0, 3, 1, 4)
    k_cmp, v_cmp, k_slc, v_slc, k_win, v_win = kv[0], kv[1], kv[2], kv[3], kv[4], kv[5]
    tbl = rel_table.reshape(REL_BUCKETS, G, R)
    pos = jnp.arange(S_)

    kc = compress_blocks(k_cmp, cmp_pos[0], cmp_w1[0], cmp_w2[0])
    vc = compress_blocks(v_cmp, cmp_pos[1], cmp_w1[1], cmp_w2[1])
    n_cmp = kc.shape[2]
    cmp_end = jnp.arange(n_cmp) * CMP_STRIDE + CMP_BLOCK - 1
    valid_c = cmp_end[None, :] <= pos[:, None]
    bias_c = tbl[rel_bucket(pos[:, None] - cmp_end[None, :])].transpose(2, 3, 0, 1)
    logit_c = jnp.einsum("bgrsd,bgcd->bgrsc", q, kc).astype(f32) + bias_c
    p_c = jax.nn.softmax(jnp.where(valid_c, logit_c, NEG_INF), axis=-1) * valid_c
    o_cmp = jnp.einsum("bgrsc,bgcd->bgrsd", p_c.astype(q.dtype), vc)

    n_slc = S_ // SLC_BLOCK
    top_n = min(SLC_TOP_N, n_slc)
    slc_start = jnp.arange(n_slc) * SLC_BLOCK
    cmp_start = cmp_end - (CMP_BLOCK - 1)
    overlap = jnp.clip(jnp.minimum(cmp_start[:, None] + CMP_BLOCK, slc_start[None, :] + SLC_BLOCK)
                       - jnp.maximum(cmp_start[:, None], slc_start[None, :]), 0).astype(f32) / CMP_BLOCK
    imp = jnp.einsum("bgrsc,cj->bgsj", p_c, overlap)
    blk = jnp.arange(n_slc)[None, :]
    cur = (pos // SLC_BLOCK)[:, None]
    forced = (blk == 0) | (blk == cur) | (blk == cur - 1)
    score = jnp.where(forced, FORCED, jnp.where(blk <= cur, imp, -FORCED))
    _, sel = lax.top_k(score, top_n)

    kb = k_slc.reshape(B_, G, n_slc, SLC_BLOCK, hd)
    vb = v_slc.reshape(B_, G, n_slc, SLC_BLOCK, hd)
    nqs = S_ // SLC_Q_BLOCK
    q_blk = q.reshape(B_, G, R, nqs, SLC_Q_BLOCK, hd).transpose(3, 0, 1, 2, 4, 5)
    sel_blk = sel.reshape(B_, G, nqs, SLC_Q_BLOCK, top_n).transpose(2, 0, 1, 3, 4)
    bi = jnp.arange(B_)[:, None, None, None]
    gi = jnp.arange(G)[None, :, None, None]
    gi5 = jnp.arange(G)[None, :, None, None, None]
    tbl_g = tbl.transpose(1, 0, 2)

    def slc_block(args):
        qb, sb, start = args
        ks = kb[bi, gi, sb]
        vs = vb[bi, gi, sb]
        tq = start + jnp.arange(SLC_Q_BLOCK)
        tk = sb[..., None] * SLC_BLOCK + jnp.arange(SLC_BLOCK)
        dist = tq[:, None, None] - tk
        bias = tbl_g[gi5, rel_bucket(dist)].transpose(0, 1, 5, 2, 3, 4)
        logit = jnp.einsum("bgrqd,bgqnld->bgrqnl", qb, ks).astype(f32) + bias
        logit = jnp.where((dist >= 0)[:, :, None], logit, NEG_INF)
        p = jax.nn.softmax(logit.reshape(B_, G, R, SLC_Q_BLOCK, top_n * SLC_BLOCK), axis=-1)
        p = p.reshape(B_, G, R, SLC_Q_BLOCK, top_n, SLC_BLOCK)
        return jnp.einsum("bgrqnl,bgqnld->bgrqd", p.astype(qb.dtype), vs)

    o_slc = lax.map(slc_block, (q_blk, sel_blk, jnp.arange(nqs) * SLC_Q_BLOCK))
    o_slc = o_slc.transpose(1, 2, 3, 0, 4, 5).reshape(B_, G, R, S_, hd)

    nqb = S_ // Q_BLOCK
    nband = WINDOW // Q_BLOCK + 1

    def band(t):
        tp = jnp.pad(t, ((0, 0), (0, 0), ((nband - 1) * Q_BLOCK, 0), (0, 0)))
        tb = tp.reshape(B_, G, nqb + nband - 1, Q_BLOCK, hd)
        return jnp.concatenate([tb[:, :, j:j + nqb] for j in range(nband)], axis=3)

    kw, vw = band(k_win), band(v_win)
    qi = jnp.arange(Q_BLOCK)
    kj = jnp.arange(nband * Q_BLOCK)
    dist_w = (nband - 1) * Q_BLOCK + qi[:, None] - kj[None, :]
    key_pos = jnp.arange(nqb)[:, None] * Q_BLOCK - (nband - 1) * Q_BLOCK + kj[None, :]
    mask_w = ((dist_w >= 0) & (dist_w < WINDOW))[None] & (key_pos >= 0)[:, None, :]
    bias_w = tbl[rel_bucket(dist_w)].transpose(2, 3, 0, 1)[:, :, None]
    qw = q.reshape(B_, G, R, nqb, Q_BLOCK, hd)
    logit_w = jnp.einsum("bgrnqd,bgnkd->bgrnqk", qw, kw).astype(f32) + bias_w
    p_w = jax.nn.softmax(jnp.where(mask_w, logit_w, NEG_INF), axis=-1)
    o_win = jnp.einsum("bgrnqk,bgnkd->bgrnqd", p_w.astype(q.dtype), vw).reshape(B_, G, R, S_, hd)

    g = jax.nn.sigmoid(gate).reshape(B_, S_, 3, G, R).transpose(2, 0, 3, 4, 1)[..., None]
    o = g[0] * o_cmp + g[1] * o_slc + g[2] * o_win
    return o.transpose(0, 3, 1, 2, 4).reshape(B_, S_, NSA_WIDTH)

def gla_mixer(q, k, v, og, lr, wa2, ba, norm_g):
    B_, S_, _ = q.shape
    f32 = jnp.float32
    nc = S_ // GLA_CHUNK
    log_alpha = jax.nn.log_sigmoid((lr @ wa2 + ba).astype(f32)) / GLA_TAU

    def heads(t, d):
        return t.reshape(B_, nc, GLA_CHUNK, GLA_HEADS, d).transpose(1, 0, 3, 2, 4).astype(f32)

    qh = heads(q, GLA_DK) * (GLA_DK ** -0.5)
    kh = heads(k, GLA_DK)
    vh = heads(v, GLA_DV)
    b = jnp.cumsum(heads(log_alpha, GLA_DK), axis=3)
    q_t = qh * jnp.exp(b)
    k_t = kh * jnp.exp(-b)
    b_last = b[:, :, :, -1:]
    k_end = kh * jnp.exp(b_last - b)
    decay = jnp.exp(b_last[:, :, :, 0])
    causal = jnp.tril(jnp.ones((GLA_CHUNK, GLA_CHUNK), bool))
    att = jnp.where(causal, jnp.einsum("nbhcd,nbhsd->nbhcs", q_t, k_t), 0.0)
    o_intra = jnp.einsum("nbhcs,nbhse->nbhce", att, vh)

    def step(state, xs):
        q_c, ke_c, v_c, dec_c = xs
        o = jnp.einsum("bhcd,bhde->bhce", q_c, state)
        state = state * dec_c[..., None] + jnp.einsum("bhcd,bhce->bhde", ke_c, v_c)
        return state, o

    s0 = jnp.zeros((B_, GLA_HEADS, GLA_DK, GLA_DV), f32)
    _, o_inter = lax.scan(step, s0, (q_t, k_end, vh, decay))
    o = rms_norm_2(o_intra + o_inter, norm_g)
    o = o.transpose(1, 0, 3, 2, 4).reshape(B_, S_, GLA_VALUE_WIDTH)
    return o.astype(og.dtype) * jax.nn.silu(og)

def hybrid_layer(x, rel_table, norm_g, w_in, conv_w, conv_b, lru_w_gates, lru_b_gates, lru_lambda,
                 cmp_pos, cmp_w1, cmp_w2, gla_wa2, gla_ba, gla_norm, w_branch, w_out, w_ffn_in, w_ffn_out):
    B_, S_, D_ = x.shape
    h = rms_norm_2(x, norm_g[0])
    proj = h @ w_in
    cuts, acc = [], 0
    for size in IN_SIZES[:-1]:
        acc += size
        cuts.append(acc)
    (lru_x, lru_g, nsa_q, nsa_kv, nsa_gate, gla_q, gla_k, gla_v, gla_og, gla_lr,
     merge_logit) = jnp.split(proj, cuts, axis=-1)
    y_a = rglru_mixer(lru_x, lru_g, conv_w, conv_b, lru_w_gates, lru_b_gates, lru_lambda)
    y_b = nsa_mixer(nsa_q, nsa_kv, nsa_gate, rel_table, cmp_pos, cmp_w1, cmp_w2)
    y_c = gla_mixer(gla_q, gla_k, gla_v, gla_og, gla_lr, gla_wa2, gla_ba, gla_norm)
    gates = jax.nn.sigmoid(merge_logit.reshape(B_, S_, N_BRANCH, D_))
    merged = (gates[:, :, 0] * (y_a @ w_branch[0])
              + gates[:, :, 1] * (y_b @ w_branch[1])
              + gates[:, :, 2] * (y_c @ w_branch[2]))
    x = x + rms_norm_2(merged @ w_out, norm_g[1])
    h = rms_norm_2(x, norm_g[2])
    gt, up = jnp.split(h @ w_ffn_in, 2, axis=-1)
    x = x + rms_norm_2((jax.nn.silu(gt) * up) @ w_ffn_out, norm_g[3])
    return x

def second_inputs(seed: int = 0) -> dict:
    key = jax.random.key(seed)
    ks = jax.random.split(key, 20)
    f32 = jnp.float32

    def nrm(k, shape, scale):
        return jax.random.normal(k, shape, f32) * scale

    u = jax.random.uniform(ks[8], (DEPTH_2, LRU_WIDTH), f32, 0.9, 0.999)
    s = u ** (1.0 / LRU_C)
    return {
        "x": nrm(ks[0], (BATCH, SEQ, D_MODEL), 1.0),
        "rel_table": nrm(ks[1], (REL_BUCKETS, NSA_HEADS), 0.5),
        "norm_g": 1.0 + nrm(ks[2], (DEPTH_2, 4, D_MODEL), 0.05),
        "w_in": nrm(ks[3], (DEPTH_2, D_MODEL, IN_WIDTH), D_MODEL ** -0.5),
        "conv_w": nrm(ks[4], (DEPTH_2, CONV_WIDTH, LRU_WIDTH), CONV_WIDTH ** -0.5),
        "conv_b": nrm(ks[5], (DEPTH_2, LRU_WIDTH), 0.01),
        "lru_w_gates": nrm(ks[6], (DEPTH_2, 2, LRU_BLOCKS, LRU_BLOCK, LRU_BLOCK), LRU_BLOCK ** -0.5),
        "lru_b_gates": nrm(ks[7], (DEPTH_2, 2, LRU_WIDTH), 0.01),
        "lru_lambda": jnp.log(s) - jnp.log1p(-s),
        "cmp_pos": nrm(ks[9], (DEPTH_2, 2, CMP_BLOCK, NSA_HEAD_DIM), 0.1),
        "cmp_w1": nrm(ks[10], (DEPTH_2, 2, CMP_BLOCK * NSA_HEAD_DIM, CMP_HIDDEN), (CMP_BLOCK * NSA_HEAD_DIM) ** -0.5),
        "cmp_w2": nrm(ks[11], (DEPTH_2, 2, CMP_HIDDEN, NSA_HEAD_DIM), CMP_HIDDEN ** -0.5),
        "gla_wa2": nrm(ks[12], (DEPTH_2, GLA_GATE_RANK, GLA_KEY_WIDTH), GLA_GATE_RANK ** -0.5),
        "gla_ba": 1.0 + nrm(ks[13], (DEPTH_2, GLA_KEY_WIDTH), 0.5),
        "gla_norm": 1.0 + nrm(ks[14], (DEPTH_2, GLA_DV), 0.05),
        "w_branch": nrm(ks[15], (DEPTH_2, N_BRANCH, BRANCH_WIDTH, D_MODEL), BRANCH_WIDTH ** -0.5),
        "w_out": nrm(ks[16], (DEPTH_2, D_MODEL, D_MODEL), D_MODEL ** -0.5),
        "w_ffn_in": nrm(ks[17], (DEPTH_2, D_MODEL, 2 * D_FF_2), D_MODEL ** -0.5),
        "w_ffn_out": nrm(ks[18], (DEPTH_2, D_FF_2, D_MODEL), D_FF_2 ** -0.5),
    }

def second_block(x, rel_table, norm_g, w_in, conv_w, conv_b, lru_w_gates, lru_b_gates, lru_lambda,
              cmp_pos, cmp_w1, cmp_w2, gla_wa2, gla_ba, gla_norm, w_branch, w_out, w_ffn_in, w_ffn_out):
    for l in range(DEPTH_2):
        x = hybrid_layer(x, rel_table, norm_g[l], w_in[l], conv_w[l], conv_b[l], lru_w_gates[l],
                         lru_b_gates[l], lru_lambda[l], cmp_pos[l], cmp_w1[l], cmp_w2[l],
                         gla_wa2[l], gla_ba[l], gla_norm[l], w_branch[l], w_out[l],
                         w_ffn_in[l], w_ffn_out[l])
    return x


def setup_inputs(seed=0):
    out = dict(first_inputs(seed))
    for name, value in second_inputs(seed + 1).items():
        if name != "x":
            out[name + "_2"] = value
    return out


def reference(
    x, ffn1_norm_w, ffn1_w_gate, ffn1_w_up, ffn1_w_down, mix_norm_w, w_in, mlstm_gate_bias,
    mlstm_norm_w, ssm_conv_w, ssm_conv_b, ssm_dt_bias, ssm_A_log, ssm_D, ssm_norm_w,
    diff_q_norm_w, diff_k_norm_w, diff_lambda, diff_subln_w, rel_bias, w_out, ffn2_norm_w,
    ffn2_w_gate, ffn2_w_up, ffn2_w_down, rel_table_2, norm_g_2, w_in_2, conv_w_2, conv_b_2,
    lru_w_gates_2, lru_b_gates_2, lru_lambda_2, cmp_pos_2, cmp_w1_2, cmp_w2_2, gla_wa2_2,
    gla_ba_2, gla_norm_2, w_branch_2, w_out_2, w_ffn_in_2, w_ffn_out_2,
):
    x = first_block(
        x, ffn1_norm_w, ffn1_w_gate, ffn1_w_up, ffn1_w_down, mix_norm_w, w_in, mlstm_gate_bias,
        mlstm_norm_w, ssm_conv_w, ssm_conv_b, ssm_dt_bias, ssm_A_log, ssm_D, ssm_norm_w,
        diff_q_norm_w, diff_k_norm_w, diff_lambda, diff_subln_w, rel_bias, w_out, ffn2_norm_w,
        ffn2_w_gate, ffn2_w_up, ffn2_w_down,
    )
    return second_block(
        x, rel_table_2, norm_g_2, w_in_2, conv_w_2, conv_b_2, lru_w_gates_2, lru_b_gates_2,
        lru_lambda_2, cmp_pos_2, cmp_w1_2, cmp_w2_2, gla_wa2_2, gla_ba_2, gla_norm_2,
        w_branch_2, w_out_2, w_ffn_in_2, w_ffn_out_2,
    )


_drawn_inputs = setup_inputs


def setup_inputs(seed=0):
    import zlib

    import numpy as np

    out = dict(_drawn_inputs(seed))
    spreads = {}
    factors = {'ssm_conv_b': 3.278,
     'conv_b_2': 3.318,
     'lru_b_gates_2': 64.0,
     'cmp_pos_2': 3.754,
     'gla_norm_2': 3.555,
     'rel_table_2': 3.475}
    for name, (base, spread) in spreads.items():
        noise = np.random.default_rng([zlib.crc32(name.encode()), seed]).standard_normal(out[name].shape)
        drawn = base * np.exp(spread * noise) if base else spread * noise
        out[name] = __import__('jax').numpy.asarray(drawn.astype(out[name].dtype))
    for name, factor in factors.items():
        out[name] = (out[name] * factor).astype(out[name].dtype)
    return out
```

```python
from contextlib import ExitStack, contextmanager

import numpy as np
import concourse.bass as bass
from concourse import mybir

F32 = mybir.dt.float32
ACT = mybir.ActivationFunctionType
ALU = mybir.AluOpType
AX = mybir.AxisListType.X

P = 128
SEQ = 512
TT = SEQ // P
D = 1024
KD = D // P
LAYERS = 2
FF = 2816
KF = FF // P
BANK = 512
EPS = 1e-6
MASKED = -1e30

TRI_W = [SEQ - P * j for j in range(TT)]
TRI_AT = [0, 512, 1024, 896]
TRI = sum(TRI_W)


class Stage:

    def __init__(self, nc):
        self.nc = nc
        self.ctx = ExitStack()
        self.sems = []
        self.engines = None

    def sem(self, name):
        s = self.ctx.enter_context(self.nc.semaphore(name))
        self.sems.append(s)
        return s

    def sb(self, name, shape):
        return self.ctx.enter_context(self.nc.sbuf_tensor(f"{name}_{self.nc.next_id()}", shape, F32))

    def block(self):
        self.engines = self.nc.Block(no_gpsimd_drain=True)
        return self.engines.__enter__()

    def __enter__(self):
        return self

    def __exit__(self, kind, value, trace):
        if self.engines is not None:
            self.engines.__exit__(kind, value, trace)
        if kind is None:
            for s in self.sems:
                self.nc.sync.sem_clear(s)
            self.nc.all_engine_barrier()
        return self.ctx.__exit__(kind, value, trace)


def bcast(ap, n):
    return ap.to_broadcast([ap.shape[0], n])


def consts(nc, c):
    with Stage(nc) as st:
        filled = st.sem("filled")
        block = st.block()

        @block.gpsimd
        def _(pool):
            pool.memset(c.ident[:, :], 0.0)
            pool.memset(c.ones[:, :], 1.0)
            pool.memset(c.eps[:, :], EPS)
            pool.memset(c.one[:, :], 1.0)
            pool.memset(c.ones64[:, :], 1.0)
            pool.memset(c.ones32[:, :], 1.0)
            pool.memset(c.bound[:, :], 0.0)
            pool.memset(c.winmask[:, :], 0.0)
            pool.memset(c.sel[:, :, :], 0.0)
            pool.memset(c.selp[:, :, :], 0.0)
            pool.memset(c.chunkmask[:, :], 1.0)
            pool.memset(c.scanone[:, :], 1.0)
            pool.drain()
            pool.affine_select(out=c.ident[:, :], in_=c.ident[:, :], compare_op=ALU.not_equal, fill=1.0,
                               base=0, pattern=[[-1, P]], channel_multiplier=1)
            pool.affine_select(out=c.bound[:, :], in_=c.bound[:, :], compare_op=ALU.is_ge, fill=MASKED,
                               base=0, pattern=[[1, SEQ]], channel_multiplier=-1)
            pool.affine_select(out=c.winmask[:, :], in_=c.winmask[:, :], compare_op=ALU.is_gt, fill=MASKED,
                               base=0, pattern=[[1, P]], channel_multiplier=-1)
            pool.affine_select(out=c.sel[:, :, :], in_=c.sel[:, :, :], compare_op=ALU.not_equal, fill=1.0,
                               base=0, pattern=[[-1, 8], [0, P]], channel_multiplier=1)
            pool.affine_select(out=c.selp[:, :, :], in_=c.selp[:, :, :], compare_op=ALU.not_equal, fill=1.0,
                               base=0, pattern=[[-2, 4], [-1, 2], [0, 64]], channel_multiplier=1)
            m = c.chunkmask[:, :]
            pool.affine_select(out=m, in_=m, compare_op=ALU.is_ge, fill=0.0,
                               base=0, pattern=[[-32, 4], [0, 32]], channel_multiplier=1)
            v = c.scanone[:, :].rearrange("p (c t) -> p c t", t=32)
            pool.memset(v[:, :, 0:1], 0.0)
            for m, b in ((c.ones64, 64), (c.ones32, 32)):
                w = m[:, :]
                pool.affine_select(out=w, in_=w, compare_op=ALU.is_ge, fill=0.0,
                                   base=0, pattern=[[-b, P // b], [0, b]], channel_multiplier=1)
            pool.drain()
            m = c.chunkmask[:, :]
            pool.affine_select(out=m, in_=m, compare_op=ALU.is_ge, fill=0.0,
                               base=0, pattern=[[32, 4], [1, 32]], channel_multiplier=-1)
            for m, b in ((c.ones64, 64), (c.ones32, 32)):
                w = m[:, :]
                pool.affine_select(out=w, in_=w, compare_op=ALU.is_ge, fill=0.0,
                                   base=b - 1, pattern=[[b, P // b], [0, b]], channel_multiplier=-1)
            pool.drain()


def load_x(nc, c, x):
    with Stage(nc) as st:
        xin = st.sb("xin", [P, TT, D])
        x_loaded, turned, kept = st.sem("x_loaded"), st.sem("turned"), st.sem("kept")
        block = st.block()

        @block.sync
        def _(sp):
            sp.dma_start(xin[:, :, :], x[0].rearrange("(t p) d -> p t d", p=P)).then_inc(x_loaded, 16)

        @block.tensor
        def _(pe):
            pe.wait_ge(x_loaded, 16)
            for k in range(KD):
                for t in range(TT):
                    mm = pe.transpose(c.ps[:, k, t * P:(t + 1) * P], xin[:, t, k * P:(k + 1) * P], c.ident[:, :])
                mm.then_inc(turned, 1)

        @block.vector
        def _(dve):
            for k in range(KD):
                dve.wait_ge(turned, k + 1)
                dve.tensor_copy(c.x_T[:, k, :], c.ps[:, k, :])


def store_x(nc, c, out):
    with Stage(nc) as st:
        xo = st.sb("xo", [P, TT, D])
        turned, kept, written = st.sem("turned"), st.sem("kept"), st.sem("written")
        block = st.block()

        @block.tensor
        def _(pe):
            for t in range(TT):
                for k in range(KD):
                    mm = pe.transpose(c.ps[:, 2 * t + k // 4, (k % 4) * P:(k % 4 + 1) * P],
                                      c.x_T[:, k, t * P:(t + 1) * P], c.ident[:, :])
                mm.then_inc(turned, 1)

        @block.vector
        def _(dve):
            for t in range(TT):
                dve.wait_ge(turned, t + 1)
                dve.tensor_copy(xo[:, t, :], c.ps[:, 2 * t:2 * t + 2, :]).then_inc(kept, 1)

        @block.sync
        def _(sp):
            for t in range(TT):
                sp.wait_ge(kept, t + 1)
                sp.dma_start(out[0, t * P:(t + 1) * P, :], xo[:, t, :]).then_inc(written, 16)
            sp.wait_ge(written, 16 * TT)


def norm(nc, c, gain, src=None, dst=None, add_to=None):
    src = c.x_T if src is None else src
    dst = c.h_T if dst is None else dst
    with Stage(nc) as st:
        sq = st.sb("sq", [P, KD, SEQ])
        rstd = st.sb("rstd", [P, SEQ])
        g = st.sb("g", [P, KD])
        gain_loaded, squared, summed = st.sem("gain_loaded"), st.sem("squared"), st.sem("summed")
        rooted = st.sem("rooted")
        block = st.block()

        @block.sync
        def _(sp):
            with nc.allow_non_contiguous_dma(reason="a column of gains"):
                sp.dma_start(g[:, :], gain.rearrange("(k p) -> p k", p=P)).then_inc(gain_loaded, 16)

        @block.tensor
        def _(pe):
            for k in range(KD):
                pe.wait_ge(squared, k + 1)
                mm = pe.matmul(c.ps[:, 0, :], c.ones[:, :], sq[:, k, :], start=(k == 0), stop=(k == KD - 1))
            mm.then_inc(summed, 1)

        @block.scalar
        def _(act):
            for k in range(KD):
                act.activation(sq[:, k, :], src[:, k, :], ACT.Square).then_inc(squared, 1)
            act.wait_ge(summed, 1)
            act.activation(rstd[:, :], c.ps[:, 0, :], ACT.Sqrt, scale=1.0 / D, bias=c.eps[:, :]).then_inc(rooted, 1)

        @block.vector
        def _(dve):
            dve.wait_ge(rooted, 1)
            dve.reciprocal(rstd[:, :], rstd[:, :])
            dve.drain()
            dve.wait_ge(gain_loaded, 16)
            for k in range(KD):
                to = dst[:, k, :] if add_to is None else sq[:, k, :]
                dve.scalar_tensor_tensor(out=to, in0=src[:, k, :], scalar=g[:, k:k + 1], in1=rstd[:, :],
                                         op0=ALU.mult, op1=ALU.mult)
            if add_to is not None:
                dve.drain()
                for k in range(KD):
                    dve.tensor_tensor(add_to[:, k, :], add_to[:, k, :], sq[:, k, :], ALU.add)


def ffn(nc, c, w_gate, w_up, w_down, scale, dst=None):
    with Stage(nc) as st:
        a_T = st.sb("a_T", [P, KF, SEQ])
        wg = st.sb("wg", [P, 2, KD, P])
        wu = st.sb("wu", [P, 2, KD, P])
        wd = st.sb("wd", [P, 2, D])
        sg = st.sb("sg", [P, 2, SEQ])
        w_loaded = [st.sem(f"w_loaded{s}") for s in range(2)]
        w_used = [st.sem(f"w_used{s}") for s in range(2)]
        silued = [st.sem(f"silued{s}") for s in range(2)]
        gated = [st.sem(f"gated{s}") for s in range(2)]
        d_loaded = [st.sem(f"d_loaded{s}") for s in range(2)]
        d_used = [st.sem(f"d_used{s}") for s in range(2)]
        done = st.sem("done")
        block = st.block()
        gate_v = w_gate.rearrange("(k p) f -> p k f", p=P)
        up_v = w_up.rearrange("(k p) f -> p k f", p=P)
        N = KF // 2

        @block.sync
        def _(sp):
            def load(f0, s):
                sp.dma_start(wg[:, s, :, :], gate_v[:, :, bass.ds(f0, P)]).then_inc(w_loaded[s], 16)
                sp.dma_start(wu[:, s, :, :], up_v[:, :, bass.ds(f0, P)]).then_inc(w_loaded[s], 16)

            for s in range(2):
                load(s * P, s)
                sp.dma_start(wd[:, s, :], w_down[s * P:(s + 1) * P, :]).then_inc(d_loaded[s], 16)
            with sp.Fori(1, N) as i:
                for s in range(2):
                    sp.wait_ge(w_used[s], i)
                    load(i * (2 * P) + s * P, s)
            with sp.Fori(1, N) as i:
                for s in range(2):
                    sp.wait_ge(d_used[s], i)
                    sp.dma_start(wd[:, s, :], w_down[bass.ds(i * (2 * P) + s * P, P), :]).then_inc(d_loaded[s], 16)

        @block.tensor
        def _(pe):
            def gate_up(i, s, first):
                pe.wait_ge(w_loaded[s], 32 * i + 32)
                if not first:
                    pe.wait_ge(gated[s], i)
                for b, w in ((s, wg), (2 + s, wu)):
                    for k in range(KD):
                        mm = pe.matmul(c.ps[:, b, :], w[:, s, k, :], c.h_T[:, k, :], start=(k == 0), stop=(k == KD - 1))
                mm.then_inc(w_used[s], 1)

            def down(i, s, first, last):
                pe.wait_ge(d_loaded[s], 16 * i + 16)
                for m in range(KD):
                    mm = pe.matmul(c.ps[:, m, :], wd[:, s, m * P:(m + 1) * P], a_T[:, 2 * i + s, :],
                                   start=first, stop=last)
                mm.then_inc(d_used[s], 1)

            gate_up(0, 0, True)
            gate_up(0, 1, True)
            with pe.Fori(1, N) as i:
                gate_up(i, 0, False)
                gate_up(i, 1, False)
            for s in range(2):
                pe.wait_ge(gated[s], N)
            down(0, 0, True, False)
            down(0, 1, False, False)
            with pe.Fori(1, N - 1) as i:
                for s in range(2):
                    pe.wait_ge(d_loaded[s], 16 * i + 16)
                    for m in range(KD):
                        mm = pe.matmul(c.ps[:, m, :], wd[:, s, m * P:(m + 1) * P],
                                       a_T[:, bass.ds(2 * i + s, 1), :], start=False, stop=False)
                    mm.then_inc(d_used[s], 1)
            down(N - 1, 0, False, False)
            down(N - 1, 1, False, True)

        @block.scalar
        def _(act):
            def silu(i, s, first):
                act.wait_ge(w_used[s], i + 1)
                if not first:
                    act.wait_ge(gated[s], i)
                act.activation(sg[:, s, :], c.ps[:, s, :], ACT.Silu).then_inc(silued[s], 1)

            silu(0, 0, True)
            silu(0, 1, True)
            with act.Fori(1, N) as i:
                silu(i, 0, False)
                silu(i, 1, False)

        @block.vector
        def _(dve):
            with dve.Fori(0, N) as i:
                for s in range(2):
                    dve.wait_ge(silued[s], i + 1)
                    dve.tensor_tensor(a_T[:, bass.ds(2 * i + s, 1), :], sg[:, s:s + 1, :], c.ps[:, 2 + s:3 + s, :],
                                      ALU.mult).then_inc(gated[s], 1)
            dve.wait_ge(d_used[1], N)
            for m in range(KD):
                if dst is None:
                    dve.scalar_tensor_tensor(out=c.x_T[:, m, :], in0=c.ps[:, m, :], scalar=scale, in1=c.x_T[:, m, :],
                                             op0=ALU.mult, op1=ALU.add)
                else:
                    dve.tensor_copy(dst[:, m, :], c.ps[:, m, :])


class Shared:

    def __init__(self, nc, ctx):
        def sb(name, shape):
            return ctx.enter_context(nc.sbuf_tensor(name, shape, F32))
        self.ps = ctx.enter_context(nc.psum_tensor("ps", [P, 8, BANK], F32))
        self.x_T = sb("x_T", [P, KD, SEQ])
        self.h_T = sb("h_T", [P, KD, SEQ])
        self.y_T = sb("y_T", [P, KD, SEQ])
        self.ident = sb("ident", [P, P])
        self.ones = sb("ones", [P, P])
        self.ones64 = sb("ones64", [P, P])
        self.ones32 = sb("ones32", [P, P])
        self.bound = sb("bound", [P, SEQ])
        self.winmask = sb("winmask", [P, P])
        self.sel = sb("sel", [8, 8, P])
        self.selp = sb("selp", [8, 4, P])
        self.chunkmask = sb("chunkmask", [P, P])
        self.scanone = sb("scanone", [P, SEQ])
        self.eps = sb("eps", [P, 1])
        self.one = sb("one", [P, 1])
        self.lam_init = sb("lam_init", [P, LAYERS])


def project(nc, c, w, pairs_to, rows_to, tokens_to, params=()):
    with Stage(nc) as st:
        wf = st.sb("wf", [P, 2, KD, P])
        wt = st.sb("wt", [P, 2, KD, 256])
        f_loaded = [st.sem(f"f_loaded{s}") for s in range(2)]
        f_done = [st.sem(f"f_done{s}") for s in range(2)]
        f_kept = [st.sem(f"f_kept{s}") for s in range(2)]
        t_loaded = [st.sem(f"t_loaded{s}") for s in range(2)]
        t_done, t_kept, param_loaded = st.sem("t_done"), st.sem("t_kept"), st.sem("param_loaded")
        block = st.block()
        view = w.rearrange("(k p) f -> p k f", p=P)
        extra = [("row", *r) for r in rows_to] + [("token", *t) for t in tokens_to]

        def each_pair(eng, body):
            base = 0
            for col0, chunks, dst in pairs_to:
                n = chunks // 2
                start = 0
                if base == 0:
                    body(0, 0, col0, dst, True)
                    start = 1
                if n - start > 2:
                    with eng.Fori(start, n) as i:
                        body(base + i, i, col0, dst, False)
                else:
                    for i in range(start, n):
                        body(base + i, i, col0, dst, False)
                base += n

        @block.sync
        def _(sp):
            def load(n, i, col0, dst, first):
                for s in range(2):
                    if not first:
                        sp.wait_ge(f_done[s], n)
                    sp.dma_start(wf[:, s, :, :], view[:, :, bass.ds(i * (2 * P) + (col0 + s * P), P)])\
                        .then_inc(f_loaded[s], 16)

            each_pair(sp, load)
            with nc.allow_non_contiguous_dma(reason="columns of parameters"):
                for dst, src in params:
                    sp.dma_start(dst, src).then_inc(param_loaded, 16)
            for n, (kind, col0, m, dst) in enumerate(extra):
                if n >= 2:
                    sp.wait_ge(t_done, n - 1)
                sp.dma_start(wt[:, n % 2, :, 0:m], view[:, :, col0:col0 + m]).then_inc(t_loaded[n % 2], 16)
            if params:
                sp.wait_ge(param_loaded, 16 * len(params))

        @block.tensor
        def _(pe):
            def product(n, i, col0, dst, first):
                for s in range(2):
                    pe.wait_ge(f_loaded[s], 16 * n + 16)
                    if not first:
                        pe.wait_ge(f_kept[s], n)
                    for k in range(KD):
                        mm = pe.matmul(c.ps[:, s, :], wf[:, s, k, :], c.h_T[:, k, :], start=(k == 0), stop=(k == KD - 1))
                    mm.then_inc(f_done[s], 1)

            each_pair(pe, product)
            for n, (kind, col0, m, dst) in enumerate(extra):
                pe.wait_ge(t_loaded[n % 2], 16 * (n // 2) + 16)
                if n >= 1:
                    pe.wait_ge(t_kept, n)
                for t in range(TT if kind == "token" else 1):
                    for k in range(KD):
                        if kind == "token":
                            mm = pe.matmul(c.ps[:, 4 + t, 0:m], c.h_T[:, k, t * P:(t + 1) * P], wt[:, n % 2, k, 0:m],
                                           start=(k == 0), stop=(k == KD - 1))
                        else:
                            mm = pe.matmul(c.ps[0:m, 4, :], wt[:, n % 2, k, 0:m], c.h_T[:, k, :],
                                           start=(k == 0), stop=(k == KD - 1))
                mm.then_inc(t_done, 1)

        def keep(eng, s, copy):
            def body(n, i, col0, dst, first):
                eng.wait_ge(f_done[s], n + 1)
                copy(dst[:, bass.ds(2 * i + s, 1), :], c.ps[:, s:s + 1, :]).then_inc(f_kept[s], 1)
            return body

        @block.scalar
        def _(act):
            each_pair(act, keep(act, 0, lambda o, i: act.activation(o, i, ACT.Copy)))
            for n, (kind, col0, m, dst) in enumerate(extra):
                act.wait_ge(t_done, n + 1)
                if kind == "token":
                    act.activation(dst, c.ps[:, 4:8, 0:m], ACT.Copy).then_inc(t_kept, 1)
                else:
                    act.activation(dst, c.ps[0:m, 4, :], ACT.Copy).then_inc(t_kept, 1)

        @block.vector
        def _(dve):
            each_pair(dve, keep(dve, 1, lambda o, i: dve.tensor_copy(o, i)))


M_HEADS, M_DIM = 4, 64
S_HEADS, S_DIM = 8, 64
DF_HEADS, DF_QK, DF_V = 4, 32, 64


class Mixer:

    def __init__(self, nc, ctx):
        def sb(name, shape):
            return ctx.enter_context(nc.sbuf_tensor(f"{name}_{nc.next_id()}", shape, F32))
        self.mqk = sb("mqk", [P, 4, SEQ])
        self.mo = sb("mo", [P, 2, SEQ])
        self.mv = sb("mv", [P, TT, 2 * P])
        self.gi = sb("gi", [M_HEADS, SEQ])
        self.gf = sb("gf", [M_HEADS, SEQ])
        self.z = sb("z", [P, 4, SEQ])
        self.xbc = sb("xbc", [P, 8, SEQ])
        self.dt = sb("dt", [S_HEADS, SEQ])
        self.dqk = sb("dqk", [P, 4, SEQ])
        self.dv = sb("dv", [P, TT, 2 * P])
        self.g_bias = sb("g_bias", [M_HEADS, 2])
        self.m_gain = sb("m_gain", [P, 2])
        self.conv_w = sb("conv_w", [P, 8, 4])
        self.conv_b = sb("conv_b", [P, 8])
        self.dt_bias = sb("dt_bias", [S_HEADS, 1])
        self.a_log = sb("a_log", [S_HEADS, 1])
        self.d_skip = sb("d_skip", [P, 4])
        self.s_gain = sb("s_gain", [P, 4])
        self.q_gain = sb("q_gain", [P, 1])
        self.k_gain = sb("k_gain", [P, 1])
        self.lam4 = sb("lam4", [P, 4, DF_QK])
        self.sub_gain = sb("sub_gain", [P, 1])


def per_partition(ap, offset_ap, pattern):
    return bass.AP(tensor=offset_ap.tensor, offset=offset_ap.offset, ap=pattern)


def gates(nc, c, m, rows, cols):
    acs, negM, negm = rows
    with Stage(nc) as st:
        x8, e8, l8, dA, nacs = (st.sb(n, [8, SEQ]) for n in ("x8", "e8", "l8", "dA", "nacs"))
        x4, e4, l4, B, g, M, s4 = (st.sb(n, [4, SEQ]) for n in ("x4", "e4", "l4", "B", "g", "M", "s4"))
        ones8 = st.sb("ones8", [8, SEQ])
        a8 = st.sb("a8", [8, 1])
        biased, logged, rowed, turned = st.sem("biased"), st.sem("logged"), st.sem("rowed"), st.sem("turned")
        block = st.block()

        @block.scalar
        def _(act):
            act.activation(a8[:, :], m.a_log[:, :], ACT.Exp)
            act.wait_ge(biased, 1)
            act.activation(e8[:, :], x8[:, :], ACT.Abs)
            act.activation(e4[:, :], x4[:, :], ACT.Abs)
            act.drain()
            act.activation(e8[:, :], e8[:, :], ACT.Exp, scale=-1.0)
            act.activation(e4[:, :], e4[:, :], ACT.Exp, scale=-1.0)
            act.drain()
            act.activation(l8[:, :], e8[:, :], ACT.Ln, bias=c.one[0:8, :])
            act.activation(l4[:, :], e4[:, :], ACT.Ln, bias=c.one[0:4, :])
            act.drain().then_inc(logged, 1)

        @block.vector
        def _(dve):
            dve.memset(ones8[:, :], 1.0)
            dve.tensor_scalar(x8[:, :], m.dt[:, :], m.dt_bias[:, :], None, ALU.add)
            dve.tensor_scalar(x4[:, :], m.gf[:, :], m.g_bias[:, 1:2], None, ALU.add)
            dve.drain().then_inc(biased, 1)
            dve.wait_ge(logged, 1)
            dve.scalar_tensor_tensor(out=m.dt[:, :], in0=x8[:, :], scalar=0.0, in1=l8[:, :], op0=ALU.max, op1=ALU.add)
            dve.scalar_tensor_tensor(out=s4[:, :], in0=x4[:, :], scalar=0.0, in1=l4[:, :], op0=ALU.min, op1=ALU.subtract)
            dve.drain()
            dve.tensor_scalar(dA[:, :], m.dt[:, :], a8[:, 0:1], -1.0, ALU.mult, ALU.mult)
            dve.tensor_tensor_scan(B[:, :], ones8[0:4, :], s4[:, :], 0.0, ALU.mult, ALU.add)
            dve.drain()
            dve.tensor_tensor_scan(acs[:, :], ones8[:, :], dA[:, :], 0.0, ALU.mult, ALU.add)
            dve.scalar_tensor_tensor(out=g[:, :], in0=m.gi[:, :], scalar=m.g_bias[:, 0:1], in1=B[:, :],
                                     op0=ALU.add, op1=ALU.subtract)
            dve.drain()
            dve.tensor_scalar(nacs[:, :], acs[:, :], -1.0, None, ALU.mult)
            dve.tensor_tensor_scan(M[:, :], g[:, :], g[:, :], 0.0, ALU.max, ALU.max)
            dve.drain()
            dve.tensor_scalar(negM[:, :], M[:, :], -1.0, None, ALU.mult)
            dve.scalar_tensor_tensor(out=negm[:, :], in0=M[:, :], scalar=-1.0, in1=B[:, :], op0=ALU.mult, op1=ALU.subtract)
            dve.drain().then_inc(rowed, 1)
            dve.wait_ge(turned, 1)
            dve.tensor_copy(cols[:, :, :], c.ps[:, 0, 0:TT * 32].rearrange("p (t n) -> p t n", n=32)[:, :, 0:20])

        @block.tensor
        def _(pe):
            pe.wait_ge(rowed, 1)
            for t in range(TT):
                at = t * P
                for off, src, n in ((0, g, 4), (4, nacs, 8), (12, m.dt, 8)):
                    mm = pe.transpose(c.ps[:, 0, 32 * t + off:32 * t + off + n], src[:, at:at + P], c.ident[0:n, 0:n])
            mm.then_inc(turned, 1)


def conv(nc, c, m, xdt, cols):
    with Stage(nc) as st:
        y = st.sb("y", [P, 8, SEQ])
        convolved, silued, turned = st.sem("convolved"), st.sem("silued"), st.sem("turned")
        block = st.block()

        @block.vector
        def _(dve):
            for k in range(8):
                dve.tensor_scalar(y[:, k, :], m.xbc[:, k, :], m.conv_w[:, k, 3:4], None, ALU.mult)
            for s in range(1, 4):
                dve.drain()
                for k in range(8):
                    ins = dve.scalar_tensor_tensor(out=y[:, k, s:], in0=m.xbc[:, k, 0:SEQ - s],
                                                   scalar=m.conv_w[:, k, 3 - s:4 - s], in1=y[:, k, s:],
                                                   op0=ALU.mult, op1=ALU.add)
                    if s == 3:
                        ins.then_inc(convolved, 1)
            for t in range(TT):
                dve.wait_ge(turned, t + 1)
                dve.tensor_tensor(xdt[:, t, :].rearrange("p (h d) -> p h d", d=S_DIM),
                                  c.ps[:, t, :].rearrange("p (h d) -> p h d", d=S_DIM),
                                  cols[:, t, 12:20].rearrange("p (h o) -> p h o", o=1).to_broadcast([P, S_HEADS, S_DIM]),
                                  ALU.mult)

        @block.scalar
        def _(act):
            for k in range(8):
                act.wait_ge(convolved, k + 1)
                if k == 0:
                    act.wait_ge(convolved, 8)
                act.activation(m.xbc[:, k, :], y[:, k, :], ACT.Silu, bias=m.conv_b[:, k:k + 1]).then_inc(silued, 1)

        @block.tensor
        def _(pe):
            pe.wait_ge(silued, 4)
            for t in range(TT):
                for k in range(4):
                    mm = pe.transpose(c.ps[:, t, k * P:(k + 1) * P], m.xbc[:, k, t * P:(t + 1) * P], c.ident[:, :])
                mm.then_inc(turned, 1)


def recurrences(nc, c, m, rows, cols, xdt, y_ssm, num, den):
    acs, negM, negm = rows
    units = [("ssm", h) for h in range(S_HEADS)] + [("mlstm", h) for h in range(M_HEADS)]
    score_of, scores = [], []
    for kind, h in units:
        key = (kind, h // 4 if kind == "ssm" else h)
        if key not in scores:
            scores.append(key)
        score_of.append(scores.index(key))
    last_use = {n: max(u for u, k in enumerate(score_of) if k == n) for n in range(len(scores))}
    with Stage(nc) as st:
        arg = st.sb("arg", [P, 2, TRI])
        wgt = st.sb("wgt", [P, 2, TRI])
        vone = st.sb("vone", [P, TT, M_HEADS, P])
        v_ready, row_sent, arged, exped = (st.sem(n) for n in ("v_ready", "row_sent", "arged", "exped"))
        scored, weighted, outed, kept = (st.sem(n) for n in ("scored", "weighted", "outed", "kept"))
        block = st.block()
        ROW, OUT = 6, 7

        def tri(buf, j):
            return c.ps[:, 3 * buf + TRI_AT[j] // BANK, TRI_AT[j] % BANK:TRI_AT[j] % BANK + TRI_W[j]]

        @block.tensor
        def _(pe):
            def row(u):
                kind, h = units[u]
                if u >= 1:
                    pe.wait_ge(arged, u)
                n, src = (8, acs) if kind == "ssm" else (4, negM)
                pe.matmul(c.ps[:, ROW, :], c.sel[0:n, h, :], src[:, :], start=True, stop=True).then_inc(row_sent, 1)
                k = score_of[u]
                if u and score_of[u - 1] == k:
                    return
                if k >= 2:
                    pe.wait_ge(weighted, last_use[k - 2] + 1)
                for j in range(TT):
                    if kind == "ssm":
                        key, query = m.xbc[:, 4 + h // 4, j * P:(j + 1) * P], m.xbc[:, 6 + h // 4, j * P:]
                    else:
                        b = 64 * (h % 2)
                        key, query = m.mqk[b:b + 64, 2 + h // 2, j * P:(j + 1) * P], m.mqk[b:b + 64, h // 2, j * P:]
                    mm = pe.matmul(tri(k % 2, j), key, query, start=True, stop=True)
                mm.then_inc(scored, 1)

            def out(u):
                kind, h = units[u]
                pe.wait_ge(weighted, u + 1)
                if u >= 1:
                    pe.wait_ge(kept, u)
                if u == 8:
                    pe.wait_ge(v_ready, 1)
                b = 64 * (h % 2)
                for j in range(TT):
                    if kind == "ssm":
                        v, to = xdt[:, j, h * 64:(h + 1) * 64], c.ps[b:b + 64, OUT, j * P:]
                    else:
                        v, to = vone[:, j, h, :], c.ps[:, OUT, j * P:]
                    mm = pe.matmul(to, v, wgt[:, u % 2, TRI_AT[j]:TRI_AT[j] + TRI_W[j]], start=(j == 0), stop=(j == TT - 1))
                mm.then_inc(outed, 1)

            row(0)
            for u in range(len(units)):
                if u + 1 < len(units):
                    row(u + 1)
                out(u)

        @block.vector
        def _(dve):
            dve.memset(vone[:, :, :, 64:P], 1.0)
            dve.tensor_copy(vone[:, :, :, 0:64], m.mv[:, :, :].rearrange("p t (h d) -> p t h d", d=64)).then_inc(v_ready, 1)

            def args(u):
                kind, h = units[u]
                dve.wait_ge(row_sent, u + 1)
                for j in range(TT):
                    col = cols[:, j, 4 + h:5 + h] if kind == "ssm" else cols[:, j, h:h + 1]
                    ins = dve.scalar_tensor_tensor(out=arg[:, u % 2, TRI_AT[j]:TRI_AT[j] + TRI_W[j]],
                                                   in0=c.ps[:, ROW, j * P:], scalar=col, in1=c.bound[:, 0:TRI_W[j]],
                                                   op0=ALU.add, op1=ALU.min)
                ins.then_inc(arged, 1)

            def weigh(u):
                kind, h = units[u]
                dve.wait_ge(exped, u + 1)
                dve.wait_ge(scored, score_of[u] + 1)
                if u >= 2:
                    dve.wait_ge(outed, u - 1)
                k = score_of[u] % 2
                dve.scalar_tensor_tensor(
                    out=wgt[:, u % 2, :], in0=c.ps[:, 3 * k:3 * k + 3, :].rearrange("p b n -> p (b n)")[:, 0:TRI],
                    scalar=(1.0 if kind == "ssm" else M_DIM ** -0.5), in1=arg[:, u % 2, :],
                    op0=ALU.mult, op1=ALU.mult).then_inc(weighted, 1)

            args(0)
            for u in range(len(units)):
                if u + 1 < len(units):
                    args(u + 1)
                weigh(u)

        @block.scalar
        def _(act):
            def exps(u):
                act.wait_ge(arged, u + 1)
                act.activation(arg[:, u % 2, :], arg[:, u % 2, :], ACT.Exp).then_inc(exped, 1)

            exps(0)
            for u, (kind, h) in enumerate(units):
                if u + 1 < len(units):
                    exps(u + 1)
                act.wait_ge(outed, u + 1)
                b = 64 * (h % 2)
                if kind == "ssm":
                    act.activation(y_ssm[b:b + 64, h // 2, :], c.ps[b:b + 64, OUT, :], ACT.Copy).then_inc(kept, 1)
                else:
                    act.activation(num[b:b + 64, h // 2, :], c.ps[0:64, OUT, :], ACT.Copy)
                    act.activation(den[b:b + 64, h // 2, :], c.ps[64:P, OUT, :], ACT.Copy).then_inc(kept, 1)


def finish_recurrences(nc, c, m, rows, y_ssm, num, den):
    acs, negM, negm = rows
    with Stage(nc) as st:
        floor = st.sb("floor", [P, 2, SEQ])
        sq = st.sb("sq", [P, 6, SEQ])
        rstd = st.sb("rstd", [P, 4, SEQ])
        row_sent, exped, y_ready, squared, summed, rooted, sigmoided, zed = (
            st.sem(n) for n in ("row_sent", "exped", "y_ready", "squared", "summed", "rooted", "sigmoided", "zed"))
        block = st.block()

        @block.tensor
        def _(pe):
            for p in range(2):
                mm = pe.matmul(c.ps[:, p, :], c.selp[0:4, p, :], negm[:, :], start=True, stop=True)
            mm.then_inc(row_sent, 1)
            pe.wait_ge(squared, 1)
            for g in range(2):
                for k in range(2):
                    pe.matmul(c.ps[:, 2 + g, :], c.ones[:, :], sq[:, 2 * g + k, :], start=(k == 0), stop=(k == 1))
            for p in range(2):
                mm = pe.matmul(c.ps[:, 4 + p, :], c.ones64[:, :], sq[:, 4 + p, :], start=True, stop=True)
            mm.then_inc(summed, 1)

        @block.scalar
        def _(act):
            act.activation(m.z[:, :, :], m.z[:, :, :], ACT.Silu).then_inc(zed, 1)
            act.activation(m.mo[:, :, :], m.mo[:, :, :], ACT.Sigmoid).then_inc(sigmoided, 1)
            act.activation(den[:, :, :], den[:, :, :], ACT.Abs)
            act.wait_ge(row_sent, 1)
            act.activation(floor[:, :, :], c.ps[:, 0:2, :], ACT.Exp)
            act.drain().then_inc(exped, 1)
            act.wait_ge(y_ready, 1)
            act.activation(sq[:, 0:4, :], y_ssm[:, :, :], ACT.Square)
            act.activation(sq[:, 4:6, :], num[:, :, :], ACT.Square)
            act.drain().then_inc(squared, 1)
            act.wait_ge(summed, 1)
            act.activation(rstd[:, 0:2, :], c.ps[:, 2:4, :], ACT.Sqrt, scale=1.0 / 256, bias=c.eps[:, :])
            act.activation(rstd[:, 2:4, :], c.ps[:, 4:6, :], ACT.Sqrt, scale=1.0 / 64, bias=c.eps[:, :])
            act.drain().then_inc(rooted, 1)

        @block.vector
        def _(dve):
            for k in range(4):
                dve.scalar_tensor_tensor(out=y_ssm[:, k, :], in0=m.xbc[:, k, :], scalar=m.d_skip[:, k:k + 1],
                                         in1=y_ssm[:, k, :], op0=ALU.mult, op1=ALU.add)
            dve.drain()
            dve.wait_ge(zed, 1)
            dve.tensor_tensor(y_ssm[:, :, :], y_ssm[:, :, :], m.z[:, :, :], ALU.mult)
            dve.wait_ge(exped, 1)
            dve.tensor_tensor(den[:, :, :], den[:, :, :], floor[:, :, :], ALU.max)
            dve.drain()
            dve.reciprocal(den[:, :, :], den[:, :, :])
            dve.drain()
            dve.tensor_tensor(num[:, :, :], num[:, :, :], den[:, :, :], ALU.mult)
            dve.drain().then_inc(y_ready, 1)
            dve.wait_ge(sigmoided, 1)
            dve.wait_ge(rooted, 1)
            dve.reciprocal(rstd[:, :, :], rstd[:, :, :])
            dve.drain()
            for p in range(2):
                dve.scalar_tensor_tensor(out=num[:, p, :], in0=num[:, p, :], scalar=m.m_gain[:, p:p + 1],
                                         in1=rstd[:, 2 + p, :], op0=ALU.mult, op1=ALU.mult)
            for k in range(4):
                dve.scalar_tensor_tensor(out=c.y_T[:, 2 + k, :], in0=y_ssm[:, k, :], scalar=m.s_gain[:, k:k + 1],
                                         in1=rstd[:, k // 2, :], op0=ALU.mult, op1=ALU.mult)
            dve.drain()
            dve.tensor_tensor(c.y_T[:, 0:2, :], num[:, :, :], m.mo[:, :, :], ALU.mult)


def bias_rows(nc, c, table, heads, scratch):
    edges = bucket_edges()
    with Stage(nc) as st:
        tab = st.sb("tab", [heads, 32])
        f = st.sb("f", [heads, BACK + SEQ])
        loaded, laid, written = st.sem("loaded"), st.sem("laid"), st.sem("written")
        block = st.block()

        @block.sync
        def _(sp):
            with nc.allow_non_contiguous_dma(reason="a small table, turned"):
                sp.dma_start(tab[:, :], table.rearrange("b h -> h b")).then_inc(loaded, 16)
            sp.wait_ge(laid, 1)
            sp.dma_start(scratch[:, :], f[:, :]).then_inc(written, 16)
            sp.wait_ge(written, 16)

        @block.vector
        def _(dve):
            dve.memset(f[:, 0:BACK], MASKED)
            dve.wait_ge(loaded, 16)
            dve.tensor_copy(f[:, BACK:BACK + 16], tab[:, 0:16])
            for b in range(16, 32):
                lo, hi = edges[b], edges[b + 1]
                if lo < hi:
                    dve.tensor_copy(f[:, BACK + lo:BACK + hi], tab[:, b:b + 1].to_broadcast([heads, hi - lo]))
            dve.drain().then_inc(laid, 1)


def bucket_edges():
    n = np.arange(SEQ)
    nf = np.maximum(n, 16).astype(np.float32)
    large = 16 + (np.log(nf / np.float32(16)) / np.float32(np.log(8.0)) * np.float32(16)).astype(np.int32)
    bucket = np.where(n < 16, n, np.minimum(large, 31))
    return {b: int(np.argmax(bucket >= b)) for b in range(16, 32)} | {32: SEQ}


BACK = P


def bias_tiles(nc, c, scratch, heads, tiles):
    with Stage(nc) as st:
        turned = st.sb("turned", [P, 2, SEQ])
        loaded, used = [st.sem(f"loaded{s}") for s in range(2)], st.sem("used")
        block = st.block()

        @block.sync
        def _(sp):
            for h in range(heads):
                if h >= 2:
                    sp.wait_ge(used, h - 1)
                src = scratch[h, BACK - 127:BACK - 127 + SEQ]
                sp.dma_start(turned[:, h % 2, :], bass.AP(tensor=src.tensor, offset=src.offset, ap=[[1, P], [1, SEQ]]))\
                    .then_inc(loaded[h % 2], 16)

        @block.vector
        def _(dve):
            for h in range(heads):
                dve.wait_ge(loaded[h % 2], 16 * (h // 2) + 16)
                dve.tensor_copy(tiles[:, h, :], turned[:, h % 2, ::-1]).then_inc(used, 1)


def first_mixer_projections(nc, c, m, L, w):
    FM = [(0, 4, m.mqk[:, :, :]), (768, 2, m.mo[:, :, :]), (1032, 4, m.z[:, :, :]), (1544, 8, m.xbc[:, :, :]),
          (2576, 4, m.dqk[:, :, :])]
    rows = [(1024, 4, m.gi[:, :]), (1028, 4, m.gf[:, :]), (2568, 8, m.dt[:, :])]
    tokens = [(512, 256, m.mv[:, :, :]), (3088, 256, m.dv[:, :, :])]

    def col(ap):
        return ap.rearrange("(p o) -> p o", o=1)

    params = [
        (m.g_bias[:, :], L["mlstm_gate_bias"].rearrange("g h -> h g")),
        (m.m_gain[:, :], L["mlstm_norm_w"].rearrange("(k p) -> p k", p=P)),
        (m.conv_b[:, :], L["ssm_conv_b"].rearrange("(k p) -> p k", p=P)),
        (m.dt_bias[:, :], col(L["ssm_dt_bias"])),
        (m.a_log[:, :], col(L["ssm_A_log"])),
        (m.s_gain[:, :], L["ssm_norm_w"].rearrange("(k p) -> p k", p=P)),
        (m.sub_gain[0:64, :], col(L["diff_subln_w"])),
        (m.sub_gain[64:P, :], col(L["diff_subln_w"])),
        (m.lam4[:, :, :], L["diff_lambda"].rearrange("(o a) d -> o a d", o=1).to_broadcast([P, 4, DF_QK])),
    ]
    for k in range(8):
        params.append((m.conv_w[:, k, :], L["ssm_conv_w"][:, k * P:(k + 1) * P].rearrange("t p -> p t")))
    for half in range(2):
        b = 64 * half
        for name, dst in (("diff_q_norm_w", m.q_gain), ("diff_k_norm_w", m.k_gain)):
            params.append((dst[b:b + 64, :], L[name].rearrange("i (d o) -> (i d) o", o=1)))
        src = L["ssm_D"].rearrange("(k e o) -> e o k", e=2, o=1)
        params.append((m.d_skip[b:b + 64, :], src[half].to_broadcast([64, 4])))
    project(nc, c, w, FM, rows, tokens, params)


def diff_prepare(nc, c, m, lam, lam_init):
    with Stage(nc) as st:
        sq = st.sb("sq", [P, 4, SEQ])
        rstd = st.sb("rstd", [P, 4, SEQ])
        prod = st.sb("prod", [P, 2, DF_QK])
        dots = st.sb("dots", [P, 2])
        squared, summed, rooted, dotted, exped = (st.sem(n) for n in ("squared", "summed", "rooted", "dotted", "exped"))
        block = st.block()

        @block.scalar
        def _(act):
            act.activation(sq[:, :, :], m.dqk[:, :, :], ACT.Square).then_inc(squared, 1)
            act.wait_ge(dotted, 1)
            act.activation(dots[:, :], dots[:, :], ACT.Exp).then_inc(exped, 1)
            act.wait_ge(summed, 1)
            act.activation(rstd[:, :, :], c.ps[:, 0:4, :], ACT.Sqrt, scale=1.0 / DF_QK, bias=c.eps[:, :]).then_inc(rooted, 1)

        @block.tensor
        def _(pe):
            pe.wait_ge(squared, 1)
            for k in range(4):
                mm = pe.matmul(c.ps[:, k, :], c.ones32[:, :], sq[:, k, :], start=True, stop=True)
            mm.then_inc(summed, 1)

        @block.vector
        def _(dve):
            dve.tensor_tensor(prod[:, :, :], m.lam4[:, 0:4:2, :], m.lam4[:, 1:4:2, :], ALU.mult)
            dve.drain()
            dve.reduce_sum(dots[:, :], prod[:, :, :], AX).then_inc(dotted, 1)
            dve.wait_ge(exped, 1)
            dve.scalar_tensor_tensor(out=lam[:, 0:1], in0=dots[:, 1:2], scalar=dots[:, 0:1], in1=lam_init,
                                     op0=ALU.subtract, op1=ALU.subtract)
            dve.tensor_scalar(lam[:, 1:2], lam_init, -1.0, 1.0, ALU.mult, ALU.add)
            dve.drain()
            dve.tensor_tensor(lam[:, 1:2], lam[:, 1:2], m.sub_gain[:, :], ALU.mult)
            dve.wait_ge(rooted, 1)
            dve.reciprocal(rstd[:, :, :], rstd[:, :, :])
            dve.drain()
            for k in range(4):
                gain = m.q_gain if k < 2 else m.k_gain
                dve.scalar_tensor_tensor(out=m.dqk[:, k, :], in0=m.dqk[:, k, :], scalar=gain[:, 0:1], in1=rstd[:, k, :],
                                         op0=ALU.mult, op1=ALU.mult)


def diff_attention(nc, c, m, tiles, lam, o_T):
    units = [(h, qi) for h in range(DF_HEADS) for qi in range(TT)]
    with Stage(nc) as st:
        logit = st.sb("logit", [P, 2, 2, SEQ])
        prob = st.sb("prob", [P, 2, SEQ])
        prob_T = st.sb("prob_T", [P, 2, TT, SEQ])
        nmax = st.sb("nmax", [P, 2, 2])
        total = st.sb("total", [P, 2, 2])
        recip = st.sb("recip", [P, 2, 2])
        scored, biased, maxed, exped, mixed, turned, laid, outed, kept = (
            st.sem(n) for n in ("scored", "biased", "maxed", "exped", "mixed", "turned", "laid", "outed", "kept"))
        block = st.block()
        TURN, OUT = 4, 6

        @block.tensor
        def _(pe):
            def score(u):
                h, qi = units[u]
                if u >= 2:
                    pe.wait_ge(biased, u - 1)
                w = P * (qi + 1)
                for i in range(2):
                    b = 64 * (h % 2) + 32 * i
                    mm = pe.matmul(c.ps[:, 2 * (u % 2) + i, 0:w], m.dqk[b:b + 32, h // 2, qi * P:(qi + 1) * P],
                                   m.dqk[b:b + 32, 2 + h // 2, 0:w], start=True, stop=True)
                mm.then_inc(scored, 1)

            def turn(u):
                h, qi = units[u]
                pe.wait_ge(mixed, u + 1)
                if u >= 2:
                    pe.wait_ge(laid, u - 1)
                for j in range(qi + 1):
                    mm = pe.transpose(c.ps[:, TURN + u % 2, j * P:(j + 1) * P], prob[:, u % 2, j * P:(j + 1) * P], c.ident[:, :])
                mm.then_inc(turned, 1)

            def out(h):
                pe.wait_ge(laid, TT * (h + 1))
                if h >= 1:
                    pe.wait_ge(kept, h)
                b = 64 * (h % 2)
                for j in range(TT):
                    mm = pe.matmul(c.ps[b:b + 64, OUT, j * P:], m.dv[:, j, h * 64:(h + 1) * 64], prob_T[:, h % 2, j, j * P:],
                                   start=(j == 0), stop=(j == TT - 1))
                mm.then_inc(outed, 1)

            score(0)
            for u, (h, qi) in enumerate(units):
                if u + 1 < len(units):
                    score(u + 1)
                turn(u)
                if qi == TT - 1:
                    out(h)

        @block.vector
        def _(dve):
            def bias(u):
                h, qi = units[u]
                w = P * (qi + 1)
                dve.wait_ge(scored, u + 1)
                if u >= 2:
                    dve.wait_ge(mixed, u - 1)
                for i in range(2):
                    ins = dve.scalar_tensor_tensor(out=logit[:, u % 2, i, 0:w], in0=c.ps[:, 2 * (u % 2) + i, 0:w],
                                                   scalar=DF_QK ** -0.5, in1=tiles[:, h, SEQ - w:SEQ],
                                                   op0=ALU.mult, op1=ALU.add)
                ins.then_inc(biased, 1)
                dve.drain()
                dve.tensor_reduce(nmax[:, u % 2, :], logit[:, u % 2, :, 0:w], AX, ALU.max)
                dve.drain()
                dve.tensor_scalar(nmax[:, u % 2, :], nmax[:, u % 2, :], -1.0, None, ALU.mult).then_inc(maxed, 1)

            def mix(u):
                h, qi = units[u]
                w = P * (qi + 1)
                dve.wait_ge(exped, u + 1)
                if u >= 2:
                    dve.wait_ge(turned, u - 1)
                dve.reciprocal(recip[:, u % 2, :], total[:, u % 2, :])
                dve.drain()
                dve.tensor_scalar(prob[:, u % 2, 0:w], logit[:, u % 2, 1, 0:w], recip[:, u % 2, 1:2], lam[:, 0:1],
                                  ALU.mult, ALU.mult)
                dve.drain()
                dve.scalar_tensor_tensor(out=prob[:, u % 2, 0:w], in0=logit[:, u % 2, 0, 0:w], scalar=recip[:, u % 2, 0:1],
                                         in1=prob[:, u % 2, 0:w], op0=ALU.mult, op1=ALU.add).then_inc(mixed, 1)

            bias(0)
            for u in range(len(units)):
                if u + 1 < len(units):
                    bias(u + 1)
                mix(u)

        @block.scalar
        def _(act):
            def exps(u):
                h, qi = units[u]
                w = P * (qi + 1)
                act.wait_ge(maxed, u + 1)
                for i in range(2):
                    ins = act.activation(logit[:, u % 2, i, 0:w], logit[:, u % 2, i, 0:w], ACT.Exp,
                                         bias=nmax[:, u % 2, i:i + 1], accum_out=total[:, u % 2, i:i + 1])
                ins.then_inc(exped, 1)

            exps(0)
            for u, (h, qi) in enumerate(units):
                if u + 1 < len(units):
                    exps(u + 1)
                act.wait_ge(turned, u + 1)
                if h >= 2:
                    act.wait_ge(outed, h - 1)
                act.activation(prob_T[:, h % 2, 0:qi + 1, qi * P:(qi + 1) * P],
                               c.ps[:, TURN + u % 2, 0:P * (qi + 1)].rearrange("p (j q) -> p j q", q=P), ACT.Copy)\
                    .then_inc(laid, 1)
                if qi == TT - 1:
                    act.wait_ge(outed, h + 1)
                    b = 64 * (h % 2)
                    act.activation(o_T[b:b + 64, h // 2, :], c.ps[b:b + 64, OUT, :], ACT.Copy).then_inc(kept, 1)


def diff_finish(nc, c, lam, o_T):
    with Stage(nc) as st:
        sq = st.sb("sq", [P, 2, SEQ])
        rstd = st.sb("rstd", [P, 2, SEQ])
        squared, summed, rooted = (st.sem(n) for n in ("squared", "summed", "rooted"))
        block = st.block()

        @block.scalar
        def _(act):
            act.activation(sq[:, :, :], o_T[:, :, :], ACT.Square).then_inc(squared, 1)
            act.wait_ge(summed, 1)
            act.activation(rstd[:, :, :], c.ps[:, 0:2, :], ACT.Sqrt, scale=1.0 / DF_V, bias=c.eps[:, :]).then_inc(rooted, 1)

        @block.tensor
        def _(pe):
            pe.wait_ge(squared, 1)
            for k in range(2):
                mm = pe.matmul(c.ps[:, k, :], c.ones64[:, :], sq[:, k, :], start=True, stop=True)
            mm.then_inc(summed, 1)

        @block.vector
        def _(dve):
            dve.wait_ge(rooted, 1)
            dve.reciprocal(rstd[:, :, :], rstd[:, :, :])
            dve.drain()
            for k in range(2):
                dve.scalar_tensor_tensor(out=c.y_T[:, 6 + k, :], in0=o_T[:, k, :], scalar=lam[:, 1:2], in1=rstd[:, k, :],
                                         op0=ALU.mult, op1=ALU.mult)


def project_out(nc, c, w, src, dst, add):
    with Stage(nc) as st:
        wo = st.sb("wo", [P, 4, D])
        loaded = [st.sem(f"loaded{s}") for s in range(4)]
        used = st.sem("used")
        block = st.block()

        @block.sync
        def _(sp):
            for k in range(KD):
                if k >= 4:
                    sp.wait_ge(used, k - 3)
                sp.dma_start(wo[:, k % 4, :], w[k * P:(k + 1) * P, :]).then_inc(loaded[k % 4], 16)

        @block.tensor
        def _(pe):
            for k in range(KD):
                pe.wait_ge(loaded[k % 4], 16 * (k // 4) + 16)
                for n in range(KD):
                    mm = pe.matmul(c.ps[:, n, :], wo[:, k % 4, n * P:(n + 1) * P], src[:, k, :],
                                   start=(k == 0), stop=(k == KD - 1))
                mm.then_inc(used, 1)

        @block.vector
        def _(dve):
            dve.wait_ge(used, KD)
            for n in range(KD):
                if add:
                    dve.tensor_tensor(dst[:, n, :], dst[:, n, :], c.ps[:, n, :], ALU.add)
                else:
                    dve.tensor_copy(dst[:, n, :], c.ps[:, n, :])


def first_mixer(nc, c, L, w_in, w_out, tiles, lam_init):
    with ExitStack() as ctx:
        def sb(name, shape):
            return ctx.enter_context(nc.sbuf_tensor(f"{name}_{nc.next_id()}", shape, F32))
        m = Mixer(nc, ctx)
        first_mixer_projections(nc, c, m, L, w_in)
        lam = sb("lam", [P, 2])
        with ExitStack() as inner:
            def isb(name, shape):
                return inner.enter_context(nc.sbuf_tensor(f"{name}_{nc.next_id()}", shape, F32))
            rows = isb("acs", [8, SEQ]), isb("negM", [4, SEQ]), isb("negm", [4, SEQ])
            cols = isb("cols", [P, TT, 20])
            xdt = isb("xdt", [P, TT, SEQ])
            y_ssm, num, den = isb("y_ssm", [P, 4, SEQ]), isb("num", [P, 2, SEQ]), isb("den", [P, 2, SEQ])
            gates(nc, c, m, rows, cols)
            conv(nc, c, m, xdt, cols)
            recurrences(nc, c, m, rows, cols, xdt, y_ssm, num, den)
            finish_recurrences(nc, c, m, rows, y_ssm, num, den)
        o_T = sb("o_T", [P, 2, SEQ])
        diff_prepare(nc, c, m, lam, lam_init)
        diff_attention(nc, c, m, tiles, lam, o_T)
        diff_finish(nc, c, lam, o_T)
    project_out(nc, c, w_out, c.y_T, c.x_T, True)


LRU_X, LRU_G, NSA_Q, NSA_KV, NSA_GATE = 0, 1024, 2048, 3072, 4608
GLA_Q, GLA_K, GLA_V, GLA_OG, GLA_LR, MERGE = 4656, 5168, 5680, 6704, 7728, 7744
N_HEADS, N_KV, N_DIM = 16, 4, 64
GROUP = N_HEADS // N_KV
TAPS, STRIDE, HIDDEN = 32, 16, 256
N_CMP = SEQ // STRIDE - 1
G_HEADS, G_DV, G_CHUNK = 4, 256, 32
G_CHUNKS = SEQ // G_CHUNK
LRU_C = 8.0


def lru_params(nc, ctx, W):
    def sb(name, shape):
        return ctx.enter_context(nc.sbuf_tensor(f"{name}_{nc.next_id()}", shape, F32))
    q = {"conv_w": sb("conv_w", [P, 8, 4]), "conv_b": sb("conv_b", [P, 8]), "b_gates": sb("b_gates", [P, 2, 8]),
         "lam": sb("lru_lam", [P, 8])}
    loads = [(q["conv_b"][:, :], W["conv_b"].rearrange("(k p) -> p k", p=P)),
             (q["lam"][:, :], W["lru_lambda"].rearrange("(k p) -> p k", p=P))]
    for g in range(2):
        loads.append((q["b_gates"][:, g, :], W["lru_b_gates"][g].rearrange("(k p) -> p k", p=P)))
    for k in range(8):
        loads.append((q["conv_w"][:, k, :], W["conv_w"][:, k * P:(k + 1) * P].rearrange("t p -> p t")))
    return q, loads


def lru_mixer(nc, c, q, w_gates, xa, ga, y):
    with Stage(nc) as st:
        wg = st.sb("wg", [P, 2, 8, P])
        xc = st.sb("xc", [P, 8, SEQ])
        r = st.sb("r", [P, 8, SEQ])
        i = st.sb("i", [P, 8, SEQ])
        z, w, w2, s = (st.sb(n, [P, 8]) for n in ("z", "w", "w2", "s"))
        w_loaded, convolved, gated, free, opened = (st.sem(n) for n in ("w_loaded", "convolved", "gated", "free", "opened"))
        mixed = st.sem("mixed")
        z_ready, coef, tanhed, u_ready, rooted, scanned, gelued = (
            st.sem(n) for n in ("z_ready", "coef", "tanhed", "u_ready", "rooted", "scanned", "gelued"))
        block = st.block()

        @block.sync
        def _(sp):
            for g in range(2):
                sp.dma_start(wg[:, g, :, :], w_gates[g].rearrange("n c e -> c n e")).then_inc(w_loaded, 16)

        @block.vector
        def _(dve):
            dve.wait_ge(z_ready, 1)
            dve.tensor_scalar(w[:, :], z[:, :], 2.0, None, ALU.add)
            dve.drain()
            dve.reciprocal(w[:, :], w[:, :])
            dve.drain()
            dve.tensor_tensor(w[:, :], w[:, :], z[:, :], ALU.mult)
            dve.drain()
            dve.tensor_tensor(w2[:, :], w[:, :], w[:, :], ALU.mult)
            dve.drain()
            dve.tensor_scalar(s[:, :], w2[:, :], 2.0 / 19, None, ALU.mult)
            for n in range(17, 1, -2):
                dve.drain()
                dve.scalar_tensor_tensor(out=s[:, :], in0=s[:, :], scalar=2.0 / n, in1=w2[:, :], op0=ALU.add, op1=ALU.mult)
            dve.drain()
            dve.scalar_tensor_tensor(out=s[:, :], in0=s[:, :], scalar=2.0, in1=w[:, :], op0=ALU.add, op1=ALU.mult)
            dve.tensor_scalar(z[:, :], q["lam"][:, :], -1.0, 0.0, ALU.mult, ALU.max)
            dve.drain()
            dve.tensor_tensor(s[:, :], s[:, :], z[:, :], ALU.add)
            dve.drain()
            dve.tensor_scalar(s[:, :], s[:, :], LRU_C, None, ALU.mult)
            for k in range(8):
                dve.tensor_scalar(xc[:, k, :], xa[:, k, :], q["conv_w"][:, k, 3:4], q["conv_b"][:, k:k + 1], ALU.mult, ALU.add)
            for t in range(1, 4):
                dve.drain()
                for k in range(8):
                    ins = dve.scalar_tensor_tensor(out=xc[:, k, t:], in0=xa[:, k, 0:SEQ - t],
                                                   scalar=q["conv_w"][:, k, 3 - t:4 - t], in1=xc[:, k, t:],
                                                   op0=ALU.mult, op1=ALU.add)
                    if t == 3:
                        ins.then_inc(convolved, 1)
            for k in range(8):
                dve.wait_ge(opened, 2 * k + 2)
                dve.tensor_scalar(r[:, k, :], r[:, k, :], s[:, k:k + 1], None, ALU.mult).then_inc(coef, 1)
                dve.tensor_tensor(i[:, k, :], i[:, k, :], xc[:, k, :], ALU.mult).then_inc(mixed, 1)
            dve.wait_ge(tanhed, 2)
            dve.tensor_tensor(xa[:, :, :], r[:, :, :], r[:, :, :], ALU.mult)
            dve.drain()
            dve.scalar_tensor_tensor(out=xa[:, :, :], in0=xa[:, :, :], scalar=1.0, in1=xc[:, :, :],
                                     op0=ALU.add, op1=ALU.mult).then_inc(u_ready, 1)
            dve.wait_ge(rooted, 1)
            dve.tensor_tensor(xa[:, :, :], xa[:, :, :], i[:, :, :], ALU.mult)
            dve.drain()
            for k in range(8):
                dve.tensor_tensor_scan(xc[:, k, :], r[:, k, :], xa[:, k, :], 0.0, ALU.mult, ALU.add)
            dve.drain()
            dve.wait_ge(gelued, 1)
            dve.tensor_tensor(y[:, :, :], xc[:, :, :], ga[:, :, :], ALU.mult)

        @block.tensor
        def _(pe):
            pe.wait_ge(w_loaded, 32)
            for k in range(8):
                pe.wait_ge(convolved, k + 1)
                if k == 0:
                    pe.wait_ge(convolved, 8)
                for g in range(2):
                    n = 2 * k + g
                    if n >= 4:
                        pe.wait_ge(opened, n - 3)
                    pe.matmul(c.ps[:, n % 4, :], wg[:, g, k, :], xc[:, k, :], start=True, stop=True).then_inc(gated, 1)

        @block.scalar
        def _(act):
            act.activation(z[:, :], q["lam"][:, :], ACT.Abs)
            act.drain()
            act.activation(z[:, :], z[:, :], ACT.Exp, scale=-1.0).then_inc(z_ready, 1)
            act.activation(ga[:, :, :], ga[:, :, :], ACT.Gelu_apprx_tanh).then_inc(gelued, 1)
            for k in range(8):
                for g, to in enumerate((r, i)):
                    act.wait_ge(gated, 2 * k + g + 1)
                    act.activation(to[:, k, :], c.ps[:, (2 * k + g) % 4, :], ACT.Sigmoid,
                                   bias=q["b_gates"][:, g, k:k + 1]).then_inc(opened, 1)
            act.wait_ge(coef, 8)
            act.wait_ge(mixed, 8)
            act.activation(xc[:, :, :], r[:, :, :], ACT.Tanh)
            act.drain().then_inc(tanhed, 1)
            act.activation(r[:, :, :], r[:, :, :], ACT.Exp, scale=-1.0).then_inc(tanhed, 1)
            act.wait_ge(u_ready, 1)
            act.activation(xa[:, :, :], xa[:, :, :], ACT.Sqrt).then_inc(rooted, 1)


class Nsa:
    def __init__(self, nc, ctx):
        def sb(name, shape):
            return ctx.enter_context(nc.sbuf_tensor(f"{name}_{nc.next_id()}", shape, F32))
        self.q = sb("q", [P, 8, SEQ])
        self.k_slc = sb("k_slc", [P, N_KV, SEQ])
        self.k_win = sb("k_win", [P, N_KV, SEQ])
        self.v_slc = sb("v_slc", [P, TT, 256])
        self.v_win = sb("v_win", [P, TT, 256])
        self.gate = sb("gate", [P, TT, 3 * N_HEADS])
        self.k_cmp = sb("k_cmp", [P, N_KV, 32])
        self.v_cmp = sb("v_cmp", [P, N_KV, N_DIM])


def spread_keys(nc, c, n, kk):
    with Stage(nc) as st:
        block = st.block()

        @block.scalar
        def _(act):
            for i, dst in enumerate((n.k_slc, n.k_win)):
                for g in range(N_KV):
                    b = 64 * (g % 2)
                    act.activation(dst[0:64, g, :], kk[b:b + 64, 2 * i + g // 2, :], ACT.Copy)
            act.activation(n.gate[:, :, :], n.gate[:, :, :], ACT.Sigmoid)

        @block.vector
        def _(dve):
            for i, dst in enumerate((n.k_slc, n.k_win)):
                for g in range(N_KV):
                    b = 64 * (g % 2)
                    dve.tensor_copy(dst[64:P, g, :], kk[b:b + 64, 2 * i + g // 2, :])


def compress(nc, c, n, kv, pos, w1, w2):
    with Stage(nc) as st:
        base = st.sb("base", [64, 2, N_KV, SEQ])
        tap = st.sb("tap", [64, 2, 2, N_KV, SEQ])
        pos_T = st.sb("pos_T", [64, 2, TAPS])
        w1s = st.sb("w1s", [64, 2, TAPS // 2, HIDDEN])
        w2s = st.sb("w2s", [P, 2, 2, P])
        hid = st.sb("hid", [P, 2, 2, N_KV, 32])
        hid4 = st.sb("hid4", [P, 2, N_KV, GROUP, 32])
        pos_loaded, w2_loaded, moved, tapped, hidden, netted, spread, outed, multiplied = (
            st.sem(x) for x in ("pos_loaded", "w2_loaded", "moved", "tapped", "hidden", "netted", "spread", "outed",
                                "multiplied"))
        w1_loaded = [st.sem(f"w1_loaded{s}") for s in range(2)]
        block = st.block()

        @block.sync
        def _(sp):
            with nc.allow_non_contiguous_dma(reason="small positions, turned"):
                for i in range(2):
                    sp.dma_start(pos_T[:, i, :], pos[i].rearrange("l d -> d l")).then_inc(pos_loaded, 16)
            for i in range(2):
                for half in range(2):
                    u = 2 * i + half
                    if u >= 2:
                        sp.wait_ge(multiplied, u - 1)
                    sp.dma_start(w1s[:, half, :, :],
                                 w1[i, half * 1024:(half + 1) * 1024, :].rearrange("(l d) f -> d l f", d=N_DIM))\
                        .then_inc(w1_loaded[half], 16)
                for twice in range(2):
                    sp.dma_start(w2s[:, i, :, 64 * twice:64 * twice + 64], w2[i].rearrange("(k p) d -> p k d", p=P))\
                        .then_inc(w2_loaded, 16)

        @block.scalar
        def _(act):
            for i in range(2):
                for g in range(N_KV):
                    b = 64 * (g % 2)
                    ins = act.activation(base[:, i, g, :], kv[b:b + 64, 2 * i + g // 2, :], ACT.Copy)
            ins.then_inc(moved, 1)
            for i in range(2):
                act.wait_ge(hidden, i + 1)
                for k in range(2):
                    ins = act.activation(hid[:, i, k, :, 0:N_CMP],
                                         c.ps[:, 2 * i + k, 0:N_KV * N_CMP].rearrange("p (g n) -> p g n", n=N_CMP),
                                         ACT.Gelu_apprx_tanh)
                ins.then_inc(netted, 1)
            act.wait_ge(outed, 1)
            act.activation(n.k_cmp[:, :, 0:N_CMP], c.ps[:, 4, 0:N_KV * N_CMP].rearrange("p (g n) -> p g n", n=N_CMP), ACT.Copy)
            act.wait_ge(outed, 2)
            act.activation(n.v_cmp[:, :, :], c.ps[:, 5, 0:N_KV * N_DIM].rearrange("p (g d) -> p g d", d=N_DIM), ACT.Copy)

        @block.vector
        def _(dve):
            dve.memset(hid[:, :, :, :, N_CMP:32], 0.0)
            dve.wait_ge(pos_loaded, 32)
            dve.wait_ge(moved, 1)
            for i in range(2):
                for half in range(2):
                    add = pos_T[:, i, 16 * half:16 * half + 16].rearrange("p (o l) -> p o l", o=1)
                    ins = dve.tensor_tensor(tap[:, i, half, :, :].rearrange("p g (n l) -> p (g n) l", l=16),
                                            base[:, i, :, :].rearrange("p g (n l) -> p (g n) l", l=16),
                                            add.to_broadcast([64, N_KV * 32, 16]), ALU.add)
            ins.then_inc(tapped, 1)
            dve.drain()
            dve.wait_ge(netted, 2)
            for k in range(2):
                ins = dve.tensor_copy(hid4[:, k, :, :, :],
                                      hid[:, 1, k, :, :].rearrange("p g (o n) -> p g o n", o=1)
                                      .to_broadcast([P, N_KV, GROUP, 32]))
            ins.then_inc(spread, 1)

        @block.tensor
        def _(pe):
            pe.wait_ge(tapped, 1)
            for i in range(2):
                for half in range(2):
                    pe.wait_ge(w1_loaded[half], 16 * i + 16)
                    for k in range(2):
                        for l in range(16):
                            src = tap[:, i, half, :, :].rearrange("p g (n l) -> p g n l", l=16)[:, :, half:half + N_CMP, l]
                            mm = pe.matmul(c.ps[:, 2 * i + k, 0:N_KV * N_CMP], w1s[:, half, l, k * P:(k + 1) * P], src,
                                           start=(half == 0 and l == 0), stop=(half == 1 and l == 15))
                    mm.then_inc(multiplied, 1)
                    if half == 1:
                        pe.wait_ge(multiplied, 2 * i + 2)
                        pe.drain().then_inc(hidden, 1)
            pe.wait_ge(w2_loaded, 64)
            pe.wait_ge(netted, 2)
            for k in range(2):
                mm = pe.matmul(c.ps[:, 4, 0:N_KV * N_CMP], w2s[:, 0, k, :], hid[:, 0, k, :, 0:N_CMP], start=(k == 0), stop=(k == 1))
            mm.then_inc(outed, 1)
            pe.wait_ge(spread, 1)
            for g in range(N_KV):
                for k in range(2):
                    mm = pe.matmul(c.ps[:, 5, g * N_DIM:(g + 1) * N_DIM], hid4[:, k, g, :, :].rearrange("p r n -> p (r n)"),
                                   w2s[:, 1, k, 0:N_DIM], start=(k == 0), stop=(k == 1))
            mm.then_inc(outed, 1)


def compressed_scores(nc, c, n, tiles):
    with Stage(nc) as st:
        e = st.sb("e", [P, 2, N_HEADS, 32])
        mx = st.sb("mx", [P, 2, N_HEADS])
        tot = st.sb("tot", [P, 2, N_HEADS])
        scored, shifted, exped, ready, turned, laid = (
            st.sem(x) for x in ("scored", "shifted", "exped", "ready", "turned", "laid"))
        block = st.block()

        def wide(ap, w):
            return ap.rearrange("p (h o) -> p h o", o=1).to_broadcast([P, N_HEADS, w])

        @block.tensor
        def _(pe):
            for qi in range(TT):
                nv = 8 * qi + 7
                if qi >= 2:
                    pe.wait_ge(shifted, qi - 1)
                for h in range(N_HEADS):
                    b = 64 * (h % 2)
                    at = 32 * (h // 2)
                    mm = pe.matmul(c.ps[:, 2 * (qi % 2) + h % 2, at:at + nv], n.q[b:b + 64, h // 2, qi * P:(qi + 1) * P],
                                   n.k_cmp[b:b + 64, h // GROUP, 0:nv], start=True, stop=True)
                mm.then_inc(scored, 1)
                pe.wait_ge(ready, qi + 1)
                if qi >= 1:
                    pe.wait_ge(laid, qi)
                for g in range(N_KV):
                    mm = pe.transpose(c.ps[:, 4, g * P:(g + 1) * P],
                                      e[:, qi % 2, GROUP * g:GROUP * (g + 1), :].rearrange("p h n -> p (h n)"), c.ident[:, :])
                mm.then_inc(turned, 1)

        @block.vector
        def _(dve):
            dve.memset(e[:, :, :, :], 0.0)
            for qi in range(TT):
                nv = 8 * qi + 7
                s = qi % 2
                dve.drain()
                dve.wait_ge(scored, qi + 1)
                if qi >= 2:
                    dve.wait_ge(turned, qi - 1)
                at = 415 - P * qi
                for half in range(2):
                    dve.scalar_tensor_tensor(out=e[:, s, half::2, 0:nv],
                                             in0=c.ps[:, 2 * s + half, 0:256].rearrange("p (h n) -> p h n", n=32)[:, :, 0:nv],
                                             scalar=N_DIM ** -0.5, in1=tiles[:, half::2, at:at + 16 * nv - 15:16],
                                             op0=ALU.mult, op1=ALU.add)
                dve.drain()
                dve.tensor_reduce(mx[:, s, :], e[:, s, :, 0:nv], AX, ALU.max)
                dve.drain()
                dve.tensor_scalar(mx[:, s, :], mx[:, s, :], MASKED / 100, None, ALU.max)
                dve.drain()
                dve.tensor_tensor(e[:, s, :, 0:nv], e[:, s, :, 0:nv], wide(mx[:, s, :], nv), ALU.subtract).then_inc(shifted, 1)
                dve.wait_ge(exped, qi + 1)
                dve.reduce_sum(tot[:, s, :], e[:, s, :, 0:nv], AX)
                dve.drain()
                dve.tensor_scalar(tot[:, s, :], tot[:, s, :], 1e-30, None, ALU.max)
                dve.drain()
                dve.reciprocal(tot[:, s, :], tot[:, s, :])
                dve.drain()
                dve.tensor_tensor(tot[:, s, :], tot[:, s, :], n.gate[:, qi, 0:N_HEADS], ALU.mult)
                dve.drain()
                dve.tensor_tensor(e[:, s, :, 0:nv], e[:, s, :, 0:nv], wide(tot[:, s, :], nv), ALU.mult).then_inc(ready, 1)

        @block.scalar
        def _(act):
            for qi in range(TT):
                nv = 8 * qi + 7
                act.wait_ge(shifted, qi + 1)
                act.activation(e[:, qi % 2, :, 0:nv], e[:, qi % 2, :, 0:nv], ACT.Exp).then_inc(exped, 1)
                act.wait_ge(turned, qi + 1)
                act.activation(n.p_cmp[:, :, qi * P:(qi + 1) * P], c.ps[:, 4, :].rearrange("p (g q) -> p g q", q=P), ACT.Copy)\
                    .then_inc(laid, 1)


def nsa_attention(nc, c, n, tiles, y):
    units = [(h, qi) for h in range(N_HEADS) for qi in range(TT)]
    with Stage(nc) as st:
        logit = st.sb("logit", [P, 2, 2, SEQ])
        prob_T = st.sb("prob_T", [P, 2, 2, TT, SEQ])
        nmax = st.sb("nmax", [P, 2, 2])
        total = st.sb("total", [P, 2, 2])
        recip = st.sb("recip", [P, 2, 2])
        scored, biased, maxed, exped, scaled, turned, laid, outed, kept = (
            st.sem(x) for x in ("scored", "biased", "maxed", "exped", "scaled", "turned", "laid", "outed", "kept"))
        block = st.block()
        TURN, OUT = 4, 6

        def first_key(i, qi):
            return 0 if i == 0 else max(0, qi - 2)

        @block.tensor
        def _(pe):
            def score(u):
                h, qi = units[u]
                if u >= 2:
                    pe.wait_ge(biased, u - 1)
                b, g = 64 * (h % 2), h // GROUP
                for i, k in enumerate((n.k_slc, n.k_win)):
                    k0 = P * first_key(i, qi)
                    mm = pe.matmul(c.ps[:, 2 * (u % 2) + i, 0:P * (qi + 1) - k0], n.q[b:b + 64, h // 2, qi * P:(qi + 1) * P],
                                   k[b:b + 64, g, k0:P * (qi + 1)], start=True, stop=True)
                mm.then_inc(scored, 1)

            def turn(u):
                h, qi = units[u]
                pe.wait_ge(scaled, u + 1)
                if u >= 1:
                    pe.wait_ge(laid, 2 * u)
                for i in range(2):
                    for j in range(qi + 1 - first_key(i, qi)):
                        mm = pe.transpose(c.ps[:, TURN + i, j * P:(j + 1) * P], logit[:, u % 2, i, j * P:(j + 1) * P], c.ident[:, :])
                mm.then_inc(turned, 1)

            def out(h):
                pe.wait_ge(laid, 2 * TT * (h + 1))
                if h >= 2:
                    pe.wait_ge(kept, h - 1)
                b, g, r = 64 * (h % 2), h // GROUP, h % GROUP
                to = OUT + h % 2
                pe.matmul(c.ps[b:b + 64, to, :], n.v_cmp[32 * r:32 * r + 32, g, :], n.p_cmp[32 * r:32 * r + 32, g, :],
                          start=True, stop=False)
                for i, v in enumerate((n.v_slc, n.v_win)):
                    for j in range(TT):
                        end = SEQ if i == 0 else min(SEQ, P * (j + 3))
                        mm = pe.matmul(c.ps[b:b + 64, to, j * P:end], v[:, j, g * N_DIM:(g + 1) * N_DIM],
                                       prob_T[:, h % 2, i, j, j * P:end], start=False, stop=(i == 1 and j == TT - 1))
                mm.then_inc(outed, 1)

            score(0)
            for u, (h, qi) in enumerate(units):
                if u + 1 < len(units):
                    score(u + 1)
                turn(u)
                if qi == TT - 1:
                    out(h)

        @block.vector
        def _(dve):
            def bias(u):
                h, qi = units[u]
                dve.wait_ge(scored, u + 1)
                if u >= 2:
                    dve.wait_ge(turned, u - 1)
                for i in range(2):
                    w = P * (qi + 1 - first_key(i, qi))
                    ins = dve.scalar_tensor_tensor(out=logit[:, u % 2, i, 0:w], in0=c.ps[:, 2 * (u % 2) + i, 0:w],
                                                   scalar=N_DIM ** -0.5, in1=tiles[:, h, SEQ - w:SEQ],
                                                   op0=ALU.mult, op1=ALU.add)
                ins.then_inc(biased, 1)
                dve.drain()
                if qi >= 2:
                    dve.tensor_tensor(logit[:, u % 2, 1, 0:P], logit[:, u % 2, 1, 0:P], c.winmask[:, :], ALU.add)
                    dve.drain()
                for i in range(2):
                    w = P * (qi + 1 - first_key(i, qi))
                    dve.tensor_reduce(nmax[:, u % 2, i:i + 1], logit[:, u % 2, i, 0:w], AX, ALU.max)
                dve.drain()
                dve.tensor_scalar(nmax[:, u % 2, :], nmax[:, u % 2, :], -1.0, None, ALU.mult).then_inc(maxed, 1)

            def scale(u):
                h, qi = units[u]
                dve.wait_ge(exped, u + 1)
                dve.reciprocal(recip[:, u % 2, :], total[:, u % 2, :])
                dve.drain()
                for i in range(2):
                    w = P * (qi + 1 - first_key(i, qi))
                    at = N_HEADS * (i + 1) + h
                    ins = dve.tensor_scalar(logit[:, u % 2, i, 0:w], logit[:, u % 2, i, 0:w], recip[:, u % 2, i:i + 1],
                                            n.gate[:, qi, at:at + 1], ALU.mult, ALU.mult)
                ins.then_inc(scaled, 1)

            bias(0)
            for u in range(len(units)):
                if u + 1 < len(units):
                    bias(u + 1)
                scale(u)

        @block.scalar
        def _(act):
            def exps(u):
                h, qi = units[u]
                act.wait_ge(maxed, u + 1)
                for i in range(2):
                    w = P * (qi + 1 - first_key(i, qi))
                    ins = act.activation(logit[:, u % 2, i, 0:w], logit[:, u % 2, i, 0:w], ACT.Exp,
                                         bias=nmax[:, u % 2, i:i + 1], accum_out=total[:, u % 2, i:i + 1])
                ins.then_inc(exped, 1)

            exps(0)
            for u, (h, qi) in enumerate(units):
                if u + 1 < len(units):
                    exps(u + 1)
                act.wait_ge(turned, u + 1)
                if h >= 2 and qi == 0:
                    act.wait_ge(outed, h - 1)
                for i in range(2):
                    j0 = first_key(i, qi)
                    act.activation(prob_T[:, h % 2, i, j0:qi + 1, qi * P:(qi + 1) * P],
                                   c.ps[:, TURN + i, 0:P * (qi + 1 - j0)].rearrange("p (j q) -> p j q", q=P), ACT.Copy)\
                        .then_inc(laid, 1)
                if qi == TT - 1:
                    act.wait_ge(outed, h + 1)
                    b = 64 * (h % 2)
                    act.activation(y[b:b + 64, h // 2, :], c.ps[b:b + 64, OUT + h % 2, :], ACT.Copy).then_inc(kept, 1)


class Gla:
    def __init__(self, nc, ctx):
        def sb(name, shape):
            return ctx.enter_context(nc.sbuf_tensor(f"{name}_{nc.next_id()}", shape, F32))
        self.q = sb("gq", [P, 4, SEQ])
        self.k = sb("gk", [P, 4, SEQ])
        self.og = sb("og", [P, 8, SEQ])
        self.v = sb("gv", [P, TT, D])
        self.lr = sb("lr", [16, SEQ])
        self.wa2 = sb("wa2", [16, 512])
        self.ba = sb("ba", [P, 4])
        self.gain = sb("ggain", [P, 2])
        self.k_end = sb("k_end", [P, 4, SEQ])
        self.k_end_t = sb("k_end_t", [P, TT, 4, P])
        self.decay = sb("decay", [P, 4, G_CHUNKS])


def gla_prepare(nc, c, g):
    with Stage(nc) as st:
        x, l, b, d = (st.sb(n, [P, 4, SEQ]) for n in ("x", "l", "b", "d"))
        gated, logged, ready, b_ready, exped, k_ready, turned, q_ready = (
            st.sem(n) for n in ("gated", "logged", "ready", "b_ready", "exped", "k_ready", "turned", "q_ready"))
        block = st.block()

        def chunks(ap):
            return ap.rearrange("p h (c t) -> p (h c) t", t=G_CHUNK)

        @block.tensor
        def _(pe):
            for h in range(G_HEADS):
                mm = pe.matmul(c.ps[:, h, :], g.wa2[:, h * P:(h + 1) * P], g.lr[:, :], start=True, stop=True)
            mm.then_inc(gated, 1)
            pe.wait_ge(k_ready, 1)
            for t in range(TT):
                for h in range(G_HEADS):
                    mm = pe.transpose(c.ps[:, 4 + t, h * P:(h + 1) * P], g.k_end[:, h, t * P:(t + 1) * P], c.ident[:, :])
            mm.then_inc(turned, 1)

        @block.scalar
        def _(act):
            act.wait_ge(gated, 1)
            for h in range(G_HEADS):
                act.activation(x[:, h, :], c.ps[:, h, :], ACT.Identity, bias=g.ba[:, h:h + 1])
            act.drain()
            act.activation(l[:, :, :], x[:, :, :], ACT.Abs)
            act.drain()
            act.activation(l[:, :, :], l[:, :, :], ACT.Exp, scale=-1.0)
            act.drain()
            act.activation(l[:, :, :], l[:, :, :], ACT.Ln, bias=c.one[:, :])
            act.drain().then_inc(logged, 1)
            act.wait_ge(b_ready, 1)
            act.activation(x[:, :, :], b[:, :, :], ACT.Exp, scale=1.0 / 16)
            act.activation(l[:, :, :], b[:, :, :], ACT.Exp, scale=-1.0 / 16)
            act.activation(g.decay[:, :, :].rearrange("p h c -> p (h c)"), chunks(b[:, :, :])[:, :, G_CHUNK - 1], ACT.Exp,
                           scale=1.0 / 16)
            act.activation(d[:, :, :], d[:, :, :], ACT.Exp, scale=1.0 / 16)
            act.drain().then_inc(exped, 1)
            act.wait_ge(turned, 1)
            act.activation(g.k_end_t[:, :, :, :].rearrange("p t h d -> p t (h d)"), c.ps[:, 4:8, :], ACT.Copy)

        @block.vector
        def _(dve):
            dve.wait_ge(logged, 1)
            dve.scalar_tensor_tensor(out=x[:, :, :], in0=x[:, :, :], scalar=0.0, in1=l[:, :, :], op0=ALU.min, op1=ALU.subtract)
            dve.drain()
            for h in range(G_HEADS):
                dve.tensor_tensor_scan(b[:, h, :], c.scanone[:, :], x[:, h, :], 0.0, ALU.mult, ALU.add)
            dve.drain()
            last = chunks(b[:, :, :])[:, :, G_CHUNK - 1:G_CHUNK].to_broadcast([P, 4 * G_CHUNKS, G_CHUNK])
            dve.tensor_tensor(chunks(d[:, :, :]), last, chunks(b[:, :, :]), ALU.subtract)
            dve.drain().then_inc(b_ready, 1)
            dve.wait_ge(exped, 1)
            dve.tensor_tensor(g.k_end[:, :, :], g.k[:, :, :], d[:, :, :], ALU.mult).then_inc(k_ready, 1)
            dve.tensor_tensor(g.k[:, :, :], g.k[:, :, :], l[:, :, :], ALU.mult)
            dve.scalar_tensor_tensor(out=g.q[:, :, :], in0=g.q[:, :, :], scalar=P ** -0.5, in1=x[:, :, :],
                                     op0=ALU.mult, op1=ALU.mult)


def gla_scan(nc, c, g, o_T):
    with Stage(nc) as st:
        att = st.sb("att", [P, TT, G_HEADS, P])
        state = st.sb("state", [P, 2, G_HEADS, G_DV])
        scored, masked, updated, stepped, outed, kept = (
            st.sem(n) for n in ("scored", "masked", "updated", "stepped", "outed", "kept"))
        block = st.block()

        @block.tensor
        def _(pe):
            def scores(t):
                if t >= 1:
                    pe.wait_ge(masked, t)
                for h in range(G_HEADS):
                    mm = pe.matmul(c.ps[:, 4, h * P:(h + 1) * P], g.k[:, h, t * P:(t + 1) * P], g.q[:, h, t * P:(t + 1) * P],
                                   start=True, stop=True)
                mm.then_inc(scored, 1)

            for t in range(TT):
                scores(t)
                pe.wait_ge(masked, t + 1)
                if t >= 2:
                    pe.wait_ge(kept, t - 1)
                o = 2 * (t % 2)
                for h in range(G_HEADS):
                    for e in range(2):
                        n = 2 * h + e
                        pe.matmul(c.ps[:, o + n // 4, (n % 4) * P:(n % 4 + 1) * P], g.v[:, t, h * G_DV + e * P:h * G_DV + (e + 1) * P],
                                  att[:, t, h, :], start=(n % 4 == 0), stop=False, skip_group_check=True)
                for s in range(4):
                    k = 4 * t + s
                    if k >= 1:
                        pe.wait_ge(stepped, k)
                        for h in range(G_HEADS):
                            for e in range(2):
                                n = 2 * h + e
                                at = (n % 4) * P + s * G_CHUNK
                                mm = pe.matmul(c.ps[:, o + n // 4, at:at + G_CHUNK], state[:, k % 2, h, e * P:(e + 1) * P],
                                               g.q[:, h, k * G_CHUNK:(k + 1) * G_CHUNK], start=False, stop=(s == 3),
                                               skip_group_check=True)
                    if s == 3:
                        mm.then_inc(outed, 1)
                    if k + 1 < G_CHUNKS:
                        b = 32 * s
                        for h in range(G_HEADS):
                            mm = pe.matmul(c.ps[:, 6 + h // 2, (h % 2) * G_DV:(h % 2 + 1) * G_DV], g.k_end_t[b:b + 32, t, h, :],
                                           g.v[b:b + 32, t, h * G_DV:(h + 1) * G_DV], start=True, stop=True)
                        mm.then_inc(updated, 1)

        @block.vector
        def _(dve):
            for t in range(TT):
                dve.wait_ge(scored, t + 1)
                dve.tensor_tensor(att[:, t, :, :], c.ps[:, 4, :].rearrange("p (h t) -> p h t", t=P),
                                  c.chunkmask[:, :].rearrange("p (o t) -> p o t", o=1).to_broadcast([P, G_HEADS, P]), ALU.mult)\
                    .then_inc(masked, 1)
                for s in range(4):
                    k = 4 * t + s
                    if k + 1 == G_CHUNKS:
                        break
                    dve.wait_ge(updated, k + 1)
                    dve.drain()
                    for h in range(G_HEADS):
                        new = c.ps[:, 6 + h // 2, (h % 2) * G_DV:(h % 2 + 1) * G_DV]
                        if k == 0:
                            ins = dve.tensor_copy(state[:, 1, h, :], new)
                        else:
                            ins = dve.scalar_tensor_tensor(out=state[:, (k + 1) % 2, h, :], in0=state[:, k % 2, h, :],
                                                           scalar=g.decay[:, h, k:k + 1], in1=new, op0=ALU.mult, op1=ALU.add)
                    ins.then_inc(stepped, 1)

        @block.scalar
        def _(act):
            for t in range(TT):
                act.wait_ge(outed, t + 1)
                o = 2 * (t % 2)
                act.activation(o_T[:, :, t * P:(t + 1) * P], c.ps[:, o:o + 2, :].rearrange("p b (n q) -> p (b n) q", q=P), ACT.Copy)\
                    .then_inc(kept, 1)


def gla_finish(nc, c, g, o_T, y):
    with Stage(nc) as st:
        sq = st.sb("sq", [P, 8, SEQ])
        rstd = st.sb("rstd", [P, 4, SEQ])
        squared, summed, rooted, opened = (st.sem(n) for n in ("squared", "summed", "rooted", "opened"))
        block = st.block()

        @block.scalar
        def _(act):
            act.activation(sq[:, :, :], o_T[:, :, :], ACT.Square).then_inc(squared, 1)
            act.activation(g.og[:, :, :], g.og[:, :, :], ACT.Silu).then_inc(opened, 1)
            act.wait_ge(summed, 1)
            act.activation(rstd[:, :, :], c.ps[:, 0:4, :], ACT.Sqrt, scale=1.0 / G_DV, bias=c.eps[:, :]).then_inc(rooted, 1)

        @block.tensor
        def _(pe):
            pe.wait_ge(squared, 1)
            for h in range(G_HEADS):
                for e in range(2):
                    mm = pe.matmul(c.ps[:, h, :], c.ones[:, :], sq[:, 2 * h + e, :], start=(e == 0), stop=(e == 1))
            mm.then_inc(summed, 1)

        @block.vector
        def _(dve):
            dve.wait_ge(opened, 1)
            dve.tensor_tensor(g.og[:, :, :], g.og[:, :, :], o_T[:, :, :], ALU.mult)
            dve.drain()
            dve.wait_ge(rooted, 1)
            dve.reciprocal(rstd[:, :, :], rstd[:, :, :])
            dve.drain()
            for k in range(8):
                dve.scalar_tensor_tensor(out=y[:, k, :], in0=g.og[:, k, :], scalar=g.gain[:, k % 2:k % 2 + 1],
                                         in1=rstd[:, k // 2, :], op0=ALU.mult, op1=ALU.mult)


def merge(nc, c, w_in, w_branch, ys, merged):
    with Stage(nc) as st:
        wg = st.sb("wg", [P, 3, KD, P])
        wb = st.sb("wb", [P, 3, KD, P])
        sig = st.sb("sig", [P, 3, SEQ])
        t = st.sb("t", [P, 3, SEQ])
        w_loaded = [st.sem(f"w_loaded{s}") for s in range(3)]
        done = [st.sem(f"done{s}") for s in range(3)]
        opened = [st.sem(f"opened{s}") for s in range(3)]
        taken = [st.sem(f"taken{s}") for s in range(3)]
        block = st.block()
        g_v = w_in[:, MERGE:MERGE + 3 * D].rearrange("(k p) f -> p k f", p=P)
        b_v = [w_branch[i].rearrange("(k p) f -> p k f", p=P) for i in range(3)]

        def each(eng, body):
            body(0, True)
            with eng.Fori(1, KD) as n:
                body(n, False)

        @block.sync
        def _(sp):
            def load(n, first):
                for i in range(3):
                    if not first:
                        sp.wait_ge(done[i], n)
                    sp.dma_start(wg[:, i, :, :], g_v[:, :, bass.ds(n * P + i * D, P)]).then_inc(w_loaded[i], 16)
                    sp.dma_start(wb[:, i, :, :], b_v[i][:, :, bass.ds(n * P, P)]).then_inc(w_loaded[i], 16)
            each(sp, load)

        @block.tensor
        def _(pe):
            def product(n, first):
                for i in range(3):
                    pe.wait_ge(w_loaded[i], 32 * n + 32)
                    if not first:
                        pe.wait_ge(taken[i], n)
                    for b, w, src in ((i, wg, c.h_T), (3 + i, wb, ys[i])):
                        for k in range(KD):
                            mm = pe.matmul(c.ps[:, b, :], w[:, i, k, :], src[:, k, :], start=(k == 0), stop=(k == KD - 1))
                    mm.then_inc(done[i], 1)
            each(pe, product)

        @block.scalar
        def _(act):
            def sigmoid(n, first):
                for i in range(3):
                    act.wait_ge(done[i], n + 1)
                    if not first:
                        act.wait_ge(taken[i], n)
                    act.activation(sig[:, i, :], c.ps[:, i, :], ACT.Sigmoid).then_inc(opened[i], 1)
            each(act, sigmoid)

        @block.vector
        def _(dve):
            def gate(n, first):
                for i in range(3):
                    dve.wait_ge(opened[i], n + 1)
                    dve.tensor_tensor(t[:, i, :], sig[:, i, :], c.ps[:, 3 + i, :], ALU.mult).then_inc(taken[i], 1)
                dve.drain()
                dve.tensor_tensor(t[:, 0, :], t[:, 0, :], t[:, 1, :], ALU.add)
                dve.drain()
                dve.tensor_tensor(merged[:, bass.ds(n, 1), :], t[:, 0:1, :], t[:, 2:3, :], ALU.add)
                dve.drain()
            each(dve, gate)


def second_block(nc, c, W, scratch):
    w_in = W["w_in"]
    norm(nc, c, W["norm_g"][0])
    with ExitStack() as ctx:
        def sb(name, shape, to=ctx):
            return to.enter_context(nc.sbuf_tensor(f"{name}_{nc.next_id()}", shape, F32))
        y_b = c.y_T
        with ExitStack() as inner:
            n = Nsa(nc, inner)
            with ExitStack() as early:
                kk, kv = sb("kk", [P, 4, SEQ], early), sb("kv", [P, 4, SEQ], early)
                at = NSA_KV
                project(nc, c, w_in,
                        [(NSA_Q, 8, n.q[:, :, :]), (at, 4, kv[:, :, :]), (at + 512, 2, kk[:, 0:2, :]),
                         (at + 1024, 2, kk[:, 2:4, :])],
                        [], [(at + 768, 256, n.v_slc[:, :, :]), (at + 1280, 256, n.v_win[:, :, :]),
                             (NSA_GATE, 3 * N_HEADS, n.gate[:, :, :])])
                spread_keys(nc, c, n, kk)
                compress(nc, c, n, kv, W["cmp_pos"], W["cmp_w1"], W["cmp_w2"])
            n.p_cmp = sb("p_cmp", [P, N_KV, SEQ], inner)
            tiles = sb("tiles", [P, N_HEADS, SEQ], inner)
            bias_rows(nc, c, W["rel_table"], N_HEADS, scratch)
            bias_tiles(nc, c, scratch, N_HEADS, tiles)
            compressed_scores(nc, c, n, tiles)
            nsa_attention(nc, c, n, tiles, y_b)
        y_a, y_c = sb("y_a", [P, KD, SEQ]), sb("y_c", [P, KD, SEQ])
        with ExitStack() as inner:
            xa, ga = sb("xa", [P, 8, SEQ], inner), sb("ga", [P, 8, SEQ], inner)
            q, loads = lru_params(nc, inner, W)
            project(nc, c, w_in, [(LRU_X, 8, xa[:, :, :]), (LRU_G, 8, ga[:, :, :])], [], [], loads)
            lru_mixer(nc, c, q, W["lru_w_gates"], xa, ga, y_a)
        with ExitStack() as inner:
            g = Gla(nc, inner)
            params = [(g.wa2[:, :], W["gla_wa2"]), (g.ba[:, :], W["gla_ba"].rearrange("(k p) -> p k", p=P)),
                      (g.gain[:, :], W["gla_norm"].rearrange("(k p) -> p k", p=P))]
            project(nc, c, w_in, [(GLA_Q, 4, g.q[:, :, :]), (GLA_K, 4, g.k[:, :, :]), (GLA_OG, 8, g.og[:, :, :])],
                    [(GLA_LR, 16, g.lr[:, :])],
                    [(GLA_V + 256 * i, 256, g.v[:, :, 256 * i:256 * (i + 1)]) for i in range(4)], params)
            gla_prepare(nc, c, g)
            gla_scan(nc, c, g, y_c)
            gla_finish(nc, c, g, y_c, y_c)
        merged = sb("merged", [P, KD, SEQ])
        merge(nc, c, w_in, W["w_branch"], [y_a, y_b, y_c], merged)
        project_out(nc, c, W["w_out"], merged, c.h_T, False)
        norm(nc, c, W["norm_g"][1], src=c.h_T, add_to=c.x_T)
    norm(nc, c, W["norm_g"][2])
    ffn(nc, c, W["w_ffn_in"][:, 0:FF], W["w_ffn_in"][:, FF:2 * FF], W["w_ffn_out"], 1.0, dst=c.y_T)
    norm(nc, c, W["norm_g"][3], src=c.y_T, add_to=c.x_T)




FIRST = ["ffn1_norm_w", "ffn1_w_gate", "ffn1_w_up", "ffn1_w_down", "mix_norm_w", "w_in", "mlstm_gate_bias",
         "mlstm_norm_w", "ssm_conv_w", "ssm_conv_b", "ssm_dt_bias", "ssm_A_log", "ssm_D", "ssm_norm_w",
         "diff_q_norm_w", "diff_k_norm_w", "diff_lambda", "diff_subln_w", "w_out", "ffn2_norm_w", "ffn2_w_gate",
         "ffn2_w_up", "ffn2_w_down"]


def lambda_init(nc, c, layer, now):
    with Stage(nc) as st:
        block = st.block()

        @block.vector
        def _(dve):
            for l in range(LAYERS):
                dve.memset(c.lam_init[:, l:l + 1], 0.8 - 0.6 * float(np.exp(-0.3 * l)))
            dve.drain()
            dve.tensor_copy(now[:, :], c.lam_init[:, bass.ds(layer, 1)])


def program(nc, A, out):
    scratch = nc.dram_tensor("bias_scratch", [DF_HEADS + N_HEADS, BACK + SEQ], F32, kind="Internal").ap()
    with ExitStack() as ctx:
        c = Shared(nc, ctx)
        consts(nc, c)
        load_x(nc, c, A["x"])
        with ExitStack() as first:
            tiles = first.enter_context(nc.sbuf_tensor("diff_tiles", [P, DF_HEADS, SEQ], F32))
            now = first.enter_context(nc.sbuf_tensor("lam_init_now", [P, 1], F32))
            bias_rows(nc, c, A["rel_bias"], DF_HEADS, scratch[0:DF_HEADS])
            bias_tiles(nc, c, scratch[0:DF_HEADS], DF_HEADS, tiles)
            with nc.Fori(0, LAYERS) as layer:
                L = {name: A[name][layer] for name in FIRST}
                norm(nc, c, L["ffn1_norm_w"])
                ffn(nc, c, L["ffn1_w_gate"], L["ffn1_w_up"], L["ffn1_w_down"], 0.5)
                norm(nc, c, L["mix_norm_w"])
                lambda_init(nc, c, layer, now)
                first_mixer(nc, c, L, L["w_in"], L["w_out"], tiles, now[:, 0:1])
                norm(nc, c, L["ffn2_norm_w"])
                ffn(nc, c, L["ffn2_w_gate"], L["ffn2_w_up"], L["ffn2_w_down"], 0.5)
        W = {name[:-2]: (ap if name == "rel_table_2" else ap[0]) for name, ap in A.items() if name.endswith("_2")}
        second_block(nc, c, W, scratch[DF_HEADS:])
        store_x(nc, c, out)


_INS = ["x", "ffn1_norm_w", "ffn1_w_gate", "ffn1_w_up", "ffn1_w_down", "mix_norm_w", "w_in", "mlstm_gate_bias",
        "mlstm_norm_w", "ssm_conv_w", "ssm_conv_b", "ssm_dt_bias", "ssm_A_log", "ssm_D", "ssm_norm_w",
        "diff_q_norm_w", "diff_k_norm_w", "diff_lambda", "diff_subln_w", "rel_bias", "w_out", "ffn2_norm_w",
        "ffn2_w_gate", "ffn2_w_up", "ffn2_w_down", "rel_table_2", "norm_g_2", "w_in_2", "conv_w_2", "conv_b_2",
        "lru_w_gates_2", "lru_b_gates_2", "lru_lambda_2", "cmp_pos_2", "cmp_w1_2", "cmp_w2_2", "gla_wa2_2",
        "gla_ba_2", "gla_norm_2", "w_branch_2", "w_out_2", "w_ffn_in_2", "w_ffn_out_2"]
_OUTS = [((1, 512, 1024), "float32")]


def kernel(**inputs):
    import numpy as _np
    import concourse.bacc as _bacc
    from concourse import mybir as _mybir
    from concourse.bass_utils import run_bass_kernel_spmd as _run

    nc = _bacc.Bacc("TRN2", target_bir_lowering=False, num_devices=1)
    arrays, args = {}, {}
    for name in _INS:
        a = _np.ascontiguousarray(inputs[name])
        arrays[f"in_{name}_dram"] = a
        args[name] = nc.dram_tensor(f"in_{name}_dram", a.shape, _mybir.dt.from_np(a.dtype), kind="ExternalInput").ap()
    out = nc.dram_tensor("out_0_dram", _OUTS[0][0], _mybir.dt.from_np(_np.dtype(_OUTS[0][1])), kind="ExternalOutput").ap()
    program(nc, args, out)
    r = _run(nc, [arrays], core_ids=[0])
    return r.results[0]["out_0_dram"]
```

```python
from contextlib import ExitStack, contextmanager

import numpy as np
import concourse.bass as bass
from concourse import mybir

F32 = mybir.dt.float32
F32R = mybir.dt.float32r
ACT = mybir.ActivationFunctionType
ALU = mybir.AluOpType
AX = mybir.AxisListType.X

P = 128
SEQ = 512
TT = SEQ // P
D = 1024
KD = D // P
LAYERS = 2
FF = 2816
KF = FF // P
BANK = 512
EPS = 1e-6
MASKED = -1e30

TRI_W = [SEQ - P * j for j in range(TT)]
TRI_AT = [0, 512, 1024, 896]
TRI = sum(TRI_W)


class Stage:

    def __init__(self, nc):
        self.nc = nc
        self.ctx = ExitStack()
        self.sems = []
        self.engines = None

    def sem(self, name):
        s = self.ctx.enter_context(self.nc.semaphore(name))
        self.sems.append(s)
        return s

    def sb(self, name, shape, dtype=F32):
        return self.ctx.enter_context(self.nc.sbuf_tensor(f"{name}_{self.nc.next_id()}", shape, dtype))

    def block(self):
        self.engines = self.nc.Block(no_gpsimd_drain=True)
        return self.engines.__enter__()

    def __enter__(self):
        return self

    def __exit__(self, kind, value, trace):
        if self.engines is not None:
            self.engines.__exit__(kind, value, trace)
        if kind is None:
            for s in self.sems:
                self.nc.sync.sem_clear(s)
            self.nc.all_engine_barrier()
        return self.ctx.__exit__(kind, value, trace)


def bcast(ap, n):
    return ap.to_broadcast([ap.shape[0], n])


def consts(nc, c):
    with Stage(nc) as st:
        filled = st.sem("filled")
        block = st.block()

        @block.gpsimd
        def _(pool):
            pool.memset(c.ident[:, :], 0.0)
            pool.memset(c.ones[:, :], 1.0)
            pool.memset(c.eps[:, :], EPS)
            pool.memset(c.one[:, :], 1.0)
            pool.memset(c.ones64[:, :], 1.0)
            pool.memset(c.ones32[:, :], 1.0)
            pool.memset(c.bound[:, :], 0.0)
            pool.memset(c.winmask[:, :], 0.0)
            pool.memset(c.sel[:, :, :], 0.0)
            pool.memset(c.selp[:, :, :], 0.0)
            pool.memset(c.chunkmask[:, :], 1.0)
            pool.memset(c.scanone[:, :], 1.0)
            pool.drain()
            pool.affine_select(out=c.ident[:, :], in_=c.ident[:, :], compare_op=ALU.not_equal, fill=1.0,
                               base=0, pattern=[[-1, P]], channel_multiplier=1)
            pool.affine_select(out=c.bound[:, :], in_=c.bound[:, :], compare_op=ALU.is_ge, fill=MASKED,
                               base=0, pattern=[[1, SEQ]], channel_multiplier=-1)
            pool.affine_select(out=c.winmask[:, :], in_=c.winmask[:, :], compare_op=ALU.is_gt, fill=MASKED,
                               base=0, pattern=[[1, P]], channel_multiplier=-1)
            pool.affine_select(out=c.sel[:, :, :], in_=c.sel[:, :, :], compare_op=ALU.not_equal, fill=1.0,
                               base=0, pattern=[[-1, 8], [0, P]], channel_multiplier=1)
            pool.affine_select(out=c.selp[:, :, :], in_=c.selp[:, :, :], compare_op=ALU.not_equal, fill=1.0,
                               base=0, pattern=[[-2, 4], [-1, 2], [0, 64]], channel_multiplier=1)
            m = c.chunkmask[:, :]
            pool.affine_select(out=m, in_=m, compare_op=ALU.is_ge, fill=0.0,
                               base=0, pattern=[[-32, 4], [0, 32]], channel_multiplier=1)
            v = c.scanone[:, :].rearrange("p (c t) -> p c t", t=32)
            pool.memset(v[:, :, 0:1], 0.0)
            for m, b in ((c.ones64, 64), (c.ones32, 32)):
                w = m[:, :]
                pool.affine_select(out=w, in_=w, compare_op=ALU.is_ge, fill=0.0,
                                   base=0, pattern=[[-b, P // b], [0, b]], channel_multiplier=1)
            pool.drain()
            m = c.chunkmask[:, :]
            pool.affine_select(out=m, in_=m, compare_op=ALU.is_ge, fill=0.0,
                               base=0, pattern=[[32, 4], [1, 32]], channel_multiplier=-1)
            for m, b in ((c.ones64, 64), (c.ones32, 32)):
                w = m[:, :]
                pool.affine_select(out=w, in_=w, compare_op=ALU.is_ge, fill=0.0,
                                   base=b - 1, pattern=[[b, P // b], [0, b]], channel_multiplier=-1)
            pool.drain()


def load_x(nc, c, x):
    with Stage(nc) as st:
        xin = st.sb("xin", [P, TT, D])
        x_loaded, turned, kept = st.sem("x_loaded"), st.sem("turned"), st.sem("kept")
        block = st.block()

        @block.sync
        def _(sp):
            sp.dma_start(xin[:, :, :], x[0].rearrange("(t p) d -> p t d", p=P)).then_inc(x_loaded, 16)

        @block.tensor
        def _(pe):
            pe.wait_ge(x_loaded, 16)
            for k in range(KD):
                for t in range(TT):
                    mm = pe.transpose(c.ps[:, k, t * P:(t + 1) * P], xin[:, t, k * P:(k + 1) * P], c.ident[:, :])
                mm.then_inc(turned, 1)

        @block.vector
        def _(dve):
            for k in range(KD):
                dve.wait_ge(turned, k + 1)
                dve.tensor_copy(c.x_T[:, k, :], c.ps[:, k, :])


def store_x(nc, c, out):
    with Stage(nc) as st:
        xo = st.sb("xo", [P, TT, D])
        turned, kept, written = st.sem("turned"), st.sem("kept"), st.sem("written")
        block = st.block()

        @block.tensor
        def _(pe):
            for t in range(TT):
                for k in range(KD):
                    mm = pe.transpose(c.ps[:, 2 * t + k // 4, (k % 4) * P:(k % 4 + 1) * P],
                                      c.x_T[:, k, t * P:(t + 1) * P], c.ident[:, :])
                mm.then_inc(turned, 1)

        @block.vector
        def _(dve):
            for t in range(TT):
                dve.wait_ge(turned, t + 1)
                dve.tensor_copy(xo[:, t, :], c.ps[:, 2 * t:2 * t + 2, :]).then_inc(kept, 1)

        @block.sync
        def _(sp):
            for t in range(TT):
                sp.wait_ge(kept, t + 1)
                sp.dma_start(out[0, t * P:(t + 1) * P, :], xo[:, t, :]).then_inc(written, 16)
            sp.wait_ge(written, 16 * TT)


def norm(nc, c, gain, src=None, add_to=None):
    src = c.x_T if src is None else src
    with Stage(nc) as st:
        sq = st.sb("sq", [P, KD, SEQ])
        rstd = st.sb("rstd", [P, SEQ])
        g = st.sb("g", [P, KD])
        gain_loaded, squared, summed = st.sem("gain_loaded"), st.sem("squared"), st.sem("summed")
        rooted, scaled, halved = st.sem("rooted"), st.sem("scaled"), st.sem("halved")
        block = st.block()

        @block.sync
        def _(sp):
            with nc.allow_non_contiguous_dma(reason="a column of gains"):
                sp.dma_start(g[:, :], gain.rearrange("(k p) -> p k", p=P)).then_inc(gain_loaded, 16)

        @block.tensor
        def _(pe):
            for k in range(KD):
                pe.wait_ge(squared, k + 1)
                mm = pe.matmul(c.ps[:, 0, :], c.ones[:, :], sq[:, k, :], start=(k == 0), stop=(k == KD - 1))
            mm.then_inc(summed, 1)

        @block.scalar
        def _(act):
            for k in range(KD):
                act.activation(sq[:, k, :], src[:, k, :], ACT.Square).then_inc(squared, 1)
            act.wait_ge(summed, 1)
            act.activation(rstd[:, :], c.ps[:, 0, :], ACT.Sqrt, scale=1.0 / D, bias=c.eps[:, :]).then_inc(rooted, 1)
            if add_to is None:
                for k in range(KD):
                    act.wait_ge(scaled, k + 1)
                    act.activation(c.h_hi[:, k, :], sq[:, k, :], ACT.Copy).then_inc(halved, 1)

        @block.vector
        def _(dve):
            dve.wait_ge(rooted, 1)
            dve.reciprocal(rstd[:, :], rstd[:, :])
            dve.drain()
            dve.wait_ge(gain_loaded, 16)
            for k in range(KD):
                dve.scalar_tensor_tensor(out=sq[:, k, :], in0=src[:, k, :], scalar=g[:, k:k + 1], in1=rstd[:, :],
                                         op0=ALU.mult, op1=ALU.mult).then_inc(scaled, 1)
            if add_to is not None:
                dve.drain()
                for k in range(KD):
                    dve.tensor_tensor(add_to[:, k, :], add_to[:, k, :], sq[:, k, :], ALU.add)
            else:
                for k in range(KD):
                    dve.wait_ge(halved, k + 1)
                    dve.tensor_tensor(c.h_lo[:, k, :], sq[:, k, :], c.h_hi[:, k, :].bitcast(F32), ALU.subtract)


class Ring:

    def __init__(self, st, raw=None):
        self.raw = st.sb("raw", [P, 4, KD, P]) if raw is None else raw
        self.hi = st.sb("w_hi", [P, 4, KD, P], F32R)
        self.lo = st.sb("w_lo", [P, 4, KD, P], F32R)
        self.loaded = [st.sem(f"loaded{s}") for s in range(4)]
        self.halved = [st.sem(f"halved{s}") for s in range(4)]
        self.split = [st.sem(f"split{s}") for s in range(4)]
        self.used = [st.sem(f"used{s}") for s in range(4)]

    def load(self, sp, s, n, first, src):
        if not first:
            sp.wait_ge(self.split[s], n)
        sp.dma_start(self.raw[:, s, :, :], src).then_inc(self.loaded[s], 16)

    def high(self, dve, s, n, first):
        dve.wait_ge(self.loaded[s], 16 * n + 16)
        if not first:
            dve.wait_ge(self.used[s], n)
        dve.tensor_copy(self.hi[:, s, :, :], self.raw[:, s, :, :]).then_inc(self.halved[s], 1)

    def low(self, pool, s, n):
        pool.wait_ge(self.halved[s], n + 1)
        pool.tensor_tensor(self.lo[:, s, :, :], self.raw[:, s, :, :], self.hi[:, s, :, :].bitcast(F32), ALU.subtract)\
            .then_inc(self.split[s], 1)

    def passes(self, s, k):
        return ((self.hi[:, s, k, :], 0), (self.hi[:, s, k, :], 1), (self.lo[:, s, k, :], 0))


def split_product(pe, ring, s, out, parts):
    for k in range(KD):
        for i, (w, low) in enumerate(ring.passes(s, k)):
            mm = pe.matmul(out, w, parts[low][:, k, :], start=(k == 0 and i == 0), stop=(k == KD - 1 and i == 2))
    return mm


def gated_stage(nc, c, wa, wb, chunks, func, w_down=None, scale=None, raw=None, y=None, merged=None, accumulate=False):
    with Stage(nc) as st:
        ring = Ring(st, raw)
        sg = st.sb("sg", [P, 2, SEQ])
        af = st.sb("af", [P, 2, SEQ])
        if w_down is not None:
            a_hi, a_lo = st.sb("a_hi", [P, chunks, SEQ], F32R), st.sb("a_lo", [P, chunks, SEQ], F32R)
            second = (c.h_hi, c.h_lo)
        else:
            second = (st.sb("y_hi", [P, KD, SEQ], F32R), st.sb("y_lo", [P, KD, SEQ], F32R))
        opened = [st.sem(f"opened{p}") for p in range(2)]
        gated = [st.sem(f"gated{p}") for p in range(2)]
        y_split, a_split = st.sem("y_split"), st.sem("a_split")
        block = st.block()
        a_v = wa.rearrange("(k p) f -> p k f", p=P)
        b_v = wb.rearrange("(k p) f -> p k f", p=P)
        N = chunks // 2
        KD_DOWN = chunks // 2

        tiles = ((0, a_v), (1, b_v)) if w_down is not None else ((1, b_v), (0, a_v))

        @block.sync
        def _(sp):
            def load(i, p, first):
                for e, v in tiles:
                    ring.load(sp, 2 * p + e, i, first, v[:, :, bass.ds(i * (2 * P) + p * P, P)])

            load(0, 0, True)
            load(0, 1, True)
            with sp.Fori(1, N) as i:
                load(i, 0, False)
                load(i, 1, False)
            if w_down is not None:
                with sp.Fori(0, N) as i:
                    for s in range(2):
                        ring.load(sp, s, N + i, False,
                                  w_down[bass.ds(i * (2 * P) + s * P, P), :].rearrange("p (k n) -> p k n", n=P))

        @block.gpsimd
        def _(pool):
            with pool.Fori(0, N) as i:
                for s in range(4):
                    ring.low(pool, s, i)
            if w_down is not None:
                with pool.Fori(0, N) as i:
                    for s in range(2):
                        ring.low(pool, s, N + i)

        @block.tensor
        def _(pe):
            def products(i, p, first):
                pe.wait_ge(ring.split[2 * p], i + 1)
                if not first:
                    pe.wait_ge(gated[p], i)
                split_product(pe, ring, 2 * p, c.ps[:, p, :], (c.h_hi, c.h_lo)).then_inc(ring.used[2 * p], 1)
                pe.wait_ge(ring.split[2 * p + 1], i + 1)
                if y is not None and first and p == 0:
                    pe.wait_ge(y_split, 1)
                split_product(pe, ring, 2 * p + 1, c.ps[:, 2 + p, :], second).then_inc(ring.used[2 * p + 1], 1)

            products(0, 0, True)
            products(0, 1, True)
            with pe.Fori(1, N) as i:
                products(i, 0, False)
                products(i, 1, False)
            if w_down is not None:
                def down(i, s, first, last):
                    pe.wait_ge(ring.split[s], N + 1 + i)
                    for m in range(KD):
                        for n, (w, low) in enumerate(ring.passes(s, m)):
                            mm = pe.matmul(c.ps[:, m, :], w, (a_hi, a_lo)[low][:, bass.ds(2 * i + s, 1), :],
                                           start=(first and n == 0), stop=(last and n == 2))
                    mm.then_inc(ring.used[s], 1)

                pe.wait_ge(a_split, chunks)
                down(0, 0, True, False)
                down(0, 1, False, False)
                with pe.Fori(1, N - 1) as i:
                    down(i, 0, False, False)
                    down(i, 1, False, False)
                down(N - 1, 0, False, False)
                down(N - 1, 1, False, True)

        @block.scalar
        def _(act):
            def gate(i, p, first):
                act.wait_ge(ring.used[2 * p], i + 1)
                if not first:
                    act.wait_ge(gated[p], i)
                act.activation(sg[:, p, :], c.ps[:, p, :], func).then_inc(opened[p], 1)

            gate(0, 0, True)
            gate(0, 1, True)
            with act.Fori(1, N) as i:
                gate(i, 0, False)
                gate(i, 1, False)

        @block.vector
        def _(dve):
            def highs(i, p, first):
                ring.high(dve, 2 * p, i, first)
                ring.high(dve, 2 * p + 1, i, first)

            def finish(i, p):
                dve.wait_ge(opened[p], i + 1)
                dve.wait_ge(ring.used[2 * p + 1], i + 1)
                dve.tensor_tensor(af[:, p:p + 1, :], sg[:, p:p + 1, :], c.ps[:, 2 + p:3 + p, :], ALU.mult).then_inc(gated[p], 1)
                dve.drain()
                at = bass.ds(2 * i + p, 1)
                if w_down is not None:
                    dve.tensor_copy(a_hi[:, at, :], af[:, p:p + 1, :])
                    dve.drain()
                    dve.tensor_tensor(a_lo[:, at, :], af[:, p:p + 1, :], a_hi[:, at, :].bitcast(F32), ALU.subtract)\
                        .then_inc(a_split, 1)
                elif accumulate:
                    dve.tensor_tensor(merged[:, at, :], merged[:, at, :], af[:, p:p + 1, :], ALU.add)
                else:
                    dve.tensor_copy(merged[:, at, :], af[:, p:p + 1, :])
                dve.drain()

            highs(0, 0, True)
            if y is not None:
                dve.tensor_copy(second[0][:, :, :], y[:, :, :])
                dve.drain()
                dve.tensor_tensor(second[1][:, :, :], y[:, :, :], second[0][:, :, :].bitcast(F32), ALU.subtract)\
                    .then_inc(y_split, 1)
            highs(0, 1, True)
            finish(0, 0)
            with dve.Fori(1, N) as i:
                highs(i, 0, False)
                finish(i - 1, 1)
                highs(i, 1, False)
                finish(i, 0)
            if w_down is None:
                finish(N - 1, 1)
            else:
                for s in range(2):
                    ring.high(dve, s, N, False)
                finish(N - 1, 1)
                with dve.Fori(1, N) as i:
                    for s in range(2):
                        ring.high(dve, s, N + i, False)
                dve.wait_ge(ring.used[1], 2 * N)
                for m in range(KD):
                    if raw is None:
                        dve.scalar_tensor_tensor(out=c.x_T[:, m, :], in0=c.ps[:, m, :], scalar=scale, in1=c.x_T[:, m, :],
                                                 op0=ALU.mult, op1=ALU.add)
                    else:
                        dve.tensor_copy(feature_major(raw)[:, m, :], c.ps[:, m, :])


def feature_major(raw):
    return raw[:, :, :, :].rearrange("p s k n -> p (s k n)").rearrange("p (k t) -> p k t", t=SEQ)


def ffn(nc, c, w_gate, w_up, w_down, scale, raw=None):
    gated_stage(nc, c, w_gate, w_up, KF, ACT.Silu, w_down=w_down, scale=scale, raw=raw)


class Shared:

    def __init__(self, nc, ctx):
        def sb(name, shape, dtype=F32):
            return ctx.enter_context(nc.sbuf_tensor(name, shape, dtype))
        self.ps = ctx.enter_context(nc.psum_tensor("ps", [P, 8, BANK], F32))
        self.x_T = sb("x_T", [P, KD, SEQ])
        self.h_hi = sb("h_hi", [P, KD, SEQ], F32R)
        self.h_lo = sb("h_lo", [P, KD, SEQ], F32R)
        self.ident = sb("ident", [P, P])
        self.ones = sb("ones", [P, P])
        self.ones64 = sb("ones64", [P, P])
        self.ones32 = sb("ones32", [P, P])
        self.bound = sb("bound", [P, SEQ])
        self.winmask = sb("winmask", [P, P])
        self.sel = sb("sel", [8, 8, P])
        self.selp = sb("selp", [8, 4, P])
        self.chunkmask = sb("chunkmask", [P, P])
        self.scanone = sb("scanone", [P, SEQ])
        self.eps = sb("eps", [P, 1])
        self.one = sb("one", [P, 1])
        self.lam_init = sb("lam_init", [P, LAYERS])


def project(nc, c, w, runs, rows_to, tokens_to, params=()):
    with Stage(nc) as st:
        ring = Ring(st)
        kept = [st.sem(f"kept{s}") for s in range(4)]
        param_loaded = st.sem("param_loaded")
        block = st.block()
        view = w.rearrange("(k p) f -> p k f", p=P)
        singles = [("token", *t) for t in tokens_to for _ in range(2)] + [("row", *r) for r in rows_to]
        n_pairs = sum(chunks for _, chunks, _ in runs) // 2

        def each_tile(eng, body):
            base = 0
            for col0, chunks, dst in runs:
                n = chunks // 2

                def pair(j, p, idx, first):
                    for e in range(2):
                        body(2 * p + e, idx, first, "chunk", j * (2 * P) + (col0 + e * P), P, dst, 2 * j + e)

                if base % 2 == 0 and n % 2 == 0 and n >= 6:
                    start = 0
                    if base == 0:
                        pair(0, 0, 0, True)
                        pair(1, 1, 0, True)
                        start = 1
                    with eng.Fori(start, n // 2) as i:
                        pair(2 * i, 0, base // 2 + i, False)
                        pair(2 * i + 1, 1, base // 2 + i, False)
                else:
                    for j in range(n):
                        pair(j, (base + j) % 2, (base + j) // 2, base + j < 2)
                base += n
            for q, (kind, col0, m, dst) in enumerate(singles):
                n = base + q // 2
                body(2 * (n % 2) + q % 2, n // 2, n < 2, kind, col0 + (P if kind == "token" and q % 2 else 0), m, dst, 0)

        @block.sync
        def _(sp):
            each_tile(sp, lambda s, n, first, kind, col, m, dst, j:
                      ring.load(sp, s, n, first, view[:, :, bass.ds(col, P)]))
            with nc.allow_non_contiguous_dma(reason="columns of parameters"):
                for dst, src in params:
                    sp.dma_start(dst, src).then_inc(param_loaded, 16)
            if params:
                sp.wait_ge(param_loaded, 16 * len(params))

        @block.vector
        def _(dve):
            each_tile(dve, lambda s, n, first, kind, col, m, dst, j: ring.high(dve, s, n, first))

        @block.gpsimd
        def _(pool):
            each_tile(pool, lambda s, n, first, kind, col, m, dst, j: ring.low(pool, s, n))

        @block.tensor
        def _(pe):
            def product(s, n, first, kind, col, m, dst, j):
                pe.wait_ge(ring.split[s], n + 1)
                if not first:
                    pe.wait_ge(kept[s], n)
                parts = (c.h_hi, c.h_lo)
                if kind != "token":
                    split_product(pe, ring, s, c.ps[:, s, :], parts).then_inc(ring.used[s], 1)
                elif s % 2:
                    for t in range(TT):
                        for k in range(KD):
                            for i, (w, low) in enumerate(((ring.hi, 0), (ring.hi, 1), (ring.lo, 0))):
                                mm = pe.matmul(c.ps[:, s - 1 + t // 2, (t % 2) * 2 * P:(t % 2 + 1) * 2 * P],
                                               parts[low][:, k, t * P:(t + 1) * P], w[:, s - 1:s + 1, k, :],
                                               start=(k == 0 and i == 0), stop=(k == KD - 1 and i == 2))
                    mm.then_inc(ring.used[s - 1], 1)
                    pe.drain().then_inc(ring.used[s], 1)

            each_tile(pe, product)

        @block.scalar
        def _(act):
            def keep(s, n, first, kind, col, m, dst, j):
                act.wait_ge(ring.used[s], n + 1)
                if kind == "chunk":
                    ins = act.activation(dst[:, bass.ds(j, 1), :], c.ps[:, s:s + 1, :], ACT.Copy)
                elif kind == "row":
                    ins = act.activation(dst, c.ps[0:m, s, :], ACT.Copy)
                else:
                    e = s % 2
                    ins = act.activation(dst[:, 2 * e:2 * e + 2, :],
                                         c.ps[:, s, :].rearrange("p (t n) -> p t n", n=2 * P)[:, :, 0:m], ACT.Copy)
                ins.then_inc(kept[s], 1)

            each_tile(act, keep)


M_HEADS, M_DIM = 4, 64
S_HEADS, S_DIM = 8, 64
DF_HEADS, DF_QK, DF_V = 4, 32, 64


class Mixer:

    def __init__(self, nc, ctx, y_T):
        def sb(name, shape):
            return ctx.enter_context(nc.sbuf_tensor(f"{name}_{nc.next_id()}", shape, F32))
        self.y_T = y_T
        self.mqk = sb("mqk", [P, 4, SEQ])
        self.mo = sb("mo", [P, 2, SEQ])
        self.mv = sb("mv", [P, TT, 2 * P])
        self.gi = sb("gi", [M_HEADS, SEQ])
        self.gf = sb("gf", [M_HEADS, SEQ])
        self.zxbc = sb("zxbc", [P, 12, SEQ])
        self.z = self.zxbc[:, 0:4, :]
        self.xbc = self.zxbc[:, 4:12, :]
        self.dt = sb("dt", [S_HEADS, SEQ])
        self.dqk = sb("dqk", [P, 4, SEQ])
        self.dv = sb("dv", [P, TT, 2 * P])
        self.g_bias = sb("g_bias", [M_HEADS, 2])
        self.m_gain = sb("m_gain", [P, 2])
        self.conv_w = sb("conv_w", [P, 8, 4])
        self.conv_b = sb("conv_b", [P, 8])
        self.dt_bias = sb("dt_bias", [S_HEADS, 1])
        self.a_log = sb("a_log", [S_HEADS, 1])
        self.d_skip = sb("d_skip", [P, 4])
        self.s_gain = sb("s_gain", [P, 4])
        self.q_gain = sb("q_gain", [P, 1])
        self.k_gain = sb("k_gain", [P, 1])
        self.lam4 = sb("lam4", [P, 4, DF_QK])
        self.sub_gain = sb("sub_gain", [P, 1])


def per_partition(ap, offset_ap, pattern):
    return bass.AP(tensor=offset_ap.tensor, offset=offset_ap.offset, ap=pattern)


def gates(nc, c, m, rows, cols):
    acs, negM, negm = rows
    with Stage(nc) as st:
        x8, e8, l8, dA, nacs = (st.sb(n, [8, SEQ]) for n in ("x8", "e8", "l8", "dA", "nacs"))
        x4, e4, l4, B, g, M, s4 = (st.sb(n, [4, SEQ]) for n in ("x4", "e4", "l4", "B", "g", "M", "s4"))
        ones8 = st.sb("ones8", [8, SEQ])
        a8 = st.sb("a8", [8, 1])
        biased, logged, rowed, turned = st.sem("biased"), st.sem("logged"), st.sem("rowed"), st.sem("turned")
        block = st.block()

        @block.scalar
        def _(act):
            act.activation(a8[:, :], m.a_log[:, :], ACT.Exp)
            act.wait_ge(biased, 1)
            act.activation(e8[:, :], x8[:, :], ACT.Abs)
            act.activation(e4[:, :], x4[:, :], ACT.Abs)
            act.drain()
            act.activation(e8[:, :], e8[:, :], ACT.Exp, scale=-1.0)
            act.activation(e4[:, :], e4[:, :], ACT.Exp, scale=-1.0)
            act.drain()
            act.activation(l8[:, :], e8[:, :], ACT.Ln, bias=c.one[0:8, :])
            act.activation(l4[:, :], e4[:, :], ACT.Ln, bias=c.one[0:4, :])
            act.drain().then_inc(logged, 1)

        @block.vector
        def _(dve):
            dve.memset(ones8[:, :], 1.0)
            dve.tensor_scalar(x8[:, :], m.dt[:, :], m.dt_bias[:, :], None, ALU.add)
            dve.tensor_scalar(x4[:, :], m.gf[:, :], m.g_bias[:, 1:2], None, ALU.add)
            dve.drain().then_inc(biased, 1)
            dve.wait_ge(logged, 1)
            dve.scalar_tensor_tensor(out=m.dt[:, :], in0=x8[:, :], scalar=0.0, in1=l8[:, :], op0=ALU.max, op1=ALU.add)
            dve.scalar_tensor_tensor(out=s4[:, :], in0=x4[:, :], scalar=0.0, in1=l4[:, :], op0=ALU.min, op1=ALU.subtract)
            dve.drain()
            dve.tensor_scalar(dA[:, :], m.dt[:, :], a8[:, 0:1], -1.0, ALU.mult, ALU.mult)
            dve.tensor_tensor_scan(B[:, :], ones8[0:4, :], s4[:, :], 0.0, ALU.mult, ALU.add)
            dve.drain()
            dve.tensor_tensor_scan(acs[:, :], ones8[:, :], dA[:, :], 0.0, ALU.mult, ALU.add)
            dve.scalar_tensor_tensor(out=g[:, :], in0=m.gi[:, :], scalar=m.g_bias[:, 0:1], in1=B[:, :],
                                     op0=ALU.add, op1=ALU.subtract)
            dve.drain()
            dve.tensor_scalar(nacs[:, :], acs[:, :], -1.0, None, ALU.mult)
            dve.tensor_tensor_scan(M[:, :], g[:, :], g[:, :], 0.0, ALU.max, ALU.max)
            dve.drain()
            dve.tensor_scalar(negM[:, :], M[:, :], -1.0, None, ALU.mult)
            dve.scalar_tensor_tensor(out=negm[:, :], in0=M[:, :], scalar=-1.0, in1=B[:, :], op0=ALU.mult, op1=ALU.subtract)
            dve.drain().then_inc(rowed, 1)
            dve.wait_ge(turned, 1)
            dve.tensor_copy(cols[:, :, :], c.ps[:, 0, 0:TT * 32].rearrange("p (t n) -> p t n", n=32)[:, :, 0:20])

        @block.tensor
        def _(pe):
            pe.wait_ge(rowed, 1)
            for t in range(TT):
                at = t * P
                for off, src, n in ((0, g, 4), (4, nacs, 8), (12, m.dt, 8)):
                    mm = pe.transpose(c.ps[:, 0, 32 * t + off:32 * t + off + n], src[:, at:at + P], c.ident[0:n, 0:n])
            mm.then_inc(turned, 1)


def conv(nc, c, m, xdt, cols):
    with Stage(nc) as st:
        y = st.sb("y", [P, 8, SEQ])
        convolved, silued, turned = st.sem("convolved"), st.sem("silued"), st.sem("turned")
        block = st.block()

        @block.vector
        def _(dve):
            for k in range(8):
                dve.tensor_scalar(y[:, k, :], m.xbc[:, k, :], m.conv_w[:, k, 3:4], None, ALU.mult)
            for s in range(1, 4):
                dve.drain()
                for k in range(8):
                    ins = dve.scalar_tensor_tensor(out=y[:, k, s:], in0=m.xbc[:, k, 0:SEQ - s],
                                                   scalar=m.conv_w[:, k, 3 - s:4 - s], in1=y[:, k, s:],
                                                   op0=ALU.mult, op1=ALU.add)
                    if s == 3:
                        ins.then_inc(convolved, 1)
            for t in range(TT):
                dve.wait_ge(turned, t + 1)
                dve.tensor_tensor(xdt[:, t, :].rearrange("p (h d) -> p h d", d=S_DIM),
                                  c.ps[:, t, :].rearrange("p (h d) -> p h d", d=S_DIM),
                                  cols[:, t, 12:20].rearrange("p (h o) -> p h o", o=1).to_broadcast([P, S_HEADS, S_DIM]),
                                  ALU.mult)

        @block.scalar
        def _(act):
            for k in range(8):
                act.wait_ge(convolved, k + 1)
                if k == 0:
                    act.wait_ge(convolved, 8)
                act.activation(m.xbc[:, k, :], y[:, k, :], ACT.Silu, bias=m.conv_b[:, k:k + 1]).then_inc(silued, 1)

        @block.tensor
        def _(pe):
            pe.wait_ge(silued, 4)
            for t in range(TT):
                for k in range(4):
                    mm = pe.transpose(c.ps[:, t, k * P:(k + 1) * P], m.xbc[:, k, t * P:(t + 1) * P], c.ident[:, :])
                mm.then_inc(turned, 1)


def recurrences(nc, c, m, rows, cols, xdt, y_ssm, num, den):
    acs, negM, negm = rows
    units = [("ssm", h) for h in range(S_HEADS)] + [("mlstm", h) for h in range(M_HEADS)]
    score_of, scores = [], []
    for kind, h in units:
        key = (kind, h // 4 if kind == "ssm" else h)
        if key not in scores:
            scores.append(key)
        score_of.append(scores.index(key))
    last_use = {n: max(u for u, k in enumerate(score_of) if k == n) for n in range(len(scores))}
    with Stage(nc) as st:
        arg = st.sb("arg", [P, 2, TRI])
        wgt = st.sb("wgt", [P, 2, TRI])
        vone = st.sb("vone", [P, TT, M_HEADS, P])
        v_ready, row_sent, arged, exped = (st.sem(n) for n in ("v_ready", "row_sent", "arged", "exped"))
        scored, weighted, outed, kept = (st.sem(n) for n in ("scored", "weighted", "outed", "kept"))
        block = st.block()
        ROW, OUT = 6, 7

        def tri(buf, j):
            return c.ps[:, 3 * buf + TRI_AT[j] // BANK, TRI_AT[j] % BANK:TRI_AT[j] % BANK + TRI_W[j]]

        @block.tensor
        def _(pe):
            def row(u):
                kind, h = units[u]
                if u >= 1:
                    pe.wait_ge(arged, u)
                n, src = (8, acs) if kind == "ssm" else (4, negM)
                pe.matmul(c.ps[:, ROW, :], c.sel[0:n, h, :], src[:, :], start=True, stop=True).then_inc(row_sent, 1)
                k = score_of[u]
                if u and score_of[u - 1] == k:
                    return
                if k >= 2:
                    pe.wait_ge(weighted, last_use[k - 2] + 1)
                for j in range(TT):
                    if kind == "ssm":
                        key, query = m.xbc[:, 4 + h // 4, j * P:(j + 1) * P], m.xbc[:, 6 + h // 4, j * P:]
                    else:
                        b = 64 * (h % 2)
                        key, query = m.mqk[b:b + 64, 2 + h // 2, j * P:(j + 1) * P], m.mqk[b:b + 64, h // 2, j * P:]
                    mm = pe.matmul(tri(k % 2, j), key, query, start=True, stop=True)
                mm.then_inc(scored, 1)

            def out(u):
                kind, h = units[u]
                pe.wait_ge(weighted, u + 1)
                if u >= 1:
                    pe.wait_ge(kept, u)
                if u == 8:
                    pe.wait_ge(v_ready, 1)
                b = 64 * (h % 2)
                for j in range(TT):
                    if kind == "ssm":
                        v, to = xdt[:, j, h * 64:(h + 1) * 64], c.ps[b:b + 64, OUT, j * P:]
                    else:
                        v, to = vone[:, j, h, :], c.ps[:, OUT, j * P:]
                    mm = pe.matmul(to, v, wgt[:, u % 2, TRI_AT[j]:TRI_AT[j] + TRI_W[j]], start=(j == 0), stop=(j == TT - 1))
                mm.then_inc(outed, 1)

            row(0)
            for u in range(len(units)):
                if u + 1 < len(units):
                    row(u + 1)
                out(u)

        @block.vector
        def _(dve):
            dve.memset(vone[:, :, :, 64:P], 1.0)
            dve.tensor_copy(vone[:, :, :, 0:64], m.mv[:, :, :].rearrange("p t (h d) -> p t h d", d=64)).then_inc(v_ready, 1)

            def args(u):
                kind, h = units[u]
                dve.wait_ge(row_sent, u + 1)
                for j in range(TT):
                    col = cols[:, j, 4 + h:5 + h] if kind == "ssm" else cols[:, j, h:h + 1]
                    ins = dve.scalar_tensor_tensor(out=arg[:, u % 2, TRI_AT[j]:TRI_AT[j] + TRI_W[j]],
                                                   in0=c.ps[:, ROW, j * P:], scalar=col, in1=c.bound[:, 0:TRI_W[j]],
                                                   op0=ALU.add, op1=ALU.min)
                ins.then_inc(arged, 1)

            def weigh(u):
                kind, h = units[u]
                dve.wait_ge(exped, u + 1)
                dve.wait_ge(scored, score_of[u] + 1)
                if u >= 2:
                    dve.wait_ge(outed, u - 1)
                k = score_of[u] % 2
                dve.scalar_tensor_tensor(
                    out=wgt[:, u % 2, :], in0=c.ps[:, 3 * k:3 * k + 3, :].rearrange("p b n -> p (b n)")[:, 0:TRI],
                    scalar=(1.0 if kind == "ssm" else M_DIM ** -0.5), in1=arg[:, u % 2, :],
                    op0=ALU.mult, op1=ALU.mult).then_inc(weighted, 1)

            args(0)
            for u in range(len(units)):
                if u + 1 < len(units):
                    args(u + 1)
                weigh(u)

        @block.scalar
        def _(act):
            def exps(u):
                act.wait_ge(arged, u + 1)
                act.activation(arg[:, u % 2, :], arg[:, u % 2, :], ACT.Exp).then_inc(exped, 1)

            exps(0)
            for u, (kind, h) in enumerate(units):
                if u + 1 < len(units):
                    exps(u + 1)
                act.wait_ge(outed, u + 1)
                b = 64 * (h % 2)
                if kind == "ssm":
                    act.activation(y_ssm[b:b + 64, h // 2, :], c.ps[b:b + 64, OUT, :], ACT.Copy).then_inc(kept, 1)
                else:
                    act.activation(num[b:b + 64, h // 2, :], c.ps[0:64, OUT, :], ACT.Copy)
                    act.activation(den[b:b + 64, h // 2, :], c.ps[64:P, OUT, :], ACT.Copy).then_inc(kept, 1)


def finish_recurrences(nc, c, m, rows, y_ssm, num, den):
    acs, negM, negm = rows
    with Stage(nc) as st:
        floor = st.sb("floor", [P, 2, SEQ])
        sq = st.sb("sq", [P, 6, SEQ])
        rstd = st.sb("rstd", [P, 4, SEQ])
        row_sent, exped, y_ready, squared, summed, rooted, sigmoided, zed = (
            st.sem(n) for n in ("row_sent", "exped", "y_ready", "squared", "summed", "rooted", "sigmoided", "zed"))
        block = st.block()

        @block.tensor
        def _(pe):
            for p in range(2):
                mm = pe.matmul(c.ps[:, p, :], c.selp[0:4, p, :], negm[:, :], start=True, stop=True)
            mm.then_inc(row_sent, 1)
            pe.wait_ge(squared, 1)
            for g in range(2):
                for k in range(2):
                    pe.matmul(c.ps[:, 2 + g, :], c.ones[:, :], sq[:, 2 * g + k, :], start=(k == 0), stop=(k == 1))
            for p in range(2):
                mm = pe.matmul(c.ps[:, 4 + p, :], c.ones64[:, :], sq[:, 4 + p, :], start=True, stop=True)
            mm.then_inc(summed, 1)

        @block.scalar
        def _(act):
            act.activation(m.z[:, :, :], m.z[:, :, :], ACT.Silu).then_inc(zed, 1)
            act.activation(m.mo[:, :, :], m.mo[:, :, :], ACT.Sigmoid).then_inc(sigmoided, 1)
            act.activation(den[:, :, :], den[:, :, :], ACT.Abs)
            act.wait_ge(row_sent, 1)
            act.activation(floor[:, :, :], c.ps[:, 0:2, :], ACT.Exp)
            act.drain().then_inc(exped, 1)
            act.wait_ge(y_ready, 1)
            act.activation(sq[:, 0:4, :], y_ssm[:, :, :], ACT.Square)
            act.activation(sq[:, 4:6, :], num[:, :, :], ACT.Square)
            act.drain().then_inc(squared, 1)
            act.wait_ge(summed, 1)
            act.activation(rstd[:, 0:2, :], c.ps[:, 2:4, :], ACT.Sqrt, scale=1.0 / 256, bias=c.eps[:, :])
            act.activation(rstd[:, 2:4, :], c.ps[:, 4:6, :], ACT.Sqrt, scale=1.0 / 64, bias=c.eps[:, :])
            act.drain().then_inc(rooted, 1)

        @block.vector
        def _(dve):
            for k in range(4):
                dve.scalar_tensor_tensor(out=y_ssm[:, k, :], in0=m.xbc[:, k, :], scalar=m.d_skip[:, k:k + 1],
                                         in1=y_ssm[:, k, :], op0=ALU.mult, op1=ALU.add)
            dve.drain()
            dve.wait_ge(zed, 1)
            dve.tensor_tensor(y_ssm[:, :, :], y_ssm[:, :, :], m.z[:, :, :], ALU.mult)
            dve.wait_ge(exped, 1)
            dve.tensor_tensor(den[:, :, :], den[:, :, :], floor[:, :, :], ALU.max)
            dve.drain()
            dve.reciprocal(den[:, :, :], den[:, :, :])
            dve.drain()
            dve.tensor_tensor(num[:, :, :], num[:, :, :], den[:, :, :], ALU.mult)
            dve.drain().then_inc(y_ready, 1)
            dve.wait_ge(sigmoided, 1)
            dve.wait_ge(rooted, 1)
            dve.reciprocal(rstd[:, :, :], rstd[:, :, :])
            dve.drain()
            for p in range(2):
                dve.scalar_tensor_tensor(out=num[:, p, :], in0=num[:, p, :], scalar=m.m_gain[:, p:p + 1],
                                         in1=rstd[:, 2 + p, :], op0=ALU.mult, op1=ALU.mult)
            for k in range(4):
                dve.scalar_tensor_tensor(out=m.y_T[:, 2 + k, :], in0=y_ssm[:, k, :], scalar=m.s_gain[:, k:k + 1],
                                         in1=rstd[:, k // 2, :], op0=ALU.mult, op1=ALU.mult)
            dve.drain()
            dve.tensor_tensor(m.y_T[:, 0:2, :], num[:, :, :], m.mo[:, :, :], ALU.mult)


def bias_rows(nc, c, table, heads, scratch):
    edges = bucket_edges()
    with Stage(nc) as st:
        tab = st.sb("tab", [heads, 32])
        f = st.sb("f", [heads, BACK + SEQ])
        loaded, laid, written = st.sem("loaded"), st.sem("laid"), st.sem("written")
        block = st.block()

        @block.sync
        def _(sp):
            with nc.allow_non_contiguous_dma(reason="a small table, turned"):
                sp.dma_start(tab[:, :], table.rearrange("b h -> h b")).then_inc(loaded, 16)
            sp.wait_ge(laid, 1)
            sp.dma_start(scratch[:, :], f[:, :]).then_inc(written, 16)
            sp.wait_ge(written, 16)

        @block.vector
        def _(dve):
            dve.memset(f[:, 0:BACK], MASKED)
            dve.wait_ge(loaded, 16)
            dve.tensor_copy(f[:, BACK:BACK + 16], tab[:, 0:16])
            for b in range(16, 32):
                lo, hi = edges[b], edges[b + 1]
                if lo < hi:
                    dve.tensor_copy(f[:, BACK + lo:BACK + hi], tab[:, b:b + 1].to_broadcast([heads, hi - lo]))
            dve.drain().then_inc(laid, 1)


def bucket_edges():
    n = np.arange(SEQ)
    nf = np.maximum(n, 16).astype(np.float32)
    large = 16 + (np.log(nf / np.float32(16)) / np.float32(np.log(8.0)) * np.float32(16)).astype(np.int32)
    bucket = np.where(n < 16, n, np.minimum(large, 31))
    return {b: int(np.argmax(bucket >= b)) for b in range(16, 32)} | {32: SEQ}


BACK = P


def bias_tiles(nc, c, scratch, heads, tiles, times):
    with Stage(nc) as st:
        turned = st.sb("turned", [P, 2, SEQ])
        loaded, used = [st.sem(f"loaded{s}") for s in range(2)], st.sem("used")
        block = st.block()

        @block.sync
        def _(sp):
            for h in range(heads):
                if h >= 2:
                    sp.wait_ge(used, h - 1)
                src = scratch[h, BACK - 127:BACK - 127 + SEQ]
                sp.dma_start(turned[:, h % 2, :], bass.AP(tensor=src.tensor, offset=src.offset, ap=[[1, P], [1, SEQ]]))\
                    .then_inc(loaded[h % 2], 16)

        @block.vector
        def _(dve):
            for h in range(heads):
                dve.wait_ge(loaded[h % 2], 16 * (h // 2) + 16)
                dve.tensor_scalar(tiles[:, h, :], turned[:, h % 2, ::-1], times, None, ALU.mult).then_inc(used, 1)


def first_mixer_projections(nc, c, m, L, w):
    FM = [(1032, 12, m.zxbc[:, :, :]), (0, 4, m.mqk[:, :, :]), (2576, 4, m.dqk[:, :, :]), (768, 2, m.mo[:, :, :])]
    rows = [(1024, 4, m.gi[:, :]), (1028, 4, m.gf[:, :]), (2568, 8, m.dt[:, :])]
    tokens = [(512, 2 * P, m.mv[:, :, :]), (3088, 2 * P, m.dv[:, :, :])]

    def col(ap):
        return ap.rearrange("(p o) -> p o", o=1)

    params = [
        (m.g_bias[:, :], L["mlstm_gate_bias"].rearrange("g h -> h g")),
        (m.m_gain[:, :], L["mlstm_norm_w"].rearrange("(k p) -> p k", p=P)),
        (m.conv_b[:, :], L["ssm_conv_b"].rearrange("(k p) -> p k", p=P)),
        (m.dt_bias[:, :], col(L["ssm_dt_bias"])),
        (m.a_log[:, :], col(L["ssm_A_log"])),
        (m.s_gain[:, :], L["ssm_norm_w"].rearrange("(k p) -> p k", p=P)),
        (m.sub_gain[0:64, :], col(L["diff_subln_w"])),
        (m.sub_gain[64:P, :], col(L["diff_subln_w"])),
        (m.lam4[:, :, :], L["diff_lambda"].rearrange("(o a) d -> o a d", o=1).to_broadcast([P, 4, DF_QK])),
    ]
    for k in range(8):
        params.append((m.conv_w[:, k, :], L["ssm_conv_w"][:, k * P:(k + 1) * P].rearrange("t p -> p t")))
    for half in range(2):
        b = 64 * half
        for name, dst in (("diff_q_norm_w", m.q_gain), ("diff_k_norm_w", m.k_gain)):
            params.append((dst[b:b + 64, :], L[name].rearrange("i (d o) -> (i d) o", o=1)))
        src = L["ssm_D"].rearrange("(k e o) -> e o k", e=2, o=1)
        params.append((m.d_skip[b:b + 64, :], src[half].to_broadcast([64, 4])))
    project(nc, c, w, FM, rows, tokens, params)


def diff_prepare(nc, c, m, lam, lam_init):
    with Stage(nc) as st:
        sq = st.sb("sq", [P, 4, SEQ])
        rstd = st.sb("rstd", [P, 4, SEQ])
        prod = st.sb("prod", [P, 2, DF_QK])
        dots = st.sb("dots", [P, 2])
        squared, summed, rooted, dotted, exped = (st.sem(n) for n in ("squared", "summed", "rooted", "dotted", "exped"))
        block = st.block()

        @block.scalar
        def _(act):
            act.activation(sq[:, :, :], m.dqk[:, :, :], ACT.Square).then_inc(squared, 1)
            act.wait_ge(dotted, 1)
            act.activation(dots[:, :], dots[:, :], ACT.Exp).then_inc(exped, 1)
            act.wait_ge(summed, 1)
            act.activation(rstd[:, :, :], c.ps[:, 0:4, :], ACT.Sqrt, scale=1.0 / DF_QK, bias=c.eps[:, :]).then_inc(rooted, 1)

        @block.tensor
        def _(pe):
            pe.wait_ge(squared, 1)
            for k in range(4):
                mm = pe.matmul(c.ps[:, k, :], c.ones32[:, :], sq[:, k, :], start=True, stop=True)
            mm.then_inc(summed, 1)

        @block.vector
        def _(dve):
            dve.tensor_tensor(prod[:, :, :], m.lam4[:, 0:4:2, :], m.lam4[:, 1:4:2, :], ALU.mult)
            dve.drain()
            dve.reduce_sum(dots[:, :], prod[:, :, :], AX).then_inc(dotted, 1)
            dve.wait_ge(exped, 1)
            dve.scalar_tensor_tensor(out=lam[:, 0:1], in0=dots[:, 1:2], scalar=dots[:, 0:1], in1=lam_init,
                                     op0=ALU.subtract, op1=ALU.subtract)
            dve.tensor_scalar(lam[:, 1:2], lam_init, -1.0, 1.0, ALU.mult, ALU.add)
            dve.drain()
            dve.tensor_tensor(lam[:, 1:2], lam[:, 1:2], m.sub_gain[:, :], ALU.mult)
            dve.tensor_scalar(m.q_gain[:, :], m.q_gain[:, :], DF_QK ** -0.5, None, ALU.mult)
            dve.wait_ge(rooted, 1)
            dve.reciprocal(rstd[:, :, :], rstd[:, :, :])
            dve.drain()
            for k in range(4):
                gain = m.q_gain if k < 2 else m.k_gain
                dve.scalar_tensor_tensor(out=m.dqk[:, k, :], in0=m.dqk[:, k, :], scalar=gain[:, 0:1], in1=rstd[:, k, :],
                                         op0=ALU.mult, op1=ALU.mult)


def diff_attention(nc, c, m, tiles, lam, o_T):
    units = [(h, qi) for h in range(DF_HEADS) for qi in range(TT)]
    U = len(units)
    with Stage(nc) as st:
        neg = st.sb("neg", [P, 3, 2, SEQ])
        prob = st.sb("prob", [P, 2, SEQ])
        prob_T = st.sb("prob_T", [P, 2, TT, SEQ])
        nmax = st.sb("nmax", [P, 3, 2])
        total = st.sb("total", [P, 3, 2])
        recip = st.sb("recip", [P, 3, 2])
        scored, biased, exped, mixed, turned, laid, outed, kept = (
            st.sem(n) for n in ("scored", "biased", "exped", "mixed", "turned", "laid", "outed", "kept"))
        block = st.block()
        TURN, OUT = 4, 7

        @block.tensor
        def _(pe):
            def score(u):
                h, qi = units[u]
                if u >= 2:
                    pe.wait_ge(biased, u - 1)
                w = P * (qi + 1)
                for i in range(2):
                    b = 64 * (h % 2) + 32 * i
                    mm = pe.matmul(c.ps[:, 2 * (u % 2) + i, 0:w], m.dqk[b:b + 32, h // 2, qi * P:(qi + 1) * P],
                                   m.dqk[b:b + 32, 2 + h // 2, 0:w], start=True, stop=True)
                mm.then_inc(scored, 1)

            def turn(u):
                h, qi = units[u]
                pe.wait_ge(mixed, u + 1)
                if u >= 3:
                    pe.wait_ge(laid, u - 2)
                for j in range(qi + 1):
                    mm = pe.transpose(c.ps[:, TURN + u % 3, j * P:(j + 1) * P], prob[:, u % 2, j * P:(j + 1) * P], c.ident[:, :])
                mm.then_inc(turned, 1)

            def out(h):
                pe.wait_ge(laid, TT * (h + 1))
                if h >= 1:
                    pe.wait_ge(kept, h)
                b = 64 * (h % 2)
                for j in range(TT):
                    mm = pe.matmul(c.ps[b:b + 64, OUT, j * P:], m.dv[:, j, h * 64:(h + 1) * 64], prob_T[:, h % 2, j, j * P:],
                                   start=(j == 0), stop=(j == TT - 1))
                mm.then_inc(outed, 1)

            score(0)
            score(1)
            for u, (h, qi) in enumerate(units):
                if u + 2 < U:
                    score(u + 2)
                turn(u)
                if qi == 1 and h >= 1:
                    out(h - 1)
            out(DF_HEADS - 1)

        @block.vector
        def _(dve):
            def bias(u):
                h, qi = units[u]
                w = P * (qi + 1)
                dve.wait_ge(scored, u + 1)
                for i in range(2):
                    ins = dve.tensor_tensor_reduce(neg[:, u % 3, i, 0:w], c.ps[:, 2 * (u % 2) + i, 0:w], tiles[:, h, SEQ - w:SEQ],
                                                   -1.0, 3e38, ALU.add, ALU.min, nmax[:, u % 3, i:i + 1])
                ins.then_inc(biased, 1)

            def mix(u):
                h, qi = units[u]
                w = P * (qi + 1)
                s = u % 3
                dve.wait_ge(exped, u + 1)
                if u >= 2:
                    dve.wait_ge(turned, u - 1)
                dve.reciprocal(recip[:, s, :], total[:, s, :])
                dve.drain()
                dve.tensor_scalar(prob[:, u % 2, 0:w], neg[:, s, 1, 0:w], recip[:, s, 1:2], lam[:, 0:1], ALU.mult, ALU.mult)
                dve.drain()
                dve.scalar_tensor_tensor(out=prob[:, u % 2, 0:w], in0=neg[:, s, 0, 0:w], scalar=recip[:, s, 0:1],
                                         in1=prob[:, u % 2, 0:w], op0=ALU.mult, op1=ALU.add).then_inc(mixed, 1)
                dve.drain()

            bias(0)
            bias(1)
            for u in range(U):
                if u + 2 < U:
                    bias(u + 2)
                mix(u)

        @block.scalar
        def _(act):
            def exps(u):
                h, qi = units[u]
                w = P * (qi + 1)
                act.wait_ge(biased, u + 1)
                for i in range(2):
                    ins = act.activation(neg[:, u % 3, i, 0:w], neg[:, u % 3, i, 0:w], ACT.Exp, scale=-1.0,
                                         bias=nmax[:, u % 3, i:i + 1], accum_out=total[:, u % 3, i:i + 1])
                ins.then_inc(exped, 1)

            def lay(u):
                h, qi = units[u]
                act.wait_ge(turned, u + 1)
                if h >= 2:
                    act.wait_ge(outed, h - 1)
                act.activation(prob_T[:, h % 2, 0:qi + 1, qi * P:(qi + 1) * P],
                               c.ps[:, TURN + u % 3, 0:P * (qi + 1)].rearrange("p (j q) -> p j q", q=P), ACT.Copy)\
                    .then_inc(laid, 1)

            def keep(h):
                act.wait_ge(outed, h + 1)
                b = 64 * (h % 2)
                act.activation(o_T[b:b + 64, h // 2, :], c.ps[b:b + 64, OUT, :], ACT.Copy).then_inc(kept, 1)

            exps(0)
            for u in range(U):
                if u + 1 < U:
                    exps(u + 1)
                if u >= 1:
                    lay(u - 1)
                if units[u][1] == 3 and u >= TT:
                    keep(units[u][0] - 1)
            lay(U - 1)
            keep(DF_HEADS - 1)


def diff_finish(nc, c, m, lam, o_T):
    with Stage(nc) as st:
        sq = st.sb("sq", [P, 2, SEQ])
        rstd = st.sb("rstd", [P, 2, SEQ])
        squared, summed, rooted = (st.sem(n) for n in ("squared", "summed", "rooted"))
        block = st.block()

        @block.scalar
        def _(act):
            act.activation(sq[:, :, :], o_T[:, :, :], ACT.Square).then_inc(squared, 1)
            act.wait_ge(summed, 1)
            act.activation(rstd[:, :, :], c.ps[:, 0:2, :], ACT.Sqrt, scale=1.0 / DF_V, bias=c.eps[:, :]).then_inc(rooted, 1)

        @block.tensor
        def _(pe):
            pe.wait_ge(squared, 1)
            for k in range(2):
                mm = pe.matmul(c.ps[:, k, :], c.ones64[:, :], sq[:, k, :], start=True, stop=True)
            mm.then_inc(summed, 1)

        @block.vector
        def _(dve):
            dve.wait_ge(rooted, 1)
            dve.reciprocal(rstd[:, :, :], rstd[:, :, :])
            dve.drain()
            for k in range(2):
                dve.scalar_tensor_tensor(out=m.y_T[:, 6 + k, :], in0=o_T[:, k, :], scalar=lam[:, 1:2], in1=rstd[:, k, :],
                                         op0=ALU.mult, op1=ALU.mult)


def project_out(nc, c, w, src, dst, add):
    with Stage(nc) as st:
        ring = Ring(st)
        s_hi, s_lo = st.sb("s_hi", [P, KD, SEQ], F32R), st.sb("s_lo", [P, KD, SEQ], F32R)
        src_halved, src_split = st.sem("src_halved"), st.sem("src_split")
        block = st.block()

        @block.sync
        def _(sp):
            for k in range(KD):
                ring.load(sp, k % 4, k // 4, k < 4, w[k * P:(k + 1) * P, :].rearrange("p (m n) -> p m n", n=P))

        @block.gpsimd
        def _(pool):
            for k in range(KD):
                ring.low(pool, k % 4, k // 4)

        @block.scalar
        def _(act):
            for k in range(KD):
                act.activation(s_hi[:, k, :], src[:, k, :], ACT.Copy).then_inc(src_halved, 1)

        @block.tensor
        def _(pe):
            for k in range(KD):
                pe.wait_ge(ring.split[k % 4], k // 4 + 1)
                pe.wait_ge(src_split, k + 1)
                for m in range(KD):
                    for i, (wt, low) in enumerate(ring.passes(k % 4, m)):
                        mm = pe.matmul(c.ps[:, m, :], wt, (s_hi, s_lo)[low][:, k, :], start=(k == 0 and i == 0),
                                       stop=(k == KD - 1 and i == 2))
                mm.then_inc(ring.used[k % 4], 1)

        @block.vector
        def _(dve):
            for k in range(KD):
                dve.wait_ge(src_halved, k + 1)
                dve.tensor_tensor(s_lo[:, k, :], src[:, k, :], s_hi[:, k, :].bitcast(F32), ALU.subtract).then_inc(src_split, 1)
                ring.high(dve, k % 4, k // 4, k < 4)
            dve.wait_ge(ring.used[3], KD // 4)
            for m in range(KD):
                if add:
                    dve.tensor_tensor(dst[:, m, :], dst[:, m, :], c.ps[:, m, :], ALU.add)
                else:
                    dve.tensor_copy(dst[:, m, :], c.ps[:, m, :])


def first_mixer(nc, c, L, w_in, w_out, scratch, lam_init):
    with nc.sbuf_tensor(f"y_T_{nc.next_id()}", [P, KD, SEQ], F32) as y_T:
        with ExitStack() as ctx:
            def sb(name, shape):
                return ctx.enter_context(nc.sbuf_tensor(f"{name}_{nc.next_id()}", shape, F32))
            m = Mixer(nc, ctx, y_T)
            first_mixer_projections(nc, c, m, L, w_in)
            lam = sb("lam", [P, 2])
            with ExitStack() as inner:
                def isb(name, shape):
                    return inner.enter_context(nc.sbuf_tensor(f"{name}_{nc.next_id()}", shape, F32))
                rows = isb("acs", [8, SEQ]), isb("negM", [4, SEQ]), isb("negm", [4, SEQ])
                cols = isb("cols", [P, TT, 20])
                xdt = isb("xdt", [P, TT, SEQ])
                y_ssm, num, den = isb("y_ssm", [P, 4, SEQ]), isb("num", [P, 2, SEQ]), isb("den", [P, 2, SEQ])
                gates(nc, c, m, rows, cols)
                conv(nc, c, m, xdt, cols)
                recurrences(nc, c, m, rows, cols, xdt, y_ssm, num, den)
                finish_recurrences(nc, c, m, rows, y_ssm, num, den)
            o_T = sb("o_T", [P, 2, SEQ])
            tiles = sb("diff_tiles", [P, DF_HEADS, SEQ])
            bias_tiles(nc, c, scratch, DF_HEADS, tiles, 1.0)
            diff_prepare(nc, c, m, lam, lam_init)
            diff_attention(nc, c, m, tiles, lam, o_T)
            diff_finish(nc, c, m, lam, o_T)
        project_out(nc, c, w_out, y_T, c.x_T, True)


LRU_X, LRU_G, NSA_Q, NSA_KV, NSA_GATE = 0, 1024, 2048, 3072, 4608
GLA_Q, GLA_K, GLA_V, GLA_OG, GLA_LR, MERGE = 4656, 5168, 5680, 6704, 7728, 7744
N_HEADS, N_KV, N_DIM = 16, 4, 64
GROUP = N_HEADS // N_KV
TAPS, STRIDE, HIDDEN = 32, 16, 256
N_CMP = SEQ // STRIDE - 1
G_HEADS, G_DV, G_CHUNK = 4, 256, 32
G_CHUNKS = SEQ // G_CHUNK
LRU_C = 8.0


def lru_params(nc, ctx, W):
    def sb(name, shape):
        return ctx.enter_context(nc.sbuf_tensor(f"{name}_{nc.next_id()}", shape, F32))
    q = {"conv_w": sb("conv_w", [P, 8, 4]), "conv_b": sb("conv_b", [P, 8]), "b_gates": sb("b_gates", [P, 2, 8]),
         "lam": sb("lru_lam", [P, 8])}
    loads = [(q["conv_b"][:, :], W["conv_b"].rearrange("(k p) -> p k", p=P)),
             (q["lam"][:, :], W["lru_lambda"].rearrange("(k p) -> p k", p=P))]
    for g in range(2):
        loads.append((q["b_gates"][:, g, :], W["lru_b_gates"][g].rearrange("(k p) -> p k", p=P)))
    for k in range(8):
        loads.append((q["conv_w"][:, k, :], W["conv_w"][:, k * P:(k + 1) * P].rearrange("t p -> p t")))
    return q, loads


def lru_mixer(nc, c, q, w_gates, xa, ga, y):
    with Stage(nc) as st:
        wg = st.sb("wg", [P, 2, 8, P])
        xc = st.sb("xc", [P, 8, SEQ])
        r = st.sb("r", [P, 8, SEQ])
        i = st.sb("i", [P, 8, SEQ])
        z, w, w2, s = (st.sb(n, [P, 8]) for n in ("z", "w", "w2", "s"))
        w_loaded, convolved, gated, free, opened = (st.sem(n) for n in ("w_loaded", "convolved", "gated", "free", "opened"))
        mixed = st.sem("mixed")
        z_ready, coef, tanhed, u_ready, rooted, scanned, gelued = (
            st.sem(n) for n in ("z_ready", "coef", "tanhed", "u_ready", "rooted", "scanned", "gelued"))
        block = st.block()

        @block.sync
        def _(sp):
            for g in range(2):
                sp.dma_start(wg[:, g, :, :], w_gates[g].rearrange("n c e -> c n e")).then_inc(w_loaded, 16)

        @block.vector
        def _(dve):
            dve.wait_ge(z_ready, 1)
            dve.tensor_scalar(w[:, :], z[:, :], 2.0, None, ALU.add)
            dve.drain()
            dve.reciprocal(w[:, :], w[:, :])
            dve.drain()
            dve.tensor_tensor(w[:, :], w[:, :], z[:, :], ALU.mult)
            dve.drain()
            dve.tensor_tensor(w2[:, :], w[:, :], w[:, :], ALU.mult)
            dve.drain()
            dve.tensor_scalar(s[:, :], w2[:, :], 2.0 / 19, None, ALU.mult)
            for n in range(17, 1, -2):
                dve.drain()
                dve.scalar_tensor_tensor(out=s[:, :], in0=s[:, :], scalar=2.0 / n, in1=w2[:, :], op0=ALU.add, op1=ALU.mult)
            dve.drain()
            dve.scalar_tensor_tensor(out=s[:, :], in0=s[:, :], scalar=2.0, in1=w[:, :], op0=ALU.add, op1=ALU.mult)
            dve.tensor_scalar(z[:, :], q["lam"][:, :], -1.0, 0.0, ALU.mult, ALU.max)
            dve.drain()
            dve.tensor_tensor(s[:, :], s[:, :], z[:, :], ALU.add)
            dve.drain()
            dve.tensor_scalar(s[:, :], s[:, :], LRU_C, None, ALU.mult)
            for k in range(8):
                dve.tensor_scalar(xc[:, k, :], xa[:, k, :], q["conv_w"][:, k, 3:4], q["conv_b"][:, k:k + 1], ALU.mult, ALU.add)
            for t in range(1, 4):
                dve.drain()
                for k in range(8):
                    ins = dve.scalar_tensor_tensor(out=xc[:, k, t:], in0=xa[:, k, 0:SEQ - t],
                                                   scalar=q["conv_w"][:, k, 3 - t:4 - t], in1=xc[:, k, t:],
                                                   op0=ALU.mult, op1=ALU.add)
                    if t == 3:
                        ins.then_inc(convolved, 1)
            for k in range(8):
                dve.wait_ge(opened, 2 * k + 2)
                dve.tensor_scalar(r[:, k, :], r[:, k, :], s[:, k:k + 1], None, ALU.mult).then_inc(coef, 1)
                dve.tensor_tensor(i[:, k, :], i[:, k, :], xc[:, k, :], ALU.mult).then_inc(mixed, 1)
            dve.wait_ge(tanhed, 2)
            dve.tensor_tensor(xa[:, :, :], r[:, :, :], r[:, :, :], ALU.mult)
            dve.drain()
            dve.scalar_tensor_tensor(out=xa[:, :, :], in0=xa[:, :, :], scalar=1.0, in1=xc[:, :, :],
                                     op0=ALU.add, op1=ALU.mult).then_inc(u_ready, 1)
            dve.wait_ge(rooted, 1)
            dve.tensor_tensor(xa[:, :, :], xa[:, :, :], i[:, :, :], ALU.mult)
            dve.drain()
            for k in range(8):
                dve.tensor_tensor_scan(xc[:, k, :], r[:, k, :], xa[:, k, :], 0.0, ALU.mult, ALU.add)
            dve.drain()
            dve.wait_ge(gelued, 1)
            dve.tensor_tensor(y[:, :, :], xc[:, :, :], ga[:, :, :], ALU.mult)

        @block.tensor
        def _(pe):
            pe.wait_ge(w_loaded, 32)
            for k in range(8):
                pe.wait_ge(convolved, k + 1)
                if k == 0:
                    pe.wait_ge(convolved, 8)
                for g in range(2):
                    n = 2 * k + g
                    if n >= 4:
                        pe.wait_ge(opened, n - 3)
                    pe.matmul(c.ps[:, n % 4, :], wg[:, g, k, :], xc[:, k, :], start=True, stop=True).then_inc(gated, 1)

        @block.scalar
        def _(act):
            act.activation(z[:, :], q["lam"][:, :], ACT.Abs)
            act.drain()
            act.activation(z[:, :], z[:, :], ACT.Exp, scale=-1.0).then_inc(z_ready, 1)
            act.activation(ga[:, :, :], ga[:, :, :], ACT.Gelu_apprx_tanh).then_inc(gelued, 1)
            for k in range(8):
                for g, to in enumerate((r, i)):
                    act.wait_ge(gated, 2 * k + g + 1)
                    act.activation(to[:, k, :], c.ps[:, (2 * k + g) % 4, :], ACT.Sigmoid,
                                   bias=q["b_gates"][:, g, k:k + 1]).then_inc(opened, 1)
            act.wait_ge(coef, 8)
            act.wait_ge(mixed, 8)
            act.activation(xc[:, :, :], r[:, :, :], ACT.Tanh)
            act.drain().then_inc(tanhed, 1)
            act.activation(r[:, :, :], r[:, :, :], ACT.Exp, scale=-1.0).then_inc(tanhed, 1)
            act.wait_ge(u_ready, 1)
            act.activation(xa[:, :, :], xa[:, :, :], ACT.Sqrt).then_inc(rooted, 1)


class Nsa:
    def __init__(self, nc, ctx):
        def sb(name, shape):
            return ctx.enter_context(nc.sbuf_tensor(f"{name}_{nc.next_id()}", shape, F32))
        self.qk = sb("qk", [P, 14, SEQ])
        self.q = self.qk[:, 0:8, :]
        self.p_cmp = self.qk[:, 8:12, :]
        self.k_slc = sb("k_slc", [P, N_KV, SEQ])
        self.k_win = sb("k_win", [P, N_KV, SEQ])
        self.v_slc = sb("v_slc", [P, TT, 256])
        self.v_win = sb("v_win", [P, TT, 256])
        self.gate = sb("gate", [P, TT, 3 * N_HEADS])
        self.k_cmp = sb("k_cmp", [P, N_KV, 32])
        self.v_cmp = sb("v_cmp", [P, N_KV, N_DIM])


def spread_keys(nc, c, n, kw):
    with Stage(nc) as st:
        block = st.block()

        @block.scalar
        def _(act):
            for dst, kk in ((n.k_slc, n.qk[:, 12:14, :]), (n.k_win, kw)):
                for g in range(N_KV):
                    b = 64 * (g % 2)
                    act.activation(dst[0:64, g, :], kk[b:b + 64, g // 2, :], ACT.Copy)
            act.activation(n.gate[:, :, :], n.gate[:, :, :], ACT.Sigmoid)

        @block.vector
        def _(dve):
            for dst, kk in ((n.k_slc, n.qk[:, 12:14, :]), (n.k_win, kw)):
                for g in range(N_KV):
                    b = 64 * (g % 2)
                    dve.tensor_copy(dst[64:P, g, :], kk[b:b + 64, g // 2, :])


def compress(nc, c, n, kv, spare, pos, w1, w2):
    with Stage(nc) as st:
        base = spare[0:64, :, :].rearrange("p (i g) t -> p i g t", i=2)
        tap = st.sb("tap", [64, 2, 2, N_KV, SEQ])
        pos_T = st.sb("pos_T", [64, 2, TAPS])
        w1s = st.sb("w1s", [64, 2, TAPS // 2, HIDDEN])
        w2s = st.sb("w2s", [P, 2, 2, P])
        hid = st.sb("hid", [P, 2, 2, N_KV, 32])
        hid4 = st.sb("hid4", [P, 2, N_KV, GROUP, 32])
        pos_loaded, w2_loaded, moved, tapped, hidden, netted, spread, outed, multiplied = (
            st.sem(x) for x in ("pos_loaded", "w2_loaded", "moved", "tapped", "hidden", "netted", "spread", "outed",
                                "multiplied"))
        w1_loaded = [st.sem(f"w1_loaded{s}") for s in range(2)]
        block = st.block()

        @block.sync
        def _(sp):
            with nc.allow_non_contiguous_dma(reason="small positions, turned"):
                for i in range(2):
                    sp.dma_start(pos_T[:, i, :], pos[i].rearrange("l d -> d l")).then_inc(pos_loaded, 16)
            for i in range(2):
                for half in range(2):
                    u = 2 * i + half
                    if u >= 2:
                        sp.wait_ge(multiplied, u - 1)
                    sp.dma_start(w1s[:, half, :, :],
                                 w1[i, half * 1024:(half + 1) * 1024, :].rearrange("(l d) f -> d l f", d=N_DIM))\
                        .then_inc(w1_loaded[half], 16)
                for twice in range(2):
                    sp.dma_start(w2s[:, i, :, 64 * twice:64 * twice + 64], w2[i].rearrange("(k p) d -> p k d", p=P))\
                        .then_inc(w2_loaded, 16)

        @block.scalar
        def _(act):
            for i in range(2):
                for g in range(N_KV):
                    b = 64 * (g % 2)
                    ins = act.activation(base[:, i, g, :], kv[b:b + 64, 2 * i + g // 2, :], ACT.Copy)
            ins.then_inc(moved, 1)
            for i in range(2):
                act.wait_ge(hidden, i + 1)
                for k in range(2):
                    ins = act.activation(hid[:, i, k, :, 0:N_CMP],
                                         c.ps[:, 2 * i + k, 0:N_KV * N_CMP].rearrange("p (g n) -> p g n", n=N_CMP),
                                         ACT.Gelu_apprx_tanh)
                ins.then_inc(netted, 1)
            act.wait_ge(outed, 1)
            act.activation(n.k_cmp[:, :, 0:N_CMP], c.ps[:, 4, 0:N_KV * N_CMP].rearrange("p (g n) -> p g n", n=N_CMP), ACT.Copy)
            act.wait_ge(outed, 2)
            act.activation(n.v_cmp[:, :, :], c.ps[:, 5, 0:N_KV * N_DIM].rearrange("p (g d) -> p g d", d=N_DIM), ACT.Copy)

        @block.vector
        def _(dve):
            dve.memset(hid[:, :, :, :, N_CMP:32], 0.0)
            dve.wait_ge(pos_loaded, 32)
            dve.wait_ge(moved, 1)
            for i in range(2):
                for half in range(2):
                    add = pos_T[:, i, 16 * half:16 * half + 16].rearrange("p (o l) -> p o l", o=1)
                    ins = dve.tensor_tensor(tap[:, i, half, :, :].rearrange("p g (n l) -> p (g n) l", l=16),
                                            base[:, i, :, :].rearrange("p g (n l) -> p (g n) l", l=16),
                                            add.to_broadcast([64, N_KV * 32, 16]), ALU.add)
            ins.then_inc(tapped, 1)
            dve.drain()
            dve.wait_ge(netted, 2)
            for k in range(2):
                ins = dve.tensor_copy(hid4[:, k, :, :, :],
                                      hid[:, 1, k, :, :].rearrange("p g (o n) -> p g o n", o=1)
                                      .to_broadcast([P, N_KV, GROUP, 32]))
            ins.then_inc(spread, 1)

        @block.tensor
        def _(pe):
            pe.wait_ge(tapped, 1)
            for i in range(2):
                for half in range(2):
                    pe.wait_ge(w1_loaded[half], 16 * i + 16)
                    for k in range(2):
                        for l in range(16):
                            src = tap[:, i, half, :, :].rearrange("p g (n l) -> p g n l", l=16)[:, :, half:half + N_CMP, l]
                            mm = pe.matmul(c.ps[:, 2 * i + k, 0:N_KV * N_CMP], w1s[:, half, l, k * P:(k + 1) * P], src,
                                           start=(half == 0 and l == 0), stop=(half == 1 and l == 15))
                    mm.then_inc(multiplied, 1)
                    if half == 1:
                        pe.wait_ge(multiplied, 2 * i + 2)
                        pe.drain().then_inc(hidden, 1)
            pe.wait_ge(w2_loaded, 64)
            pe.wait_ge(netted, 2)
            for k in range(2):
                mm = pe.matmul(c.ps[:, 4, 0:N_KV * N_CMP], w2s[:, 0, k, :], hid[:, 0, k, :, 0:N_CMP], start=(k == 0), stop=(k == 1))
            mm.then_inc(outed, 1)
            pe.wait_ge(spread, 1)
            for g in range(N_KV):
                for k in range(2):
                    mm = pe.matmul(c.ps[:, 5, g * N_DIM:(g + 1) * N_DIM], hid4[:, k, g, :, :].rearrange("p r n -> p (r n)"),
                                   w2s[:, 1, k, 0:N_DIM], start=(k == 0), stop=(k == 1))
            mm.then_inc(outed, 1)


def compressed_scores(nc, c, n, tiles):
    with Stage(nc) as st:
        e = st.sb("e", [P, 2, N_HEADS, 32])
        mx = st.sb("mx", [P, 2, N_HEADS])
        tot = st.sb("tot", [P, 2, N_HEADS])
        scored, shifted, exped, ready, turned, laid = (
            st.sem(x) for x in ("scored", "shifted", "exped", "ready", "turned", "laid"))
        block = st.block()

        def wide(ap, w):
            return ap.rearrange("p (h o) -> p h o", o=1).to_broadcast([P, N_HEADS, w])

        @block.tensor
        def _(pe):
            for qi in range(TT):
                nv = 8 * qi + 7
                if qi >= 2:
                    pe.wait_ge(shifted, qi - 1)
                for h in range(N_HEADS):
                    b = 64 * (h % 2)
                    at = 32 * (h // 2)
                    mm = pe.matmul(c.ps[:, 2 * (qi % 2) + h % 2, at:at + nv], n.q[b:b + 64, h // 2, qi * P:(qi + 1) * P],
                                   n.k_cmp[b:b + 64, h // GROUP, 0:nv], start=True, stop=True)
                mm.then_inc(scored, 1)
                pe.wait_ge(ready, qi + 1)
                if qi >= 1:
                    pe.wait_ge(laid, qi)
                for g in range(N_KV):
                    mm = pe.transpose(c.ps[:, 4, g * P:(g + 1) * P],
                                      e[:, qi % 2, GROUP * g:GROUP * (g + 1), :].rearrange("p h n -> p (h n)"), c.ident[:, :])
                mm.then_inc(turned, 1)

        @block.vector
        def _(dve):
            dve.memset(e[:, :, :, :], 0.0)
            for qi in range(TT):
                nv = 8 * qi + 7
                s = qi % 2
                dve.drain()
                dve.wait_ge(scored, qi + 1)
                if qi >= 2:
                    dve.wait_ge(turned, qi - 1)
                at = 415 - P * qi
                for half in range(2):
                    dve.tensor_tensor(e[:, s, half::2, 0:nv],
                                      c.ps[:, 2 * s + half, 0:256].rearrange("p (h n) -> p h n", n=32)[:, :, 0:nv],
                                      tiles[:, half::2, at:at + 16 * nv - 15:16], ALU.add)
                dve.drain()
                dve.tensor_reduce(mx[:, s, :], e[:, s, :, 0:nv], AX, ALU.max)
                dve.drain()
                dve.tensor_scalar(mx[:, s, :], mx[:, s, :], MASKED / 100, None, ALU.max)
                dve.drain()
                dve.tensor_tensor(e[:, s, :, 0:nv], e[:, s, :, 0:nv], wide(mx[:, s, :], nv), ALU.subtract).then_inc(shifted, 1)
                dve.wait_ge(exped, qi + 1)
                dve.reduce_sum(tot[:, s, :], e[:, s, :, 0:nv], AX)
                dve.drain()
                dve.tensor_scalar(tot[:, s, :], tot[:, s, :], 1e-30, None, ALU.max)
                dve.drain()
                dve.reciprocal(tot[:, s, :], tot[:, s, :])
                dve.drain()
                dve.tensor_tensor(tot[:, s, :], tot[:, s, :], n.gate[:, qi, 0:N_HEADS], ALU.mult)
                dve.drain()
                dve.tensor_tensor(e[:, s, :, 0:nv], e[:, s, :, 0:nv], wide(tot[:, s, :], nv), ALU.mult).then_inc(ready, 1)

        @block.scalar
        def _(act):
            for qi in range(TT):
                nv = 8 * qi + 7
                act.wait_ge(shifted, qi + 1)
                act.activation(e[:, qi % 2, :, 0:nv], e[:, qi % 2, :, 0:nv], ACT.Exp,
                               scale=N_DIM ** -0.5).then_inc(exped, 1)
                act.wait_ge(turned, qi + 1)
                act.activation(n.p_cmp[:, :, qi * P:(qi + 1) * P], c.ps[:, 4, :].rearrange("p (g q) -> p g q", q=P), ACT.Copy)\
                    .then_inc(laid, 1)


def nsa_attention(nc, c, n, tiles, y):
    units = [(h, qi, i) for h in range(N_HEADS) for qi in range(TT) for i in range(2)]
    U = len(units)
    PER = 2 * TT
    with Stage(nc) as st:
        neg = st.sb("neg", [P, 4, SEQ])
        prob_T = st.sb("prob_T", [P, 2, 2, TT, SEQ])
        win = st.sb("win", [P, 2, 3 * P])
        nmax, total, recip = (st.sb(x, [P, 4]) for x in ("nmax", "total", "recip"))
        win_ready, scored, biased, exped, scaled, turned, laid, outed, kept = (
            st.sem(x) for x in ("win_ready", "scored", "biased", "exped", "scaled", "turned", "laid", "outed", "kept"))
        block = st.block()
        TURN, OUT = 3, 6

        def first_key(u):
            h, qi, i = units[u]
            return 0 if i == 0 else max(0, qi - 2)

        def width(u):
            return P * (units[u][1] + 1 - first_key(u))

        @block.gpsimd
        def _(pool):
            for h in range(N_HEADS):
                if h >= 2:
                    pool.wait_ge(biased, PER * (h - 1))
                pool.tensor_tensor(win[:, h % 2, 0:P], tiles[:, h, P:2 * P], c.winmask[:, :], ALU.add)
                pool.tensor_copy(win[:, h % 2, P:3 * P], tiles[:, h, 2 * P:4 * P])
                pool.drain().then_inc(win_ready, 1)

        @block.tensor
        def _(pe):
            def score(u):
                h, qi, i = units[u]
                if u >= 3:
                    pe.wait_ge(biased, u - 2)
                b, g = 64 * (h % 2), h // GROUP
                k0 = P * first_key(u)
                pe.matmul(c.ps[:, u % 3, 0:width(u)], n.q[b:b + 64, h // 2, qi * P:(qi + 1) * P],
                          (n.k_slc, n.k_win)[i][b:b + 64, g, k0:P * (qi + 1)], start=True, stop=True).then_inc(scored, 1)

            def turn(u):
                pe.wait_ge(scaled, u + 1)
                if u >= 3:
                    pe.wait_ge(laid, u - 2)
                for j in range(width(u) // P):
                    mm = pe.transpose(c.ps[:, TURN + u % 3, j * P:(j + 1) * P], neg[:, u % 4, j * P:(j + 1) * P], c.ident[:, :])
                mm.then_inc(turned, 1)

            def out(h):
                pe.wait_ge(laid, PER * (h + 1))
                if h >= 2:
                    pe.wait_ge(kept, h - 1)
                b, g, r = 64 * (h % 2), h // GROUP, h % GROUP
                to = OUT + h % 2
                pe.matmul(c.ps[b:b + 64, to, :], n.v_cmp[32 * r:32 * r + 32, g, :], n.p_cmp[32 * r:32 * r + 32, g, :],
                          start=True, stop=False)
                for i, v in enumerate((n.v_slc, n.v_win)):
                    for j in range(TT):
                        end = SEQ if i == 0 else min(SEQ, P * (j + 3))
                        mm = pe.matmul(c.ps[b:b + 64, to, j * P:end], v[:, j, g * N_DIM:(g + 1) * N_DIM],
                                       prob_T[:, h % 2, i, j, j * P:end], start=False, stop=(i == 1 and j == TT - 1))
                mm.then_inc(outed, 1)

            for u in range(3):
                score(u)
            for u in range(U):
                if u + 3 < U:
                    score(u + 3)
                turn(u)
                if u % PER == 3 and u > PER:
                    out(u // PER - 1)
            out(N_HEADS - 1)

        @block.vector
        def _(dve):
            def bias(u):
                h, qi, i = units[u]
                w = width(u)
                dve.wait_ge(scored, u + 1)
                if u >= 4:
                    dve.wait_ge(turned, u - 3)
                if u % PER == 0:
                    dve.wait_ge(win_ready, h + 1)
                bias_of = win[:, h % 2, 3 * P - w:] if i == 1 else tiles[:, h, SEQ - w:]
                dve.tensor_tensor_reduce(neg[:, u % 4, 0:w], c.ps[:, u % 3, 0:w], bias_of, -(N_DIM ** -0.5), 3e38,
                                         ALU.add, ALU.min, nmax[:, u % 4:u % 4 + 1]).then_inc(biased, 1)

            def scale(u):
                h, qi, i = units[u]
                w, s = width(u), u % 4
                dve.wait_ge(exped, u + 1)
                dve.reciprocal(recip[:, s:s + 1], total[:, s:s + 1])
                dve.drain()
                at = N_HEADS * (i + 1) + h
                dve.tensor_scalar(neg[:, s, 0:w], neg[:, s, 0:w], recip[:, s:s + 1], n.gate[:, qi, at:at + 1],
                                  ALU.mult, ALU.mult).then_inc(scaled, 1)

            bias(0)
            bias(1)
            for u in range(U):
                if u + 2 < U:
                    bias(u + 2)
                scale(u)

        @block.scalar
        def _(act):
            def exps(u):
                s, w = u % 4, width(u)
                act.wait_ge(biased, u + 1)
                act.activation(neg[:, s, 0:w], neg[:, s, 0:w], ACT.Exp, scale=-1.0, bias=nmax[:, s:s + 1],
                               accum_out=total[:, s:s + 1]).then_inc(exped, 1)

            def lay(u):
                h, qi, i = units[u]
                act.wait_ge(turned, u + 1)
                if h >= 2 and u % PER == 0:
                    act.wait_ge(outed, h - 1)
                act.activation(prob_T[:, h % 2, i, first_key(u):qi + 1, qi * P:(qi + 1) * P],
                               c.ps[:, TURN + u % 3, 0:width(u)].rearrange("p (j q) -> p j q", q=P), ACT.Copy)\
                    .then_inc(laid, 1)

            def keep(h):
                act.wait_ge(outed, h + 1)
                b = 64 * (h % 2)
                act.activation(y[b:b + 64, h // 2, :], c.ps[b:b + 64, OUT + h % 2, :], ACT.Copy).then_inc(kept, 1)

            exps(0)
            for u in range(U):
                if u + 1 < U:
                    exps(u + 1)
                if u >= 1:
                    lay(u - 1)
                if u % PER == PER - 1 and u >= PER:
                    keep(u // PER - 1)
            lay(U - 1)
            keep(N_HEADS - 1)


class Gla:
    def __init__(self, nc, ctx):
        def sb(name, shape):
            return ctx.enter_context(nc.sbuf_tensor(f"{name}_{nc.next_id()}", shape, F32))
        self.qk = sb("gqk", [P, 8, SEQ])
        self.q, self.k = self.qk[:, 0:4, :], self.qk[:, 4:8, :]
        self.og = sb("og", [P, 8, SEQ])
        self.v = sb("gv", [P, TT, D])
        self.lr = sb("lr", [16, SEQ])
        self.wa2 = sb("wa2", [16, 512])
        self.ba = sb("ba", [P, 4])
        self.gain = sb("ggain", [P, 2])


def gla_prepare(nc, c, g):
    with Stage(nc) as st:
        x, l, b, d = (st.sb(n, [P, 4, SEQ]) for n in ("x", "l", "b", "d"))
        gated, logged, ready, b_ready, exped, k_ready, turned, q_ready = (
            st.sem(n) for n in ("gated", "logged", "ready", "b_ready", "exped", "k_ready", "turned", "q_ready"))
        block = st.block()

        def chunks(ap):
            return ap.rearrange("p h (c t) -> p (h c) t", t=G_CHUNK)

        @block.tensor
        def _(pe):
            for h in range(G_HEADS):
                mm = pe.matmul(c.ps[:, h, :], g.wa2[:, h * P:(h + 1) * P], g.lr[:, :], start=True, stop=True)
            mm.then_inc(gated, 1)
            pe.wait_ge(k_ready, 1)
            for t in range(TT):
                for h in range(G_HEADS):
                    mm = pe.transpose(c.ps[:, 4 + t, h * P:(h + 1) * P], g.k_end[:, h, t * P:(t + 1) * P], c.ident[:, :])
            mm.then_inc(turned, 1)

        @block.scalar
        def _(act):
            act.wait_ge(gated, 1)
            for h in range(G_HEADS):
                act.activation(x[:, h, :], c.ps[:, h, :], ACT.Identity, bias=g.ba[:, h:h + 1])
            act.drain()
            act.activation(l[:, :, :], x[:, :, :], ACT.Abs)
            act.drain()
            act.activation(l[:, :, :], l[:, :, :], ACT.Exp, scale=-1.0)
            act.drain()
            act.activation(l[:, :, :], l[:, :, :], ACT.Ln, bias=c.one[:, :])
            act.drain().then_inc(logged, 1)
            act.wait_ge(b_ready, 1)
            act.activation(x[:, :, :], b[:, :, :], ACT.Exp, scale=1.0 / 16)
            act.activation(l[:, :, :], b[:, :, :], ACT.Exp, scale=-1.0 / 16)
            act.activation(g.decay[:, :, :].rearrange("p h c -> p (h c)"), chunks(b[:, :, :])[:, :, G_CHUNK - 1], ACT.Exp,
                           scale=1.0 / 16)
            act.activation(d[:, :, :], d[:, :, :], ACT.Exp, scale=1.0 / 16)
            act.drain().then_inc(exped, 1)
            act.wait_ge(turned, 1)
            act.activation(g.k_end_t[:, :, :, :].rearrange("p t h d -> p t (h d)"), c.ps[:, 4:8, :], ACT.Copy)

        @block.vector
        def _(dve):
            dve.wait_ge(logged, 1)
            dve.scalar_tensor_tensor(out=x[:, :, :], in0=x[:, :, :], scalar=0.0, in1=l[:, :, :], op0=ALU.min, op1=ALU.subtract)
            dve.drain()
            for h in range(G_HEADS):
                dve.tensor_tensor_scan(b[:, h, :], c.scanone[:, :], x[:, h, :], 0.0, ALU.mult, ALU.add)
            dve.drain()
            last = chunks(b[:, :, :])[:, :, G_CHUNK - 1:G_CHUNK].to_broadcast([P, 4 * G_CHUNKS, G_CHUNK])
            dve.tensor_tensor(chunks(d[:, :, :]), last, chunks(b[:, :, :]), ALU.subtract)
            dve.drain().then_inc(b_ready, 1)
            dve.wait_ge(exped, 1)
            dve.tensor_tensor(g.k_end[:, :, :], g.k[:, :, :], d[:, :, :], ALU.mult).then_inc(k_ready, 1)
            dve.tensor_tensor(g.k[:, :, :], g.k[:, :, :], l[:, :, :], ALU.mult)
            dve.scalar_tensor_tensor(out=g.q[:, :, :], in0=g.q[:, :, :], scalar=P ** -0.5, in1=x[:, :, :],
                                     op0=ALU.mult, op1=ALU.mult)


def gla_scan(nc, c, g, o_T):
    with Stage(nc) as st:
        att = st.sb("att", [P, TT, G_HEADS, P])
        state = st.sb("state", [P, 2, G_HEADS, G_DV])
        scored, masked, updated, stepped, read, outed, kept = (
            st.sem(n) for n in ("scored", "masked", "updated", "stepped", "read", "outed", "kept"))
        block = st.block()

        def product_for_state(k, h):
            return c.ps[:, 4 + 2 * (k % 2) + h // 2, (h % 2) * G_DV:(h % 2 + 1) * G_DV]

        @block.tensor
        def _(pe):
            def scores(t):
                if t >= 1:
                    pe.wait_ge(masked, t)
                for h in range(G_HEADS):
                    mm = pe.matmul(c.ps[:, 2, h * P:(h + 1) * P], g.k[:, h, t * P:(t + 1) * P], g.q[:, h, t * P:(t + 1) * P],
                                   start=True, stop=True)
                mm.then_inc(scored, 1)

            def update(k):
                if k >= 2:
                    pe.wait_ge(stepped, k - 1)
                t, b = k // 4, G_CHUNK * (k % 4)
                for h in range(G_HEADS):
                    mm = pe.matmul(product_for_state(k, h), g.k_end_t[b:b + 32, t, h, :],
                                   g.v[b:b + 32, t, h * G_DV:(h + 1) * G_DV], start=True, stop=True)
                mm.then_inc(updated, 1)

            scores(0)
            update(0)
            for t in range(TT):
                pe.wait_ge(masked, t + 1)
                if t >= 1:
                    pe.wait_ge(kept, t)
                for h in range(G_HEADS):
                    for e in range(2):
                        n = 2 * h + e
                        pe.matmul(c.ps[:, n // 4, (n % 4) * P:(n % 4 + 1) * P], g.v[:, t, h * G_DV + e * P:h * G_DV + (e + 1) * P],
                                  att[:, t, h, :], start=(n % 4 == 0), stop=False, skip_group_check=True)
                if t + 1 < TT:
                    scores(t + 1)
                for s in range(4):
                    k = 4 * t + s
                    if k + 2 < G_CHUNKS:
                        update(k + 1)
                    if k >= 1:
                        pe.wait_ge(stepped, k)
                        for h in range(G_HEADS):
                            for e in range(2):
                                n = 2 * h + e
                                at = (n % 4) * P + s * G_CHUNK
                                mm = pe.matmul(c.ps[:, n // 4, at:at + G_CHUNK], state[:, k % 2, h, e * P:(e + 1) * P],
                                               g.q[:, h, k * G_CHUNK:(k + 1) * G_CHUNK], start=False, stop=(s == 3),
                                               skip_group_check=True)
                        mm.then_inc(read, 1)
                    if s == 3:
                        mm = pe.drain().then_inc(outed, 1)

        @block.vector
        def _(dve):
            def mask(t):
                dve.wait_ge(scored, t + 1)
                dve.tensor_tensor(att[:, t, :, :], c.ps[:, 2, :].rearrange("p (h t) -> p h t", t=P),
                                  c.chunkmask[:, :].rearrange("p (o t) -> p o t", o=1).to_broadcast([P, G_HEADS, P]), ALU.mult)\
                    .then_inc(masked, 1)

            mask(0)
            for k in range(G_CHUNKS - 1):
                if k % 4 == 0 and k // 4 + 1 < TT:
                    mask(k // 4 + 1)
                dve.wait_ge(updated, k + 1)
                if k >= 2:
                    dve.wait_ge(read, k - 1)
                dve.drain()
                for h in range(G_HEADS):
                    new = product_for_state(k, h)
                    if k == 0:
                        ins = dve.tensor_copy(state[:, 1, h, :], new)
                    else:
                        ins = dve.scalar_tensor_tensor(out=state[:, (k + 1) % 2, h, :], in0=state[:, k % 2, h, :],
                                                       scalar=g.decay[:, h, k:k + 1], in1=new, op0=ALU.mult, op1=ALU.add)
                ins.then_inc(stepped, 1)

        @block.scalar
        def _(act):
            for t in range(TT):
                act.wait_ge(outed, t + 1)
                act.activation(o_T[:, :, t * P:(t + 1) * P], c.ps[:, 0:2, :].rearrange("p b (n q) -> p (b n) q", q=P), ACT.Copy)\
                    .then_inc(kept, 1)


def gla_finish(nc, c, g, o_T, y):
    with Stage(nc) as st:
        sq = st.sb("sq", [P, 8, SEQ])
        rstd = st.sb("rstd", [P, 4, SEQ])
        squared, summed, rooted, opened = (st.sem(n) for n in ("squared", "summed", "rooted", "opened"))
        block = st.block()

        @block.scalar
        def _(act):
            act.activation(sq[:, :, :], o_T[:, :, :], ACT.Square).then_inc(squared, 1)
            act.activation(g.og[:, :, :], g.og[:, :, :], ACT.Silu).then_inc(opened, 1)
            act.wait_ge(summed, 1)
            act.activation(rstd[:, :, :], c.ps[:, 0:4, :], ACT.Sqrt, scale=1.0 / G_DV, bias=c.eps[:, :]).then_inc(rooted, 1)

        @block.tensor
        def _(pe):
            pe.wait_ge(squared, 1)
            for h in range(G_HEADS):
                for e in range(2):
                    mm = pe.matmul(c.ps[:, h, :], c.ones[:, :], sq[:, 2 * h + e, :], start=(e == 0), stop=(e == 1))
            mm.then_inc(summed, 1)

        @block.vector
        def _(dve):
            dve.wait_ge(opened, 1)
            dve.tensor_tensor(g.og[:, :, :], g.og[:, :, :], o_T[:, :, :], ALU.mult)
            dve.drain()
            dve.wait_ge(rooted, 1)
            dve.reciprocal(rstd[:, :, :], rstd[:, :, :])
            dve.drain()
            for k in range(8):
                dve.scalar_tensor_tensor(out=y[:, k, :], in0=g.og[:, k, :], scalar=g.gain[:, k % 2:k % 2 + 1],
                                         in1=rstd[:, k // 2, :], op0=ALU.mult, op1=ALU.mult)


def second_block(nc, c, W, scratch):
    w_in = W["w_in"]
    norm(nc, c, W["norm_g"][0])
    with ExitStack() as ctx:
        def sb(name, shape, to=ctx):
            return to.enter_context(nc.sbuf_tensor(f"{name}_{nc.next_id()}", shape, F32))
        y = sb("y", [P, KD, SEQ])

        def branch(i, first):
            gated_stage(nc, c, w_in[:, MERGE + i * D:MERGE + (i + 1) * D], W["w_branch"][i], KD, ACT.Sigmoid,
                        y=y, merged=merged, accumulate=not first)

        with ExitStack() as work:
            n = Nsa(nc, work)
            with ExitStack() as early:
                kw = sb("kw", [P, 2, SEQ], early)
                at = NSA_KV
                project(nc, c, w_in, [(NSA_Q, 12, n.qk[:, 0:12, :]), (at + 512, 2, n.qk[:, 12:14, :]), (at + 1024, 2, kw[:, :, :])],
                        [], [(at + 768, 2 * P, n.v_slc[:, :, :]), (at + 1280, 2 * P, n.v_win[:, :, :]),
                             (NSA_GATE, 3 * N_HEADS, n.gate[:, :, :])])
                spread_keys(nc, c, n, kw)
                compress(nc, c, n, n.qk[:, 8:12, :], y, W["cmp_pos"], W["cmp_w1"], W["cmp_w2"])
            tiles = sb("tiles", [P, N_HEADS, SEQ], work)
            bias_rows(nc, c, W["rel_table"], N_HEADS, scratch)
            bias_tiles(nc, c, scratch, N_HEADS, tiles, N_DIM ** 0.5)
            compressed_scores(nc, c, n, tiles)
            nsa_attention(nc, c, n, tiles, y)
        merged = sb("merged", [P, KD, SEQ])
        branch(1, True)
        with ExitStack() as work:
            xg = sb("xg", [P, 16, SEQ], work)
            q, loads = lru_params(nc, work, W)
            project(nc, c, w_in, [(LRU_X, 16, xg[:, :, :])], [], [], loads)
            lru_mixer(nc, c, q, W["lru_w_gates"], xg[:, 0:8, :], xg[:, 8:16, :], y)
        branch(0, False)
        with ExitStack() as work:
            g = Gla(nc, work)
            params = [(g.wa2[:, :], W["gla_wa2"]), (g.ba[:, :], W["gla_ba"].rearrange("(k p) -> p k", p=P)),
                      (g.gain[:, :], W["gla_norm"].rearrange("(k p) -> p k", p=P))]
            project(nc, c, w_in, [(GLA_Q, 8, g.qk[:, :, :]), (GLA_OG, 8, g.og[:, :, :])], [(GLA_LR, 16, g.lr[:, :])],
                    [(GLA_V + 2 * P * i, 2 * P, g.v[:, :, 2 * P * i:2 * P * (i + 1)]) for i in range(4)], params)
            g.k_end, g.k_end_t = sb("k_end", [P, 4, SEQ], work), sb("k_end_t", [P, TT, 4, P], work)
            g.decay = sb("decay", [P, 4, G_CHUNKS], work)
            gla_prepare(nc, c, g)
            gla_scan(nc, c, g, y)
            gla_finish(nc, c, g, y, y)
        branch(2, False)
        mixed = sb("mixed", [P, KD, SEQ])
        project_out(nc, c, W["w_out"], merged, mixed, False)
        norm(nc, c, W["norm_g"][1], src=mixed, add_to=c.x_T)
    norm(nc, c, W["norm_g"][2])
    with ExitStack() as ctx:
        fed = ctx.enter_context(nc.sbuf_tensor("fed", [P, 4, KD, P], F32))
        ffn(nc, c, W["w_ffn_in"][:, 0:FF], W["w_ffn_in"][:, FF:2 * FF], W["w_ffn_out"], 1.0, raw=fed)
        norm(nc, c, W["norm_g"][3], src=feature_major(fed), add_to=c.x_T)




FIRST = ["ffn1_norm_w", "ffn1_w_gate", "ffn1_w_up", "ffn1_w_down", "mix_norm_w", "w_in", "mlstm_gate_bias",
         "mlstm_norm_w", "ssm_conv_w", "ssm_conv_b", "ssm_dt_bias", "ssm_A_log", "ssm_D", "ssm_norm_w",
         "diff_q_norm_w", "diff_k_norm_w", "diff_lambda", "diff_subln_w", "w_out", "ffn2_norm_w", "ffn2_w_gate",
         "ffn2_w_up", "ffn2_w_down"]


def lambda_init(nc, c, layer, now):
    with Stage(nc) as st:
        block = st.block()

        @block.vector
        def _(dve):
            for l in range(LAYERS):
                dve.memset(c.lam_init[:, l:l + 1], 0.8 - 0.6 * float(np.exp(-0.3 * l)))
            dve.drain()
            dve.tensor_copy(now[:, :], c.lam_init[:, bass.ds(layer, 1)])


def program(nc, A, out):
    scratch = nc.dram_tensor("bias_scratch", [DF_HEADS + N_HEADS, BACK + SEQ], F32, kind="Internal").ap()
    with ExitStack() as ctx:
        c = Shared(nc, ctx)
        consts(nc, c)
        load_x(nc, c, A["x"])
        with ExitStack() as first:
            now = first.enter_context(nc.sbuf_tensor("lam_init_now", [P, 1], F32))
            bias_rows(nc, c, A["rel_bias"], DF_HEADS, scratch[0:DF_HEADS])
            with nc.Fori(0, LAYERS) as layer:
                L = {name: A[name][layer] for name in FIRST}
                norm(nc, c, L["ffn1_norm_w"])
                ffn(nc, c, L["ffn1_w_gate"], L["ffn1_w_up"], L["ffn1_w_down"], 0.5)
                norm(nc, c, L["mix_norm_w"])
                lambda_init(nc, c, layer, now)
                first_mixer(nc, c, L, L["w_in"], L["w_out"], scratch[0:DF_HEADS], now[:, 0:1])
                norm(nc, c, L["ffn2_norm_w"])
                ffn(nc, c, L["ffn2_w_gate"], L["ffn2_w_up"], L["ffn2_w_down"], 0.5)
        W = {name[:-2]: (ap if name == "rel_table_2" else ap[0]) for name, ap in A.items() if name.endswith("_2")}
        second_block(nc, c, W, scratch[DF_HEADS:])
        store_x(nc, c, out)


_INS = ["x", "ffn1_norm_w", "ffn1_w_gate", "ffn1_w_up", "ffn1_w_down", "mix_norm_w", "w_in", "mlstm_gate_bias",
        "mlstm_norm_w", "ssm_conv_w", "ssm_conv_b", "ssm_dt_bias", "ssm_A_log", "ssm_D", "ssm_norm_w",
        "diff_q_norm_w", "diff_k_norm_w", "diff_lambda", "diff_subln_w", "rel_bias", "w_out", "ffn2_norm_w",
        "ffn2_w_gate", "ffn2_w_up", "ffn2_w_down", "rel_table_2", "norm_g_2", "w_in_2", "conv_w_2", "conv_b_2",
        "lru_w_gates_2", "lru_b_gates_2", "lru_lambda_2", "cmp_pos_2", "cmp_w1_2", "cmp_w2_2", "gla_wa2_2",
        "gla_ba_2", "gla_norm_2", "w_branch_2", "w_out_2", "w_ffn_in_2", "w_ffn_out_2"]
_OUTS = [((1, 512, 1024), "float32")]


def kernel(**inputs):
    import numpy as _np
    import concourse.bacc as _bacc
    from concourse import mybir as _mybir
    from concourse.bass_utils import run_bass_kernel_spmd as _run

    nc = _bacc.Bacc("TRN2", target_bir_lowering=False, num_devices=1)
    arrays, args = {}, {}
    for name in _INS:
        a = _np.ascontiguousarray(inputs[name])
        arrays[f"in_{name}_dram"] = a
        args[name] = nc.dram_tensor(f"in_{name}_dram", a.shape, _mybir.dt.from_np(a.dtype), kind="ExternalInput").ap()
    out = nc.dram_tensor("out_0_dram", _OUTS[0][0], _mybir.dt.from_np(_np.dtype(_OUTS[0][1])), kind="ExternalOutput").ap()
    program(nc, args, out)
    r = _run(nc, [arrays], core_ids=[0])
    return r.results[0]["out_0_dram"]
```

```python
from contextlib import ExitStack, contextmanager

import numpy as np
import concourse.bass as bass
from concourse import mybir

F32 = mybir.dt.float32
F32R = mybir.dt.float32r
ACT = mybir.ActivationFunctionType
ALU = mybir.AluOpType
AX = mybir.AxisListType.X

P = 128
SEQ = 512
TT = SEQ // P
D = 1024
KD = D // P
LAYERS = 2
FF = 2816
KF = FF // P
BANK = 512
EPS = 1e-6
MASKED = -1e30

TRI_W = [SEQ - P * j for j in range(TT)]
TRI_AT = [0, 512, 1024, 896]
TRI = sum(TRI_W)


class Stage:

    def __init__(self, nc, within=None):
        self.nc = nc
        self.within = within
        self.ctx = ExitStack()
        self.sems = []
        self.engines = None

    def sem(self, name):
        if self.within is not None:
            return self.within.sem(f"{name}_{self.nc.next_id()}")
        s = self.ctx.enter_context(self.nc.semaphore(name))
        self.sems.append(s)
        return s

    def sb(self, name, shape, dtype=F32):
        if self.within is not None:
            return self.within.sb(name, shape, dtype)
        return self.ctx.enter_context(self.nc.sbuf_tensor(f"{name}_{self.nc.next_id()}", shape, dtype))

    def block(self):
        if self.within is not None:
            return self.within.block()
        if self.engines is None:
            self.engines = self.nc.Block(no_gpsimd_drain=True)
            self.open_block = self.engines.__enter__()
        return self.open_block

    def __enter__(self):
        return self

    def __exit__(self, kind, value, trace):
        if self.within is not None:
            return False
        if self.engines is not None:
            self.engines.__exit__(kind, value, trace)
        if kind is None:
            for s in self.sems:
                self.nc.sync.sem_clear(s)
            self.nc.all_engine_barrier()
        return self.ctx.__exit__(kind, value, trace)


def bcast(ap, n):
    return ap.to_broadcast([ap.shape[0], n])


def consts(nc, c):
    with Stage(nc) as st:
        filled = st.sem("filled")
        block = st.block()

        @block.gpsimd
        def _(pool):
            pool.memset(c.ident[:, :], 0.0)
            pool.memset(c.ones[:, :], 1.0)
            pool.memset(c.eps[:, :], EPS)
            pool.memset(c.one[:, :], 1.0)
            pool.memset(c.ones64[:, :], 1.0)
            pool.memset(c.ones32[:, :], 1.0)
            pool.memset(c.bound[:, :], 0.0)
            pool.memset(c.winmask[:, :], 0.0)
            pool.memset(c.sel[:, :, :], 0.0)
            pool.memset(c.selp[:, :, :], 0.0)
            pool.memset(c.chunkmask[:, :], 1.0)
            pool.memset(c.scanone[:, :], 1.0)
            pool.drain()
            pool.affine_select(out=c.ident[:, :], in_=c.ident[:, :], compare_op=ALU.not_equal, fill=1.0,
                               base=0, pattern=[[-1, P]], channel_multiplier=1)
            pool.affine_select(out=c.bound[:, :], in_=c.bound[:, :], compare_op=ALU.is_ge, fill=MASKED,
                               base=0, pattern=[[1, SEQ]], channel_multiplier=-1)
            pool.affine_select(out=c.winmask[:, :], in_=c.winmask[:, :], compare_op=ALU.is_gt, fill=MASKED,
                               base=0, pattern=[[1, P]], channel_multiplier=-1)
            pool.affine_select(out=c.sel[:, :, :], in_=c.sel[:, :, :], compare_op=ALU.not_equal, fill=1.0,
                               base=0, pattern=[[-1, 8], [0, P]], channel_multiplier=1)
            pool.affine_select(out=c.selp[:, :, :], in_=c.selp[:, :, :], compare_op=ALU.not_equal, fill=1.0,
                               base=0, pattern=[[-2, 4], [-1, 2], [0, 64]], channel_multiplier=1)
            m = c.chunkmask[:, :]
            pool.affine_select(out=m, in_=m, compare_op=ALU.is_ge, fill=0.0,
                               base=0, pattern=[[-32, 4], [0, 32]], channel_multiplier=1)
            v = c.scanone[:, :].rearrange("p (c t) -> p c t", t=32)
            pool.memset(v[:, :, 0:1], 0.0)
            for m, b in ((c.ones64, 64), (c.ones32, 32)):
                w = m[:, :]
                pool.affine_select(out=w, in_=w, compare_op=ALU.is_ge, fill=0.0,
                                   base=0, pattern=[[-b, P // b], [0, b]], channel_multiplier=1)
            pool.drain()
            m = c.chunkmask[:, :]
            pool.affine_select(out=m, in_=m, compare_op=ALU.is_ge, fill=0.0,
                               base=0, pattern=[[32, 4], [1, 32]], channel_multiplier=-1)
            for m, b in ((c.ones64, 64), (c.ones32, 32)):
                w = m[:, :]
                pool.affine_select(out=w, in_=w, compare_op=ALU.is_ge, fill=0.0,
                                   base=b - 1, pattern=[[b, P // b], [0, b]], channel_multiplier=-1)
            pool.drain()


def load_x(nc, c, x, within=None):
    with Stage(nc, within) as st:
        xin = st.sb("xin", [P, TT, D])
        x_loaded, turned = st.sem("x_loaded"), st.sem("turned")
        block = st.block()

        @block.sync
        def _(sp):
            sp.dma_start(xin[:, :, :], x[0].rearrange("(t p) d -> p t d", p=P)).then_inc(x_loaded, 16)

        @block.tensor
        def _(pe):
            pe.wait_ge(x_loaded, 16)
            for k in range(KD):
                for t in range(TT):
                    mm = pe.transpose(c.ps[:, k, t * P:(t + 1) * P], xin[:, t, k * P:(k + 1) * P], c.ident[:, :])
                mm.then_inc(turned, 1)

        @block.vector
        def _(dve):
            for k in range(KD):
                dve.wait_ge(turned, k + 1)
                dve.tensor_copy(c.x_T[:, k, :], c.ps[:, k, :])


def store_x(nc, c, out):
    with Stage(nc) as st:
        xo = st.sb("xo", [P, TT, D])
        turned, kept, written = st.sem("turned"), st.sem("kept"), st.sem("written")
        block = st.block()

        @block.tensor
        def _(pe):
            for t in range(TT):
                for k in range(KD):
                    mm = pe.transpose(c.ps[:, 2 * t + k // 4, (k % 4) * P:(k % 4 + 1) * P],
                                      c.x_T[:, k, t * P:(t + 1) * P], c.ident[:, :])
                mm.then_inc(turned, 1)

        @block.vector
        def _(dve):
            for t in range(TT):
                dve.wait_ge(turned, t + 1)
                dve.tensor_copy(xo[:, t, :], c.ps[:, 2 * t:2 * t + 2, :]).then_inc(kept, 1)

        @block.sync
        def _(sp):
            for t in range(TT):
                sp.wait_ge(kept, t + 1)
                sp.dma_start(out[0, t * P:(t + 1) * P, :], xo[:, t, :]).then_inc(written, 16)
            sp.wait_ge(written, 16 * TT)


def add_norm(nc, c, gain, src):
    with Stage(nc) as st:
        sq = st.sb("sq", [P, 2, SEQ])
        rstd = st.sb("rstd", [P, SEQ])
        g = st.sb("g", [P, KD])
        gain_loaded, squared, summed, rooted = (st.sem(n) for n in ("gain_loaded", "squared", "summed", "rooted"))
        scaled, used = st.sem("scaled"), st.sem("used")
        block = st.block()

        @block.sync
        def _(sp):
            with nc.allow_non_contiguous_dma(reason="a column of gains"):
                sp.dma_start(g[:, :], gain.rearrange("(k p) -> p k", p=P)).then_inc(gain_loaded, 16)

        @block.tensor
        def _(pe):
            for k in range(KD):
                pe.wait_ge(squared, k + 1)
                mm = pe.matmul(c.ps[:, 0, :], c.ones[:, :], sq[:, k % 2, :], start=(k == 0), stop=(k == KD - 1))
                mm.then_inc(used, 1)
            pe.drain().then_inc(summed, 1)

        @block.scalar
        def _(act):
            for k in range(KD):
                if k >= 2:
                    act.wait_ge(used, k - 1)
                act.activation(sq[:, k % 2, :], src[:, k, :], ACT.Square).then_inc(squared, 1)
            act.wait_ge(summed, 1)
            act.activation(rstd[:, :], c.ps[:, 0, :], ACT.Sqrt, scale=1.0 / D, bias=c.eps[:, :]).then_inc(rooted, 1)

        @block.vector
        def _(dve):
            dve.wait_ge(rooted, 1)
            dve.reciprocal(rstd[:, :], rstd[:, :])
            dve.drain()
            dve.wait_ge(gain_loaded, 16)
            for k in range(KD):
                dve.scalar_tensor_tensor(out=src[:, k, :], in0=src[:, k, :], scalar=g[:, k:k + 1], in1=rstd[:, :],
                                         op0=ALU.mult, op1=ALU.mult).then_inc(scaled, 1)
                if k % 2:
                    dve.drain()
                    dve.tensor_tensor(c.x_T[:, k - 1, :], c.x_T[:, k - 1, :], src[:, k - 1, :], ALU.add)

        @block.gpsimd
        def _(pool):
            for k in range(1, KD, 2):
                pool.wait_ge(scaled, k + 1)
                pool.tensor_tensor(c.x_T[:, k, :], c.x_T[:, k, :], src[:, k, :], ALU.add)


class Ring:

    def __init__(self, st, raw=None):
        self.raw = st.sb("raw", [P, 4, KD, P]) if raw is None else raw
        self.hi = st.sb("w_hi", [P, 4, KD, P], F32R)
        self.lo = st.sb("w_lo", [P, 4, KD, P], F32R)
        self.loaded = [st.sem(f"loaded{s}") for s in range(4)]
        self.halved = [st.sem(f"halved{s}") for s in range(4)]
        self.split = [st.sem(f"split{s}") for s in range(4)]
        self.used = [st.sem(f"used{s}") for s in range(4)]

    def load(self, sp, s, n, first, src):
        if not first:
            sp.wait_ge(self.split[s], n)
        sp.dma_start(self.raw[:, s, :, :], src).then_inc(self.loaded[s], 16)

    def high(self, dve, s, n, first):
        dve.wait_ge(self.loaded[s], 16 * n + 16)
        if not first:
            dve.wait_ge(self.used[s], n)
        dve.tensor_copy(self.hi[:, s, :, :], self.raw[:, s, :, :]).then_inc(self.halved[s], 1)

    def low(self, pool, s, n):
        pool.wait_ge(self.halved[s], n + 1)
        pool.tensor_tensor(self.lo[:, s, :, :], self.raw[:, s, :, :], self.hi[:, s, :, :].bitcast(F32), ALU.subtract)\
            .then_inc(self.split[s], 1)

    def passes(self, s, k):
        return ((self.hi[:, s, k, :], 0), (self.hi[:, s, k, :], 1), (self.lo[:, s, k, :], 0))


class NormInto:

    def __init__(self, st, nc, c, ring, gain):
        self.nc, self.c, self.gain = nc, c, gain
        self.g = st.sb("g", [P, KD])
        rstd = st.sb("rstd", [P, SEQ])
        self.rstd = rstd[:, :]
        self.now = ring.raw[:, 3, :, :].rearrange("p k n -> p (k n)").rearrange("p (b t) -> p b t", t=SEQ)
        self.sums = c.ps[:, 7, :]
        self.gain_loaded, self.squared, self.summed = st.sem("gain_loaded"), st.sem("squared"), st.sem("summed")
        self.summing = st.sem("summing")
        self.rooted, self.scaled, self.h_halved = st.sem("rooted"), st.sem("scaled"), st.sem("h_halved")
        self.low_even, self.low_odd = st.sem("low_even"), st.sem("low_odd")

    def load(self, sp):
        with self.nc.allow_non_contiguous_dma(reason="a column of gains"):
            sp.dma_start(self.g[:, :], self.gain.rearrange("(k p) -> p k", p=P)).then_inc(self.gain_loaded, 16)

    def squares(self, act):
        c = self.c
        for k in range(KD):
            if k >= 2:
                act.wait_ge(self.summing, k - 1)
            act.activation(self.now[:, k % 2, :], c.x_T[:, k, :], ACT.Square).then_inc(self.squared, 1)
        act.wait_ge(self.summed, 1)
        act.activation(self.rstd, self.sums, ACT.Sqrt, scale=1.0 / D, bias=c.eps[:, :]).then_inc(self.rooted, 1)
        for k in range(KD):
            act.wait_ge(self.scaled, k + 1)
            act.activation(c.h_hi[:, k, :], self.now[:, k % 2, :], ACT.Copy).then_inc(self.h_halved, 1)

    def sum(self, pe):
        for k in range(KD):
            pe.wait_ge(self.squared, k + 1)
            pe.matmul(self.sums, self.c.ones[:, :], self.now[:, k % 2, :], start=(k == 0), stop=(k == KD - 1))\
                .then_inc(self.summing, 1)
        pe.drain().then_inc(self.summed, 1)

    def scale(self, dve):
        c = self.c
        dve.wait_ge(self.rooted, 1)
        dve.reciprocal(self.rstd, self.rstd)
        dve.drain()
        dve.wait_ge(self.gain_loaded, 16)
        for k in range(KD):
            if k >= 3 and k % 2:
                dve.wait_ge(self.low_odd, (k - 1) // 2)
            if k and k % 2 == 0:
                dve.drain()
            dve.scalar_tensor_tensor(out=self.now[:, k % 2, :], in0=c.x_T[:, k, :], scalar=self.g[:, k:k + 1],
                                     in1=self.rstd, op0=ALU.mult, op1=ALU.mult).then_inc(self.scaled, 1)
            if k % 2:
                dve.wait_ge(self.h_halved, k)
                dve.tensor_tensor(c.h_lo[:, k - 1, :], self.now[:, 0, :], c.h_hi[:, k - 1, :].bitcast(F32), ALU.subtract)\
                    .then_inc(self.low_even, 1)

    def lows(self, pool):
        for k in range(1, KD, 2):
            pool.wait_ge(self.h_halved, k + 1)
            pool.tensor_tensor(self.c.h_lo[:, k, :], self.now[:, 1, :], self.c.h_hi[:, k, :].bitcast(F32), ALU.subtract)\
                .then_inc(self.low_odd, 1)

    def free(self, sp):
        sp.wait_ge(self.low_even, KD // 2)
        sp.wait_ge(self.low_odd, KD // 2)

    def wait(self, pe, k):
        pe.wait_ge(self.low_odd if k % 2 else self.low_even, k // 2 + 1)


def split_product(pe, ring, s, out, parts, norm=None):
    for k in range(KD):
        if norm is not None:
            norm.wait(pe, k)
        for i, (w, low) in enumerate(ring.passes(s, k)):
            mm = pe.matmul(out, w, parts[low][:, k, :], start=(k == 0 and i == 0), stop=(k == KD - 1 and i == 2))
    return mm


def gated_stage(nc, c, wa, wb, chunks, func, w_down=None, scale=None, raw=None, y=None, merged=None, accumulate=False,
                gain=None):
    with Stage(nc) as st:
        ring = Ring(st, raw)
        sg = st.sb("sg", [P, 2, SEQ])
        af = st.sb("af", [P, 2, SEQ])
        if w_down is not None:
            a_hi, a_lo = st.sb("a_hi", [P, chunks, SEQ], F32R), st.sb("a_lo", [P, chunks, SEQ], F32R)
            second = (c.h_hi, c.h_lo)
        else:
            second = (st.sb("y_hi", [P, KD, SEQ], F32R), st.sb("y_lo", [P, KD, SEQ], F32R))
        opened = [st.sem(f"opened{p}") for p in range(2)]
        gated = [st.sem(f"gated{p}") for p in range(2)]
        y_split, a_split = st.sem("y_split"), st.sem("a_split")
        norm = None if gain is None else NormInto(st, nc, c, ring, gain)
        block = st.block()
        a_v = wa.rearrange("(k p) f -> p k f", p=P)
        b_v = wb.rearrange("(k p) f -> p k f", p=P)
        N = chunks // 2

        tiles = ((0, a_v), (1, b_v)) if w_down is not None else ((1, b_v), (0, a_v))

        @block.sync
        def _(sp):
            def load(i, p, first):
                for e, v in tiles:
                    if first and 2 * p + e == 3 and norm is not None:
                        norm.free(sp)
                    ring.load(sp, 2 * p + e, i, first, v[:, :, bass.ds(i * (2 * P) + p * P, P)])

            if norm is not None:
                norm.load(sp)
            load(0, 0, True)
            load(0, 1, True)
            with sp.Fori(1, N) as i:
                load(i, 0, False)
                load(i, 1, False)
            if w_down is not None:
                with sp.Fori(0, N) as i:
                    for s in range(2):
                        ring.load(sp, s, N + i, False,
                                  w_down[bass.ds(i * (2 * P) + s * P, P), :].rearrange("p (k n) -> p k n", n=P))

        @block.gpsimd
        def _(pool):
            for s in range(4):
                if s == 2 and norm is not None:
                    norm.lows(pool)
                ring.low(pool, s, 0)
            with pool.Fori(1, N) as i:
                for s in range(4):
                    ring.low(pool, s, i)
            if w_down is not None:
                with pool.Fori(0, N) as i:
                    for s in range(2):
                        ring.low(pool, s, N + i)

        @block.tensor
        def _(pe):
            if norm is not None:
                norm.sum(pe)

            def products(i, p, first):
                pe.wait_ge(ring.split[2 * p], i + 1)
                if not first:
                    pe.wait_ge(gated[p], i)
                split_product(pe, ring, 2 * p, c.ps[:, p, :], (c.h_hi, c.h_lo),
                              norm if first and p == 0 else None).then_inc(ring.used[2 * p], 1)
                pe.wait_ge(ring.split[2 * p + 1], i + 1)
                if y is not None and first and p == 0:
                    pe.wait_ge(y_split, 1)
                split_product(pe, ring, 2 * p + 1, c.ps[:, 2 + p, :], second).then_inc(ring.used[2 * p + 1], 1)

            products(0, 0, True)
            products(0, 1, True)
            with pe.Fori(1, N) as i:
                products(i, 0, False)
                products(i, 1, False)
            if w_down is not None:
                def down(i, s, first, last):
                    pe.wait_ge(ring.split[s], N + 1 + i)
                    for m in range(KD):
                        for n, (w, low) in enumerate(ring.passes(s, m)):
                            mm = pe.matmul(c.ps[:, m, :], w, (a_hi, a_lo)[low][:, bass.ds(2 * i + s, 1), :],
                                           start=(first and n == 0), stop=(last and n == 2))
                    mm.then_inc(ring.used[s], 1)

                pe.wait_ge(a_split, chunks)
                down(0, 0, True, False)
                down(0, 1, False, False)
                with pe.Fori(1, N - 1) as i:
                    down(i, 0, False, False)
                    down(i, 1, False, False)
                down(N - 1, 0, False, False)
                down(N - 1, 1, False, True)

        @block.scalar
        def _(act):
            if norm is not None:
                norm.squares(act)

            def gate(i, p, first):
                act.wait_ge(ring.used[2 * p], i + 1)
                if not first:
                    act.wait_ge(gated[p], i)
                act.activation(sg[:, p, :], c.ps[:, p, :], func).then_inc(opened[p], 1)

            gate(0, 0, True)
            gate(0, 1, True)
            with act.Fori(1, N) as i:
                gate(i, 0, False)
                gate(i, 1, False)

        @block.vector
        def _(dve):
            def highs(i, p, first):
                ring.high(dve, 2 * p, i, first)
                ring.high(dve, 2 * p + 1, i, first)

            def finish(i, p):
                dve.wait_ge(opened[p], i + 1)
                dve.wait_ge(ring.used[2 * p + 1], i + 1)
                dve.tensor_tensor(af[:, p:p + 1, :], sg[:, p:p + 1, :], c.ps[:, 2 + p:3 + p, :], ALU.mult).then_inc(gated[p], 1)
                dve.drain()
                at = bass.ds(2 * i + p, 1)
                if w_down is not None:
                    dve.tensor_copy(a_hi[:, at, :], af[:, p:p + 1, :])
                    dve.drain()
                    dve.tensor_tensor(a_lo[:, at, :], af[:, p:p + 1, :], a_hi[:, at, :].bitcast(F32), ALU.subtract)\
                        .then_inc(a_split, 1)
                elif accumulate:
                    dve.tensor_tensor(merged[:, at, :], merged[:, at, :], af[:, p:p + 1, :], ALU.add)
                else:
                    dve.tensor_copy(merged[:, at, :], af[:, p:p + 1, :])
                dve.drain()

            highs(0, 0, True)
            if y is not None:
                dve.tensor_copy(second[0][:, :, :], y[:, :, :])
                dve.drain()
                dve.tensor_tensor(second[1][:, :, :], y[:, :, :], second[0][:, :, :].bitcast(F32), ALU.subtract)\
                    .then_inc(y_split, 1)
            if norm is not None:
                norm.scale(dve)
            highs(0, 1, True)
            finish(0, 0)
            with dve.Fori(1, N) as i:
                highs(i, 0, False)
                finish(i - 1, 1)
                highs(i, 1, False)
                finish(i, 0)
            if w_down is None:
                finish(N - 1, 1)
            else:
                for s in range(2):
                    ring.high(dve, s, N, False)
                finish(N - 1, 1)
                with dve.Fori(1, N) as i:
                    for s in range(2):
                        ring.high(dve, s, N + i, False)
                dve.wait_ge(ring.used[1], 2 * N)
                for m in range(KD):
                    if raw is None:
                        dve.scalar_tensor_tensor(out=c.x_T[:, m, :], in0=c.ps[:, m, :], scalar=scale, in1=c.x_T[:, m, :],
                                                 op0=ALU.mult, op1=ALU.add)
                    else:
                        dve.tensor_copy(feature_major(raw)[:, m, :], c.ps[:, m, :])


def feature_major(raw):
    return raw[:, :, :, :].rearrange("p s k n -> p (s k n)").rearrange("p (k t) -> p k t", t=SEQ)


def ffn(nc, c, gain, w_gate, w_up, w_down, scale, raw=None):
    gated_stage(nc, c, w_gate, w_up, KF, ACT.Silu, w_down=w_down, scale=scale, raw=raw, gain=gain)


class Shared:

    def __init__(self, nc, ctx):
        def sb(name, shape, dtype=F32):
            return ctx.enter_context(nc.sbuf_tensor(name, shape, dtype))
        self.ps = ctx.enter_context(nc.psum_tensor("ps", [P, 8, BANK], F32))
        self.x_T = sb("x_T", [P, KD, SEQ])
        self.h_hi = sb("h_hi", [P, KD, SEQ], F32R)
        self.h_lo = sb("h_lo", [P, KD, SEQ], F32R)
        self.ident = sb("ident", [P, P])
        self.ones = sb("ones", [P, P])
        self.ones64 = sb("ones64", [P, P])
        self.ones32 = sb("ones32", [P, P])
        self.bound = sb("bound", [P, SEQ])
        self.winmask = sb("winmask", [P, P])
        self.sel = sb("sel", [8, 8, P])
        self.selp = sb("selp", [8, 4, P])
        self.chunkmask = sb("chunkmask", [P, P])
        self.scanone = sb("scanone", [P, SEQ])
        self.eps = sb("eps", [P, 1])
        self.one = sb("one", [P, 1])
        self.lam_init = sb("lam_init", [P, LAYERS])


def project(nc, c, w, runs, rows_to, tokens_to, params=(), gain=None):
    with Stage(nc) as st:
        ring = Ring(st)
        kept = [st.sem(f"kept{s}") for s in range(4)]
        param_loaded = st.sem("param_loaded")
        norm = None if gain is None else NormInto(st, nc, c, ring, gain)
        block = st.block()
        view = w.rearrange("(k p) f -> p k f", p=P)
        singles = [("token", *t) for t in tokens_to for _ in range(2)] + [("row", *r) for r in rows_to]
        n_pairs = sum(chunks for _, chunks, _ in runs) // 2

        def each_tile(eng, body):
            base = 0
            for col0, chunks, dst in runs:
                n = chunks // 2

                def pair(j, p, idx, first):
                    for e in range(2):
                        body(2 * p + e, idx, first, "chunk", j * (2 * P) + (col0 + e * P), P, dst, 2 * j + e)

                if base % 2 == 0 and n % 2 == 0 and n >= 6:
                    start = 0
                    if base == 0:
                        pair(0, 0, 0, True)
                        pair(1, 1, 0, True)
                        start = 1
                    with eng.Fori(start, n // 2) as i:
                        pair(2 * i, 0, base // 2 + i, False)
                        pair(2 * i + 1, 1, base // 2 + i, False)
                else:
                    for j in range(n):
                        pair(j, (base + j) % 2, (base + j) // 2, base + j < 2)
                base += n
            for q, (kind, col0, m, dst) in enumerate(singles):
                n = base + q // 2
                body(2 * (n % 2) + q % 2, n // 2, n < 2, kind, col0 + (P if kind == "token" and q % 2 else 0), m, dst, 0)

        @block.sync
        def _(sp):
            if norm is not None:
                norm.load(sp)
            def load(s, n, first, kind, col, m, dst, j):
                if norm is not None and first and s == 3:
                    norm.free(sp)
                ring.load(sp, s, n, first, view[:, :, bass.ds(col, P)])

            each_tile(sp, load)
            with nc.allow_non_contiguous_dma(reason="columns of parameters"):
                for dst, src in params:
                    sp.dma_start(dst, src).then_inc(param_loaded, 16)
            if params:
                sp.wait_ge(param_loaded, 16 * len(params))

        @block.vector
        def _(dve):
            def high(s, n, first, kind, col, m, dst, j):
                if norm is not None and first and s == 2:
                    norm.scale(dve)
                ring.high(dve, s, n, first)

            each_tile(dve, high)

        @block.gpsimd
        def _(pool):
            def low(s, n, first, kind, col, m, dst, j):
                if norm is not None and first and s == 2:
                    norm.lows(pool)
                ring.low(pool, s, n)

            each_tile(pool, low)

        @block.tensor
        def _(pe):
            def product(s, n, first, kind, col, m, dst, j):
                pe.wait_ge(ring.split[s], n + 1)
                if not first:
                    pe.wait_ge(kept[s], n)
                parts = (c.h_hi, c.h_lo)
                if kind != "token":
                    split_product(pe, ring, s, c.ps[:, s, :], parts, norm if first and s == 0 else None)\
                        .then_inc(ring.used[s], 1)
                elif s % 2:
                    for t in range(TT):
                        for k in range(KD):
                            for i, (w, low) in enumerate(((ring.hi, 0), (ring.hi, 1), (ring.lo, 0))):
                                mm = pe.matmul(c.ps[:, s - 1 + t // 2, (t % 2) * 2 * P:(t % 2 + 1) * 2 * P],
                                               parts[low][:, k, t * P:(t + 1) * P], w[:, s - 1:s + 1, k, :],
                                               start=(k == 0 and i == 0), stop=(k == KD - 1 and i == 2))
                    mm.then_inc(ring.used[s - 1], 1)
                    pe.drain().then_inc(ring.used[s], 1)

            if norm is not None:
                norm.sum(pe)
            each_tile(pe, product)

        @block.scalar
        def _(act):
            def keep(s, n, first, kind, col, m, dst, j):
                act.wait_ge(ring.used[s], n + 1)
                if kind == "chunk":
                    ins = act.activation(dst[:, bass.ds(j, 1), :], c.ps[:, s:s + 1, :], ACT.Copy)
                elif kind == "row":
                    ins = act.activation(dst, c.ps[0:m, s, :], ACT.Copy)
                else:
                    e = s % 2
                    ins = act.activation(dst[:, 2 * e:2 * e + 2, :],
                                         c.ps[:, s, :].rearrange("p (t n) -> p t n", n=2 * P)[:, :, 0:m], ACT.Copy)
                ins.then_inc(kept[s], 1)

            if norm is not None:
                norm.squares(act)
            each_tile(act, keep)


M_HEADS, M_DIM = 4, 64
S_HEADS, S_DIM = 8, 64
DF_HEADS, DF_QK, DF_V = 4, 32, 64


class Mixer:

    def __init__(self, nc, ctx, y_T):
        def sb(name, shape):
            return ctx.enter_context(nc.sbuf_tensor(f"{name}_{nc.next_id()}", shape, F32))
        self.y_T = y_T
        self.mqk = sb("mqk", [P, 4, SEQ])
        self.mo = sb("mo", [P, 2, SEQ])
        self.mv = sb("mv", [P, TT, 2 * P])
        self.gi = sb("gi", [M_HEADS, SEQ])
        self.gf = sb("gf", [M_HEADS, SEQ])
        self.zxbc = sb("zxbc", [P, 12, SEQ])
        self.z = self.zxbc[:, 0:4, :]
        self.xbc = self.zxbc[:, 4:12, :]
        self.dt = sb("dt", [S_HEADS, SEQ])
        self.dqk = sb("dqk", [P, 4, SEQ])
        self.dv = sb("dv", [P, TT, 2 * P])
        self.g_bias = sb("g_bias", [M_HEADS, 2])
        self.m_gain = sb("m_gain", [P, 2])
        self.conv_w = sb("conv_w", [P, 8, 4])
        self.conv_b = sb("conv_b", [P, 8])
        self.dt_bias = sb("dt_bias", [S_HEADS, 1])
        self.a_log = sb("a_log", [S_HEADS, 1])
        self.d_skip = sb("d_skip", [P, 4])
        self.s_gain = sb("s_gain", [P, 4])
        self.q_gain = sb("q_gain", [P, 1])
        self.k_gain = sb("k_gain", [P, 1])
        self.lam4 = sb("lam4", [P, 4, DF_QK])
        self.sub_gain = sb("sub_gain", [P, 1])


def gates(nc, c, m, rows, cols, within):
    acs, negM, negm = rows
    with Stage(nc, within) as st:
        x8, e8, l8, dA, nacs = (st.sb(n, [8, SEQ]) for n in ("x8", "e8", "l8", "dA", "nacs"))
        x4, e4, l4, B, g, M, s4 = (st.sb(n, [4, SEQ]) for n in ("x4", "e4", "l4", "B", "g", "M", "s4"))
        ones8 = st.sb("ones8", [8, SEQ])
        a8 = st.sb("a8", [8, 1])
        biased, logged, rowed, turned = st.sem("biased"), st.sem("logged"), st.sem("rowed"), st.sem("turned")
        block = st.block()

        @block.scalar
        def _(act):
            act.activation(a8[:, :], m.a_log[:, :], ACT.Exp)
            act.wait_ge(biased, 1)
            act.activation(e8[:, :], x8[:, :], ACT.Abs)
            act.activation(e4[:, :], x4[:, :], ACT.Abs)
            act.drain()
            act.activation(e8[:, :], e8[:, :], ACT.Exp, scale=-1.0)
            act.activation(e4[:, :], e4[:, :], ACT.Exp, scale=-1.0)
            act.drain()
            act.activation(l8[:, :], e8[:, :], ACT.Ln, bias=c.one[0:8, :])
            act.activation(l4[:, :], e4[:, :], ACT.Ln, bias=c.one[0:4, :])
            act.drain().then_inc(logged, 1)

        @block.vector
        def _(dve):
            dve.memset(ones8[:, :], 1.0)
            dve.tensor_scalar(x8[:, :], m.dt[:, :], m.dt_bias[:, :], None, ALU.add)
            dve.tensor_scalar(x4[:, :], m.gf[:, :], m.g_bias[:, 1:2], None, ALU.add)
            dve.drain().then_inc(biased, 1)

    def rest():
        @block.vector
        def _(dve):
            dve.wait_ge(logged, 1)
            dve.scalar_tensor_tensor(out=m.dt[:, :], in0=x8[:, :], scalar=0.0, in1=l8[:, :], op0=ALU.max, op1=ALU.add)
            dve.scalar_tensor_tensor(out=s4[:, :], in0=x4[:, :], scalar=0.0, in1=l4[:, :], op0=ALU.min, op1=ALU.subtract)
            dve.drain()
            dve.tensor_scalar(dA[:, :], m.dt[:, :], a8[:, 0:1], -1.0, ALU.mult, ALU.mult)
            dve.tensor_tensor_scan(B[:, :], ones8[0:4, :], s4[:, :], 0.0, ALU.mult, ALU.add)
            dve.drain()
            dve.tensor_tensor_scan(acs[:, :], ones8[:, :], dA[:, :], 0.0, ALU.mult, ALU.add)
            dve.scalar_tensor_tensor(out=g[:, :], in0=m.gi[:, :], scalar=m.g_bias[:, 0:1], in1=B[:, :],
                                     op0=ALU.add, op1=ALU.subtract)
            dve.drain()
            dve.tensor_scalar(nacs[:, :], acs[:, :], -1.0, None, ALU.mult)
            dve.tensor_tensor_scan(M[:, :], g[:, :], g[:, :], 0.0, ALU.max, ALU.max)
            dve.drain()
            dve.tensor_scalar(negM[:, :], M[:, :], -1.0, None, ALU.mult)
            dve.scalar_tensor_tensor(out=negm[:, :], in0=M[:, :], scalar=-1.0, in1=B[:, :], op0=ALU.mult, op1=ALU.subtract)
            dve.drain().then_inc(rowed, 1)
            dve.wait_ge(turned, 1)
            dve.tensor_copy(cols[:, :, :], c.ps[:, 4, 0:TT * 32].rearrange("p (t n) -> p t n", n=32)[:, :, 0:20])

        @block.tensor
        def _(pe):
            pe.wait_ge(rowed, 1)
            for t in range(TT):
                at = t * P
                for off, src, n in ((0, g, 4), (4, nacs, 8), (12, m.dt, 8)):
                    mm = pe.transpose(c.ps[:, 4, 32 * t + off:32 * t + off + n], src[:, at:at + P], c.ident[0:n, 0:n])
            mm.then_inc(turned, 1)

    return rest


def conv(nc, c, m, xdt, cols, within):
    with Stage(nc, within) as st:
        y = m.y_T
        convolved, silued, turned = st.sem("convolved"), st.sem("silued"), st.sem("turned")
        block = st.block()

        @block.vector
        def _(dve):
            for k in range(8):
                dve.tensor_scalar(y[:, k, :], m.xbc[:, k, :], m.conv_w[:, k, 3:4], None, ALU.mult)
            for s in range(1, 4):
                dve.drain()
                for k in range(8):
                    ins = dve.scalar_tensor_tensor(out=y[:, k, s:], in0=m.xbc[:, k, 0:SEQ - s],
                                                   scalar=m.conv_w[:, k, 3 - s:4 - s], in1=y[:, k, s:],
                                                   op0=ALU.mult, op1=ALU.add)
                    if s == 3:
                        ins.then_inc(convolved, 1)

    def rest():
        @block.vector
        def _(dve):
            dve.drain()
            for t in range(TT):
                dve.wait_ge(turned, t + 1)
                dve.tensor_tensor(xdt[:, t, :].rearrange("p (h d) -> p h d", d=S_DIM),
                                  c.ps[:, t, :].rearrange("p (h d) -> p h d", d=S_DIM),
                                  cols[:, t, 12:20].rearrange("p (h o) -> p h o", o=1).to_broadcast([P, S_HEADS, S_DIM]),
                                  ALU.mult)

        @block.scalar
        def _(act):
            for k in range(8):
                act.wait_ge(convolved, k + 1)
                if k == 0:
                    act.wait_ge(convolved, 8)
                act.activation(m.xbc[:, k, :], y[:, k, :], ACT.Silu, bias=m.conv_b[:, k:k + 1]).then_inc(silued, 1)

        @block.tensor
        def _(pe):
            pe.wait_ge(silued, 4)
            for t in range(TT):
                for k in range(4):
                    mm = pe.transpose(c.ps[:, t, k * P:(k + 1) * P], m.xbc[:, k, t * P:(t + 1) * P], c.ident[:, :])
                mm.then_inc(turned, 1)

    return rest


def recurrences(nc, c, m, rows, cols, xdt, y_ssm, num, den):
    acs, negM, negm = rows
    units = [("ssm", h) for h in range(S_HEADS)] + [("mlstm", h) for h in range(M_HEADS)]
    score_of, scores = [], []
    for kind, h in units:
        key = (kind, h // 4 if kind == "ssm" else h)
        if key not in scores:
            scores.append(key)
        score_of.append(scores.index(key))
    last_use = {n: max(u for u, k in enumerate(score_of) if k == n) for n in range(len(scores))}
    with Stage(nc) as st:
        arg = st.sb("arg", [P, 3, TRI])
        wgt = st.sb("wgt", [P, 2, TRI])
        vone = m.y_T[:, 0:TT, :].rearrange("p t (h n) -> p t h n", n=P)
        v_ready, row_sent, arged, exped = (st.sem(n) for n in ("v_ready", "row_sent", "arged", "exped"))
        scored, weighted, outed, kept = (st.sem(n) for n in ("scored", "weighted", "outed", "kept"))
        block = st.block()
        ROW, OUT = 6, 7

        def tri(buf, j):
            return c.ps[:, 3 * buf + TRI_AT[j] // BANK, TRI_AT[j] % BANK:TRI_AT[j] % BANK + TRI_W[j]]

        @block.tensor
        def _(pe):
            def row(u):
                kind, h = units[u]
                if u >= 1:
                    pe.wait_ge(arged, u)
                n, src = (8, acs) if kind == "ssm" else (4, negM)
                pe.matmul(c.ps[:, ROW, :], c.sel[0:n, h, :], src[:, :], start=True, stop=True).then_inc(row_sent, 1)
                k = score_of[u]
                if u and score_of[u - 1] == k:
                    return
                if k >= 2:
                    pe.wait_ge(weighted, last_use[k - 2] + 1)
                for j in range(TT):
                    if kind == "ssm":
                        key, query = m.xbc[:, 4 + h // 4, j * P:(j + 1) * P], m.xbc[:, 6 + h // 4, j * P:]
                    else:
                        b = 64 * (h % 2)
                        key, query = m.mqk[b:b + 64, 2 + h // 2, j * P:(j + 1) * P], m.mqk[b:b + 64, h // 2, j * P:]
                    mm = pe.matmul(tri(k % 2, j), key, query, start=True, stop=True)
                mm.then_inc(scored, 1)

            def out(u):
                kind, h = units[u]
                pe.wait_ge(weighted, u + 1)
                if u >= 1:
                    pe.wait_ge(kept, u)
                if u == 8:
                    pe.wait_ge(v_ready, 1)
                b = 64 * (h % 2)
                for j in range(TT):
                    if kind == "ssm":
                        v, to = xdt[:, j, h * 64:(h + 1) * 64], c.ps[b:b + 64, OUT, j * P:]
                    else:
                        v, to = vone[:, j, h, :], c.ps[:, OUT, j * P:]
                    mm = pe.matmul(to, v, wgt[:, u % 2, TRI_AT[j]:TRI_AT[j] + TRI_W[j]], start=(j == 0), stop=(j == TT - 1))
                mm.then_inc(outed, 1)

            row(0)
            row(1)
            for u in range(len(units)):
                if u + 2 < len(units):
                    row(u + 2)
                out(u)

        @block.vector
        def _(dve):
            dve.memset(vone[:, :, :, 64:P], 1.0)
            dve.tensor_copy(vone[:, :, :, 0:64], m.mv[:, :, :].rearrange("p t (h d) -> p t h d", d=64)).then_inc(v_ready, 1)

            def args(u):
                kind, h = units[u]
                dve.wait_ge(row_sent, u + 1)
                for j in range(TT):
                    col = cols[:, j, 4 + h:5 + h] if kind == "ssm" else cols[:, j, h:h + 1]
                    ins = dve.scalar_tensor_tensor(out=arg[:, u % 3, TRI_AT[j]:TRI_AT[j] + TRI_W[j]],
                                                   in0=c.ps[:, ROW, j * P:], scalar=col, in1=c.bound[:, 0:TRI_W[j]],
                                                   op0=ALU.add, op1=ALU.min)
                ins.then_inc(arged, 1)

            def weigh(u):
                kind, h = units[u]
                dve.wait_ge(exped, u + 1)
                dve.wait_ge(scored, score_of[u] + 1)
                if u >= 2:
                    dve.wait_ge(outed, u - 1)
                k = score_of[u] % 2
                dve.scalar_tensor_tensor(
                    out=wgt[:, u % 2, :], in0=c.ps[:, 3 * k:3 * k + 3, :].rearrange("p b n -> p (b n)")[:, 0:TRI],
                    scalar=(1.0 if kind == "ssm" else M_DIM ** -0.5), in1=arg[:, u % 3, :],
                    op0=ALU.mult, op1=ALU.mult).then_inc(weighted, 1)

            args(0)
            args(1)
            for u in range(len(units)):
                weigh(u)
                if u + 2 < len(units):
                    args(u + 2)

        @block.scalar
        def _(act):
            def exps(u):
                act.wait_ge(arged, u + 1)
                act.activation(arg[:, u % 3, :], arg[:, u % 3, :], ACT.Exp).then_inc(exped, 1)

            exps(0)
            exps(1)
            for u, (kind, h) in enumerate(units):
                act.wait_ge(outed, u + 1)
                b = 64 * (h % 2)
                if kind == "ssm":
                    act.activation(y_ssm[b:b + 64, h // 2, :], c.ps[b:b + 64, OUT, :], ACT.Copy).then_inc(kept, 1)
                else:
                    act.activation(num[b:b + 64, h // 2, :], c.ps[0:64, OUT, :], ACT.Copy)
                    act.activation(den[b:b + 64, h // 2, :], c.ps[64:P, OUT, :], ACT.Copy).then_inc(kept, 1)
                if u + 2 < len(units):
                    exps(u + 2)


def finish_first_mixer(nc, c, m, rows, y_ssm, num, den, lam, o_T):
    acs, negM, negm = rows
    with Stage(nc) as st:
        floor = st.sb("floor", [P, 2, SEQ])
        sq = st.sb("sq", [P, 8, SEQ])
        rstd = st.sb("rstd", [P, 6, SEQ])
        row_sent, exped, y_ready, squared, summed, rooted, sigmoided, zed, normed = (
            st.sem(n) for n in ("row_sent", "exped", "y_ready", "squared", "summed", "rooted", "sigmoided", "zed", "normed"))
        block = st.block()

        @block.tensor
        def _(pe):
            for p in range(2):
                mm = pe.matmul(c.ps[:, p, :], c.selp[0:4, p, :], negm[:, :], start=True, stop=True)
            mm.then_inc(row_sent, 1)
            pe.wait_ge(squared, 1)
            for k in range(2):
                mm = pe.matmul(c.ps[:, 6 + k, :], c.ones64[:, :], sq[:, 6 + k, :], start=True, stop=True)
            mm.then_inc(summed, 1)
            pe.wait_ge(squared, 2)
            for g in range(2):
                for k in range(2):
                    mm = pe.matmul(c.ps[:, 2 + g, :], c.ones[:, :], sq[:, 2 * g + k, :], start=(k == 0), stop=(k == 1))
            mm.then_inc(summed, 1)
            pe.wait_ge(squared, 3)
            for p in range(2):
                mm = pe.matmul(c.ps[:, 4 + p, :], c.ones64[:, :], sq[:, 4 + p, :], start=True, stop=True)
            mm.then_inc(summed, 1)

        @block.scalar
        def _(act):
            act.activation(sq[:, 6:8, :], o_T[:, :, :], ACT.Square).then_inc(squared, 1)
            act.activation(m.z[:, :, :], m.z[:, :, :], ACT.Silu).then_inc(zed, 1)
            act.activation(m.mo[:, :, :], m.mo[:, :, :], ACT.Sigmoid).then_inc(sigmoided, 1)
            act.activation(den[:, :, :], den[:, :, :], ACT.Abs)
            act.wait_ge(row_sent, 1)
            act.activation(floor[:, :, :], c.ps[:, 0:2, :], ACT.Exp)
            act.drain().then_inc(exped, 1)
            act.wait_ge(summed, 1)
            act.activation(rstd[:, 4:6, :], c.ps[:, 6:8, :], ACT.Sqrt, scale=1.0 / DF_V, bias=c.eps[:, :]).then_inc(rooted, 1)
            act.wait_ge(y_ready, 1)
            act.activation(sq[:, 0:4, :], y_ssm[:, :, :], ACT.Square).then_inc(squared, 1)
            act.wait_ge(summed, 2)
            act.activation(rstd[:, 0:2, :], c.ps[:, 2:4, :], ACT.Sqrt, scale=1.0 / 256, bias=c.eps[:, :]).then_inc(rooted, 1)
            act.wait_ge(y_ready, 2)
            act.activation(sq[:, 4:6, :], num[:, :, :], ACT.Square).then_inc(squared, 1)
            act.wait_ge(summed, 3)
            act.activation(rstd[:, 2:4, :], c.ps[:, 4:6, :], ACT.Sqrt, scale=1.0 / 64, bias=c.eps[:, :]).then_inc(rooted, 1)

        @block.gpsimd
        def _(pool):
            pool.wait_ge(sigmoided, 1)
            for p in range(2):
                pool.wait_ge(normed, p + 1)
                pool.tensor_tensor(m.y_T[:, p, :], num[:, p, :], m.mo[:, p, :], ALU.mult)

        @block.vector
        def _(dve):
            for k in range(4):
                dve.scalar_tensor_tensor(out=y_ssm[:, k, :], in0=m.xbc[:, k, :], scalar=m.d_skip[:, k:k + 1],
                                         in1=y_ssm[:, k, :], op0=ALU.mult, op1=ALU.add)
            dve.drain()
            dve.wait_ge(zed, 1)
            dve.tensor_tensor(y_ssm[:, :, :], y_ssm[:, :, :], m.z[:, :, :], ALU.mult).then_inc(y_ready, 1)
            dve.wait_ge(exped, 1)
            dve.tensor_tensor(den[:, :, :], den[:, :, :], floor[:, :, :], ALU.max)
            dve.drain()
            dve.reciprocal(den[:, :, :], den[:, :, :])
            dve.drain()
            dve.tensor_tensor(num[:, :, :], num[:, :, :], den[:, :, :], ALU.mult).then_inc(y_ready, 1)

            def divide(count, at):
                dve.wait_ge(rooted, count)
                dve.reciprocal(rstd[:, at:at + 2, :], rstd[:, at:at + 2, :])
                dve.drain()

            divide(1, 4)
            for k in range(2):
                dve.scalar_tensor_tensor(out=m.y_T[:, 6 + k, :], in0=o_T[:, k, :], scalar=lam[:, 1:2],
                                         in1=rstd[:, 4 + k, :], op0=ALU.mult, op1=ALU.mult)
            divide(2, 0)
            for k in range(4):
                dve.scalar_tensor_tensor(out=m.y_T[:, 2 + k, :], in0=y_ssm[:, k, :], scalar=m.s_gain[:, k:k + 1],
                                         in1=rstd[:, k // 2, :], op0=ALU.mult, op1=ALU.mult)
            divide(3, 2)
            for p in range(2):
                dve.scalar_tensor_tensor(out=num[:, p, :], in0=num[:, p, :], scalar=m.m_gain[:, p:p + 1],
                                         in1=rstd[:, 2 + p, :], op0=ALU.mult, op1=ALU.mult).then_inc(normed, 1)


def bias_rows(nc, c, table, heads, scratch, within=None):
    edges = bucket_edges()
    with Stage(nc, within) as st:
        tab = st.sb("tab", [heads, 32])
        f = st.sb("f", [heads, BACK + SEQ])
        loaded, laid, written = st.sem("loaded"), st.sem("laid"), st.sem("written")
        block = st.block()

        @block.sync
        def _(sp):
            with nc.allow_non_contiguous_dma(reason="a small table, turned"):
                sp.dma_start(tab[:, :], table.rearrange("b h -> h b")).then_inc(loaded, 16)
            sp.wait_ge(laid, 1)
            sp.dma_start(scratch[:, :], f[:, :]).then_inc(written, 16)
            sp.wait_ge(written, 16)

        @block.vector
        def _(dve):
            dve.memset(f[:, 0:BACK], MASKED)
            dve.wait_ge(loaded, 16)
            dve.tensor_copy(f[:, BACK:BACK + 16], tab[:, 0:16])
            for b in range(16, 32):
                lo, hi = edges[b], edges[b + 1]
                if lo < hi:
                    dve.tensor_copy(f[:, BACK + lo:BACK + hi], tab[:, b:b + 1].to_broadcast([heads, hi - lo]))
            dve.drain().then_inc(laid, 1)


def bucket_edges():
    n = np.arange(SEQ)
    nf = np.maximum(n, 16).astype(np.float32)
    large = 16 + (np.log(nf / np.float32(16)) / np.float32(np.log(8.0)) * np.float32(16)).astype(np.int32)
    bucket = np.where(n < 16, n, np.minimum(large, 31))
    return {b: int(np.argmax(bucket >= b)) for b in range(16, 32)} | {32: SEQ}


BACK = P


def bias_tiles(nc, c, scratch, heads, tiles, times, within=None, turned=None):
    with Stage(nc, within) as st:
        turned = st.sb("turned", [P, 2, SEQ]) if turned is None else turned
        loaded, used = [st.sem(f"loaded{s}") for s in range(2)], st.sem("used")
        block = st.block()

        @block.sync
        def _(sp):
            for h in range(heads):
                if h >= 2:
                    sp.wait_ge(used, h - 1)
                src = scratch[h, BACK - 127:BACK - 127 + SEQ]
                sp.dma_start(turned[:, h % 2, :], bass.AP(tensor=src.tensor, offset=src.offset, ap=[[1, P], [1, SEQ]]))\
                    .then_inc(loaded[h % 2], 16)

        @block.vector
        def _(dve):
            for h in range(heads):
                dve.wait_ge(loaded[h % 2], 16 * (h // 2) + 16)
                dve.tensor_scalar(tiles[:, h, :], turned[:, h % 2, ::-1], times, None, ALU.mult).then_inc(used, 1)


def first_mixer_projections(nc, c, m, L, w, gain):
    FM = [(1032, 12, m.zxbc[:, :, :]), (0, 4, m.mqk[:, :, :]), (2576, 4, m.dqk[:, :, :]), (768, 2, m.mo[:, :, :])]
    rows = [(1024, 4, m.gi[:, :]), (1028, 4, m.gf[:, :]), (2568, 8, m.dt[:, :])]
    tokens = [(512, 2 * P, m.mv[:, :, :]), (3088, 2 * P, m.dv[:, :, :])]

    def col(ap):
        return ap.rearrange("(p o) -> p o", o=1)

    params = [
        (m.g_bias[:, :], L["mlstm_gate_bias"].rearrange("g h -> h g")),
        (m.m_gain[:, :], L["mlstm_norm_w"].rearrange("(k p) -> p k", p=P)),
        (m.conv_b[:, :], L["ssm_conv_b"].rearrange("(k p) -> p k", p=P)),
        (m.dt_bias[:, :], col(L["ssm_dt_bias"])),
        (m.a_log[:, :], col(L["ssm_A_log"])),
        (m.s_gain[:, :], L["ssm_norm_w"].rearrange("(k p) -> p k", p=P)),
        (m.sub_gain[0:64, :], col(L["diff_subln_w"])),
        (m.sub_gain[64:P, :], col(L["diff_subln_w"])),
        (m.lam4[:, :, :], L["diff_lambda"].rearrange("(o a) d -> o a d", o=1).to_broadcast([P, 4, DF_QK])),
    ]
    for k in range(8):
        params.append((m.conv_w[:, k, :], L["ssm_conv_w"][:, k * P:(k + 1) * P].rearrange("t p -> p t")))
    for half in range(2):
        b = 64 * half
        for name, dst in (("diff_q_norm_w", m.q_gain), ("diff_k_norm_w", m.k_gain)):
            params.append((dst[b:b + 64, :], L[name].rearrange("i (d o) -> (i d) o", o=1)))
        src = L["ssm_D"].rearrange("(k e o) -> e o k", e=2, o=1)
        params.append((m.d_skip[b:b + 64, :], src[half].to_broadcast([64, 4])))
    project(nc, c, w, FM, rows, tokens, params, gain)


def diff_prepare(nc, c, m, lam, lam_init, sq, rstd, within):
    with Stage(nc, within) as st:
        prod = st.sb("prod", [P, 2, DF_QK])
        dots = st.sb("dots", [P, 2])
        squared, summed, rooted, dotted, exped = (st.sem(n) for n in ("squared", "summed", "rooted", "dotted", "exped"))
        block = st.block()

        @block.scalar
        def _(act):
            act.activation(sq[:, :, :], m.dqk[:, :, :], ACT.Square).then_inc(squared, 1)
            act.wait_ge(dotted, 1)
            act.activation(dots[:, :], dots[:, :], ACT.Exp).then_inc(exped, 1)
            act.wait_ge(summed, 1)
            act.activation(rstd[:, :, :], c.ps[:, 4:8, :], ACT.Sqrt, scale=1.0 / DF_QK, bias=c.eps[:, :]).then_inc(rooted, 1)

        @block.tensor
        def _(pe):
            pe.wait_ge(squared, 1)
            for k in range(4):
                mm = pe.matmul(c.ps[:, 4 + k, :], c.ones32[:, :], sq[:, k, :], start=True, stop=True)
            mm.then_inc(summed, 1)

        @block.vector
        def _(dve):
            dve.tensor_tensor(prod[:, :, :], m.lam4[:, 0:4:2, :], m.lam4[:, 1:4:2, :], ALU.mult)
            dve.drain()
            dve.reduce_sum(dots[:, :], prod[:, :, :], AX).then_inc(dotted, 1)
            dve.wait_ge(exped, 1)
            dve.scalar_tensor_tensor(out=lam[:, 0:1], in0=dots[:, 1:2], scalar=dots[:, 0:1], in1=lam_init,
                                     op0=ALU.subtract, op1=ALU.subtract)
            dve.tensor_scalar(lam[:, 1:2], lam_init, -1.0, 1.0, ALU.mult, ALU.add)
            dve.drain()
            dve.tensor_tensor(lam[:, 1:2], lam[:, 1:2], m.sub_gain[:, :], ALU.mult)
            dve.tensor_scalar(m.q_gain[:, :], m.q_gain[:, :], DF_QK ** -0.5, None, ALU.mult)
            dve.wait_ge(rooted, 1)
            dve.reciprocal(rstd[:, :, :], rstd[:, :, :])
            dve.drain()
            for k in range(4):
                gain = m.q_gain if k < 2 else m.k_gain
                dve.scalar_tensor_tensor(out=m.dqk[:, k, :], in0=m.dqk[:, k, :], scalar=gain[:, 0:1], in1=rstd[:, k, :],
                                         op0=ALU.mult, op1=ALU.mult)


def diff_attention(nc, c, m, tiles, lam, o_T):
    units = [(h, qi) for h in range(DF_HEADS) for qi in range(TT)]
    U = len(units)
    with Stage(nc) as st:
        neg = st.sb("neg", [P, 3, 2, SEQ])
        prob = st.sb("prob", [P, 2, SEQ])
        prob_T = st.sb("prob_T", [P, 2, TT, SEQ])
        nmax = st.sb("nmax", [P, 3, 2])
        total = st.sb("total", [P, 3, 2])
        recip = st.sb("recip", [P, 3, 2])
        scored, biased, exped, mixed, turned, laid, outed, kept = (
            st.sem(n) for n in ("scored", "biased", "exped", "mixed", "turned", "laid", "outed", "kept"))
        block = st.block()
        TURN, OUT = 4, 7

        @block.tensor
        def _(pe):
            def score(u):
                h, qi = units[u]
                if u >= 2:
                    pe.wait_ge(biased, u - 1)
                w = P * (qi + 1)
                for i in range(2):
                    b = 64 * (h % 2) + 32 * i
                    mm = pe.matmul(c.ps[:, 2 * (u % 2) + i, 0:w], m.dqk[b:b + 32, h // 2, qi * P:(qi + 1) * P],
                                   m.dqk[b:b + 32, 2 + h // 2, 0:w], start=True, stop=True)
                mm.then_inc(scored, 1)

            def turn(u):
                h, qi = units[u]
                pe.wait_ge(mixed, u + 1)
                if u >= 3:
                    pe.wait_ge(laid, u - 2)
                for j in range(qi + 1):
                    mm = pe.transpose(c.ps[:, TURN + u % 3, j * P:(j + 1) * P], prob[:, u % 2, j * P:(j + 1) * P], c.ident[:, :])
                mm.then_inc(turned, 1)

            def out(h):
                pe.wait_ge(laid, TT * (h + 1))
                if h >= 1:
                    pe.wait_ge(kept, h)
                b = 64 * (h % 2)
                for j in range(TT):
                    mm = pe.matmul(c.ps[b:b + 64, OUT, j * P:], m.dv[:, j, h * 64:(h + 1) * 64], prob_T[:, h % 2, j, j * P:],
                                   start=(j == 0), stop=(j == TT - 1))
                mm.then_inc(outed, 1)

            score(0)
            score(1)
            for u, (h, qi) in enumerate(units):
                if u + 2 < U:
                    score(u + 2)
                turn(u)
                if qi == 1 and h >= 1:
                    out(h - 1)
            out(DF_HEADS - 1)

        @block.vector
        def _(dve):
            def bias(u):
                h, qi = units[u]
                w = P * (qi + 1)
                dve.wait_ge(scored, u + 1)
                for i in range(2):
                    ins = dve.tensor_tensor_reduce(neg[:, u % 3, i, 0:w], c.ps[:, 2 * (u % 2) + i, 0:w], tiles[:, h, SEQ - w:SEQ],
                                                   -1.0, 3e38, ALU.add, ALU.min, nmax[:, u % 3, i:i + 1])
                ins.then_inc(biased, 1)

            def mix(u):
                h, qi = units[u]
                w = P * (qi + 1)
                s = u % 3
                dve.wait_ge(exped, u + 1)
                if u >= 2:
                    dve.wait_ge(turned, u - 1)
                dve.reciprocal(recip[:, s, :], total[:, s, :])
                dve.drain()
                dve.tensor_scalar(prob[:, u % 2, 0:w], neg[:, s, 1, 0:w], recip[:, s, 1:2], lam[:, 0:1], ALU.mult, ALU.mult)
                dve.drain()
                dve.scalar_tensor_tensor(out=prob[:, u % 2, 0:w], in0=neg[:, s, 0, 0:w], scalar=recip[:, s, 0:1],
                                         in1=prob[:, u % 2, 0:w], op0=ALU.mult, op1=ALU.add).then_inc(mixed, 1)
                dve.drain()

            bias(0)
            bias(1)
            for u in range(U):
                mix(u)
                if u + 2 < U:
                    bias(u + 2)

        @block.scalar
        def _(act):
            def exps(u):
                h, qi = units[u]
                w = P * (qi + 1)
                act.wait_ge(biased, u + 1)
                for i in range(2):
                    ins = act.activation(neg[:, u % 3, i, 0:w], neg[:, u % 3, i, 0:w], ACT.Exp, scale=-1.0,
                                         bias=nmax[:, u % 3, i:i + 1], accum_out=total[:, u % 3, i:i + 1])
                ins.then_inc(exped, 1)

            def lay(u):
                h, qi = units[u]
                act.wait_ge(turned, u + 1)
                if h >= 2:
                    act.wait_ge(outed, h - 1)
                act.activation(prob_T[:, h % 2, 0:qi + 1, qi * P:(qi + 1) * P],
                               c.ps[:, TURN + u % 3, 0:P * (qi + 1)].rearrange("p (j q) -> p j q", q=P), ACT.Copy)\
                    .then_inc(laid, 1)

            def keep(h):
                act.wait_ge(outed, h + 1)
                b = 64 * (h % 2)
                act.activation(o_T[b:b + 64, h // 2, :], c.ps[b:b + 64, OUT, :], ACT.Copy).then_inc(kept, 1)

            exps(0)
            for u in range(U):
                if u + 1 < U:
                    exps(u + 1)
                if u >= 1:
                    lay(u - 1)
                if units[u][1] == 3 and u >= TT:
                    keep(units[u][0] - 1)
            lay(U - 1)
            keep(DF_HEADS - 1)


def project_out(nc, c, w, src, dst, add):
    with Stage(nc) as st:
        ring = Ring(st)
        s_hi, s_lo = st.sb("s_hi", [P, KD, SEQ], F32R), st.sb("s_lo", [P, KD, SEQ], F32R)
        src_halved, src_split = st.sem("src_halved"), st.sem("src_split")
        block = st.block()

        @block.sync
        def _(sp):
            for k in range(KD):
                ring.load(sp, k % 4, k // 4, k < 4, w[k * P:(k + 1) * P, :].rearrange("p (m n) -> p m n", n=P))

        @block.gpsimd
        def _(pool):
            for k in range(KD):
                ring.low(pool, k % 4, k // 4)

        @block.scalar
        def _(act):
            for k in range(KD):
                act.activation(s_hi[:, k, :], src[:, k, :], ACT.Copy).then_inc(src_halved, 1)

        @block.tensor
        def _(pe):
            for k in range(KD):
                pe.wait_ge(ring.split[k % 4], k // 4 + 1)
                pe.wait_ge(src_split, k + 1)
                for m in range(KD):
                    for i, (wt, low) in enumerate(ring.passes(k % 4, m)):
                        mm = pe.matmul(c.ps[:, m, :], wt, (s_hi, s_lo)[low][:, k, :], start=(k == 0 and i == 0),
                                       stop=(k == KD - 1 and i == 2))
                mm.then_inc(ring.used[k % 4], 1)

        @block.vector
        def _(dve):
            for k in range(KD):
                dve.wait_ge(src_halved, k + 1)
                dve.tensor_tensor(s_lo[:, k, :], src[:, k, :], s_hi[:, k, :].bitcast(F32), ALU.subtract).then_inc(src_split, 1)
                ring.high(dve, k % 4, k // 4, k < 4)
            dve.wait_ge(ring.used[3], KD // 4)
            for m in range(KD):
                if add:
                    dve.tensor_tensor(dst[:, m, :], dst[:, m, :], c.ps[:, m, :], ALU.add)
                else:
                    dve.tensor_copy(dst[:, m, :], c.ps[:, m, :])


def first_mixer(nc, c, L, gain, w_in, w_out, scratch, lam_init):
    with nc.sbuf_tensor(f"y_T_{nc.next_id()}", [P, KD, SEQ], F32) as y_T:
        with ExitStack() as ctx:
            def sb(name, shape):
                return ctx.enter_context(nc.sbuf_tensor(f"{name}_{nc.next_id()}", shape, F32))
            m = Mixer(nc, ctx, y_T)
            first_mixer_projections(nc, c, m, L, w_in, gain)
            lam = sb("lam", [P, 2])
            rows = sb("acs", [8, SEQ]), sb("negM", [4, SEQ]), sb("negm", [4, SEQ])
            cols = sb("cols", [P, TT, 20])
            y_ssm, num, den = sb("y_ssm", [P, 4, SEQ]), sb("num", [P, 2, SEQ]), sb("den", [P, 2, SEQ])
            o_T = sb("o_T", [P, 2, SEQ])
            tiles = sb("diff_tiles", [P, DF_HEADS, SEQ])
            with nc.sbuf_tensor(f"xdt_{nc.next_id()}", [P, TT, SEQ], F32) as xdt:
                with Stage(nc) as together:
                    rest_of_gates = gates(nc, c, m, rows, cols, together)
                    rest_of_conv = conv(nc, c, m, xdt, cols, together)
                    diff_prepare(nc, c, m, lam, lam_init, y_ssm, xdt, together)
                    rest_of_gates()
                    rest_of_conv()
                    bias_tiles(nc, c, scratch, DF_HEADS, tiles, 1.0, together, num)
                recurrences(nc, c, m, rows, cols, xdt, y_ssm, num, den)
            diff_attention(nc, c, m, tiles, lam, o_T)
            finish_first_mixer(nc, c, m, rows, y_ssm, num, den, lam, o_T)
        project_out(nc, c, w_out, y_T, c.x_T, True)


LRU_X, LRU_G, NSA_Q, NSA_KV, NSA_GATE = 0, 1024, 2048, 3072, 4608
GLA_Q, GLA_K, GLA_V, GLA_OG, GLA_LR, MERGE = 4656, 5168, 5680, 6704, 7728, 7744
N_HEADS, N_KV, N_DIM = 16, 4, 64
GROUP = N_HEADS // N_KV
TAPS, STRIDE, HIDDEN = 32, 16, 256
N_CMP = SEQ // STRIDE - 1
G_HEADS, G_DV, G_CHUNK = 4, 256, 32
G_CHUNKS = SEQ // G_CHUNK
LRU_C = 8.0


def lru_params(nc, ctx, W):
    def sb(name, shape):
        return ctx.enter_context(nc.sbuf_tensor(f"{name}_{nc.next_id()}", shape, F32))
    q = {"conv_w": sb("conv_w", [P, 8, 4]), "conv_b": sb("conv_b", [P, 8]), "b_gates": sb("b_gates", [P, 2, 8]),
         "lam": sb("lru_lam", [P, 8])}
    loads = [(q["conv_b"][:, :], W["conv_b"].rearrange("(k p) -> p k", p=P)),
             (q["lam"][:, :], W["lru_lambda"].rearrange("(k p) -> p k", p=P))]
    for g in range(2):
        loads.append((q["b_gates"][:, g, :], W["lru_b_gates"][g].rearrange("(k p) -> p k", p=P)))
    for k in range(8):
        loads.append((q["conv_w"][:, k, :], W["conv_w"][:, k * P:(k + 1) * P].rearrange("t p -> p t")))
    return q, loads


def lru_mixer(nc, c, q, w_gates, xa, ga, y):
    with Stage(nc) as st:
        wg = st.sb("wg", [P, 2, 8, P])
        xc = st.sb("xc", [P, 8, SEQ])
        r = st.sb("r", [P, 8, SEQ])
        i = st.sb("i", [P, 8, SEQ])
        z, w, w2, s = (st.sb(n, [P, 8]) for n in ("z", "w", "w2", "s"))
        w_loaded, convolved, gated, opened = (st.sem(n) for n in ("w_loaded", "convolved", "gated", "opened"))
        mixed = st.sem("mixed")
        z_ready, coef, tanhed, u_ready, rooted, scanned, gelued = (
            st.sem(n) for n in ("z_ready", "coef", "tanhed", "u_ready", "rooted", "scanned", "gelued"))
        block = st.block()

        @block.sync
        def _(sp):
            for g in range(2):
                sp.dma_start(wg[:, g, :, :], w_gates[g].rearrange("n c e -> c n e")).then_inc(w_loaded, 16)

        @block.vector
        def _(dve):
            for k in range(8):
                dve.tensor_scalar(xc[:, k, :], xa[:, k, :], q["conv_w"][:, k, 3:4], q["conv_b"][:, k:k + 1], ALU.mult, ALU.add)
            for t in range(1, 4):
                dve.drain()
                for k in range(8):
                    ins = dve.scalar_tensor_tensor(out=xc[:, k, t:], in0=xa[:, k, 0:SEQ - t],
                                                   scalar=q["conv_w"][:, k, 3 - t:4 - t], in1=xc[:, k, t:],
                                                   op0=ALU.mult, op1=ALU.add)
                    if t == 3:
                        ins.then_inc(convolved, 1)
            dve.wait_ge(z_ready, 1)
            dve.tensor_scalar(w[:, :], z[:, :], 2.0, None, ALU.add)
            dve.drain()
            dve.reciprocal(w[:, :], w[:, :])
            dve.drain()
            dve.tensor_tensor(w[:, :], w[:, :], z[:, :], ALU.mult)
            dve.drain()
            dve.tensor_tensor(w2[:, :], w[:, :], w[:, :], ALU.mult)
            dve.drain()
            dve.tensor_scalar(s[:, :], w2[:, :], 2.0 / 19, None, ALU.mult)
            for n in range(17, 1, -2):
                dve.drain()
                dve.scalar_tensor_tensor(out=s[:, :], in0=s[:, :], scalar=2.0 / n, in1=w2[:, :], op0=ALU.add, op1=ALU.mult)
            dve.drain()
            dve.scalar_tensor_tensor(out=s[:, :], in0=s[:, :], scalar=2.0, in1=w[:, :], op0=ALU.add, op1=ALU.mult)
            dve.tensor_scalar(z[:, :], q["lam"][:, :], -1.0, 0.0, ALU.mult, ALU.max)
            dve.drain()
            dve.tensor_tensor(s[:, :], s[:, :], z[:, :], ALU.add)
            dve.drain()
            dve.tensor_scalar(s[:, :], s[:, :], LRU_C, None, ALU.mult)
            dve.drain()
            for k in range(8):
                dve.wait_ge(opened, 2 * k + 2)
                dve.tensor_scalar(r[:, k, :], r[:, k, :], s[:, k:k + 1], None, ALU.mult).then_inc(coef, 1)
            dve.wait_ge(tanhed, 2)
            dve.tensor_tensor(xa[:, :, :], r[:, :, :], r[:, :, :], ALU.mult)
            dve.drain()
            dve.scalar_tensor_tensor(out=xa[:, :, :], in0=xa[:, :, :], scalar=1.0, in1=xc[:, :, :],
                                     op0=ALU.add, op1=ALU.mult).then_inc(u_ready, 1)
            dve.wait_ge(rooted, 1)
            dve.wait_ge(mixed, 8)
            dve.tensor_tensor(xa[:, :, :], xa[:, :, :], i[:, :, :], ALU.mult)
            dve.drain()
            for k in range(8):
                dve.tensor_tensor_scan(xc[:, k, :], r[:, k, :], xa[:, k, :], 0.0, ALU.mult, ALU.add).then_inc(scanned, 1)

        @block.gpsimd
        def _(pool):
            for k in range(8):
                pool.wait_ge(opened, 2 * k + 2)
                pool.tensor_tensor(i[:, k, :], i[:, k, :], xc[:, k, :], ALU.mult).then_inc(mixed, 1)
            pool.wait_ge(gelued, 1)
            for k in range(8):
                pool.wait_ge(scanned, k + 1)
                pool.tensor_tensor(y[:, k, :], xc[:, k, :], ga[:, k, :], ALU.mult)

        @block.tensor
        def _(pe):
            pe.wait_ge(w_loaded, 32)
            for k in range(8):
                pe.wait_ge(convolved, k + 1)
                if k == 0:
                    pe.wait_ge(convolved, 8)
                for g in range(2):
                    n = 2 * k + g
                    if n >= 4:
                        pe.wait_ge(opened, n - 3)
                    pe.matmul(c.ps[:, n % 4, :], wg[:, g, k, :], xc[:, k, :], start=True, stop=True).then_inc(gated, 1)

        @block.scalar
        def _(act):
            act.activation(z[:, :], q["lam"][:, :], ACT.Abs)
            act.drain()
            act.activation(z[:, :], z[:, :], ACT.Exp, scale=-1.0).then_inc(z_ready, 1)
            act.activation(ga[:, :, :], ga[:, :, :], ACT.Gelu_apprx_tanh).then_inc(gelued, 1)
            for k in range(8):
                for g, to in enumerate((r, i)):
                    act.wait_ge(gated, 2 * k + g + 1)
                    act.activation(to[:, k, :], c.ps[:, (2 * k + g) % 4, :], ACT.Sigmoid,
                                   bias=q["b_gates"][:, g, k:k + 1]).then_inc(opened, 1)
            act.wait_ge(coef, 8)
            act.wait_ge(mixed, 8)
            act.activation(xc[:, :, :], r[:, :, :], ACT.Tanh)
            act.drain().then_inc(tanhed, 1)
            act.activation(r[:, :, :], r[:, :, :], ACT.Exp, scale=-1.0).then_inc(tanhed, 1)
            act.wait_ge(u_ready, 1)
            act.activation(xa[:, :, :], xa[:, :, :], ACT.Sqrt).then_inc(rooted, 1)


class Nsa:
    def __init__(self, nc, ctx):
        def sb(name, shape):
            return ctx.enter_context(nc.sbuf_tensor(f"{name}_{nc.next_id()}", shape, F32))
        self.qk = sb("qk", [P, 14, SEQ])
        self.q = self.qk[:, 0:8, :]
        self.p_cmp = self.qk[:, 8:12, :]
        self.k_slc = sb("k_slc", [P, N_KV, SEQ])
        self.k_win = sb("k_win", [P, N_KV, SEQ])
        self.v_slc = sb("v_slc", [P, TT, 256])
        self.v_win = sb("v_win", [P, TT, 256])
        self.gate = sb("gate", [P, TT, 3 * N_HEADS])
        self.k_cmp = sb("k_cmp", [P, N_KV, 32])
        self.v_cmp = sb("v_cmp", [P, N_KV, N_DIM])


def spread_keys(nc, c, n, kw, within):
    with Stage(nc, within) as st:
        block = st.block()

        @block.scalar
        def _(act):
            for dst, kk in ((n.k_slc, n.qk[:, 12:14, :]), (n.k_win, kw)):
                for g in range(N_KV):
                    b = 64 * (g % 2)
                    act.activation(dst[0:64, g, :], kk[b:b + 64, g // 2, :], ACT.Copy)
            act.activation(n.gate[:, :, :], n.gate[:, :, :], ACT.Sigmoid)

        @block.vector
        def _(dve):
            for dst, kk in ((n.k_slc, n.qk[:, 12:14, :]), (n.k_win, kw)):
                for g in range(N_KV):
                    b = 64 * (g % 2)
                    dve.tensor_copy(dst[64:P, g, :], kk[b:b + 64, g // 2, :])


def compress(nc, c, n, kv, spare, pos, w1, w2, within):
    with Stage(nc, within) as st:
        base = spare[0:64, :, :].rearrange("p (i g) t -> p i g t", i=2)
        tap = st.sb("tap", [64, 2, 2, N_KV, SEQ])
        pos_T = st.sb("pos_T", [64, 2, TAPS])
        w1s = st.sb("w1s", [64, 2, TAPS // 2, HIDDEN])
        w2s = st.sb("w2s", [P, 2, 2, P])
        hid = st.sb("hid", [P, 2, 2, N_KV, 32])
        hid4 = st.sb("hid4", [P, 2, N_KV, GROUP, 32])
        pos_loaded, w2_loaded, moved, tapped, hidden, netted, spread, outed, multiplied = (
            st.sem(x) for x in ("pos_loaded", "w2_loaded", "moved", "tapped", "hidden", "netted", "spread", "outed",
                                "multiplied"))
        w1_loaded = [st.sem(f"w1_loaded{s}") for s in range(2)]
        block = st.block()

        @block.sync
        def _(sp):
            with nc.allow_non_contiguous_dma(reason="small positions, turned"):
                for i in range(2):
                    sp.dma_start(pos_T[:, i, :], pos[i].rearrange("l d -> d l")).then_inc(pos_loaded, 16)
            for i in range(2):
                for half in range(2):
                    u = 2 * i + half
                    if u >= 2:
                        sp.wait_ge(multiplied, u - 1)
                    sp.dma_start(w1s[:, half, :, :],
                                 w1[i, half * 1024:(half + 1) * 1024, :].rearrange("(l d) f -> d l f", d=N_DIM))\
                        .then_inc(w1_loaded[half], 16)
                for twice in range(2):
                    sp.dma_start(w2s[:, i, :, 64 * twice:64 * twice + 64], w2[i].rearrange("(k p) d -> p k d", p=P))\
                        .then_inc(w2_loaded, 16)

        @block.scalar
        def _(act):
            for i in range(2):
                for g in range(N_KV):
                    b = 64 * (g % 2)
                    ins = act.activation(base[:, i, g, :], kv[b:b + 64, 2 * i + g // 2, :], ACT.Copy)
            ins.then_inc(moved, 1)
            for i in range(2):
                act.wait_ge(hidden, i + 1)
                for k in range(2):
                    ins = act.activation(hid[:, i, k, :, 0:N_CMP],
                                         c.ps[:, 2 * i + k, 0:N_KV * N_CMP].rearrange("p (g n) -> p g n", n=N_CMP),
                                         ACT.Gelu_apprx_tanh)
                ins.then_inc(netted, 1)
            act.wait_ge(outed, 1)
            act.activation(n.k_cmp[:, :, 0:N_CMP], c.ps[:, 4, 0:N_KV * N_CMP].rearrange("p (g n) -> p g n", n=N_CMP), ACT.Copy)
            act.wait_ge(outed, 2)
            act.activation(n.v_cmp[:, :, :], c.ps[:, 5, 0:N_KV * N_DIM].rearrange("p (g d) -> p g d", d=N_DIM), ACT.Copy)

        @block.vector
        def _(dve):
            dve.memset(hid[:, :, :, :, N_CMP:32], 0.0)
            dve.wait_ge(pos_loaded, 32)
            dve.wait_ge(moved, 1)
            for i in range(2):
                for half in range(2):
                    add = pos_T[:, i, 16 * half:16 * half + 16].rearrange("p (o l) -> p o l", o=1)
                    ins = dve.tensor_tensor(tap[:, i, half, :, :].rearrange("p g (n l) -> p (g n) l", l=16),
                                            base[:, i, :, :].rearrange("p g (n l) -> p (g n) l", l=16),
                                            add.to_broadcast([64, N_KV * 32, 16]), ALU.add)
            ins.then_inc(tapped, 1)
            dve.drain()
            dve.wait_ge(netted, 2)
            for k in range(2):
                ins = dve.tensor_copy(hid4[:, k, :, :, :],
                                      hid[:, 1, k, :, :].rearrange("p g (o n) -> p g o n", o=1)
                                      .to_broadcast([P, N_KV, GROUP, 32]))
            ins.then_inc(spread, 1)

        @block.tensor
        def _(pe):
            pe.wait_ge(tapped, 1)
            for i in range(2):
                for half in range(2):
                    pe.wait_ge(w1_loaded[half], 16 * i + 16)
                    for k in range(2):
                        for l in range(16):
                            src = tap[:, i, half, :, :].rearrange("p g (n l) -> p g n l", l=16)[:, :, half:half + N_CMP, l]
                            mm = pe.matmul(c.ps[:, 2 * i + k, 0:N_KV * N_CMP], w1s[:, half, l, k * P:(k + 1) * P], src,
                                           start=(half == 0 and l == 0), stop=(half == 1 and l == 15))
                    mm.then_inc(multiplied, 1)
                    if half == 1:
                        pe.wait_ge(multiplied, 2 * i + 2)
                        pe.drain().then_inc(hidden, 1)
            pe.wait_ge(w2_loaded, 64)
            pe.wait_ge(netted, 2)
            for k in range(2):
                mm = pe.matmul(c.ps[:, 4, 0:N_KV * N_CMP], w2s[:, 0, k, :], hid[:, 0, k, :, 0:N_CMP], start=(k == 0), stop=(k == 1))
            mm.then_inc(outed, 1)
            pe.wait_ge(spread, 1)
            for g in range(N_KV):
                for k in range(2):
                    mm = pe.matmul(c.ps[:, 5, g * N_DIM:(g + 1) * N_DIM], hid4[:, k, g, :, :].rearrange("p r n -> p (r n)"),
                                   w2s[:, 1, k, 0:N_DIM], start=(k == 0), stop=(k == 1))
            mm.then_inc(outed, 1)


def compressed_scores(nc, c, n, tiles):
    with Stage(nc) as st:
        e = st.sb("e", [P, 2, N_HEADS, 32])
        mx = st.sb("mx", [P, 2, N_HEADS])
        tot = st.sb("tot", [P, 2, N_HEADS])
        scored, shifted, exped, ready, turned, laid = (
            st.sem(x) for x in ("scored", "shifted", "exped", "ready", "turned", "laid"))
        block = st.block()

        def wide(ap, w):
            return ap.rearrange("p (h o) -> p h o", o=1).to_broadcast([P, N_HEADS, w])

        @block.tensor
        def _(pe):
            def score(qi):
                nv = 8 * qi + 7
                if qi >= 2:
                    pe.wait_ge(shifted, qi - 1)
                for h in range(N_HEADS):
                    b = 64 * (h % 2)
                    at = 32 * (h // 2)
                    mm = pe.matmul(c.ps[:, 2 * (qi % 2) + h % 2, at:at + nv], n.q[b:b + 64, h // 2, qi * P:(qi + 1) * P],
                                   n.k_cmp[b:b + 64, h // GROUP, 0:nv], start=True, stop=True)
                mm.then_inc(scored, 1)

            def turn(qi):
                pe.wait_ge(ready, qi + 1)
                if qi >= 1:
                    pe.wait_ge(laid, qi)
                for g in range(N_KV):
                    mm = pe.transpose(c.ps[:, 4, g * P:(g + 1) * P],
                                      e[:, qi % 2, GROUP * g:GROUP * (g + 1), :].rearrange("p h n -> p (h n)"), c.ident[:, :])
                mm.then_inc(turned, 1)

            score(0)
            score(1)
            for qi in range(TT):
                turn(qi)
                if qi + 2 < TT:
                    score(qi + 2)

        @block.vector
        def _(dve):
            dve.memset(e[:, :, :, :], 0.0)

            def shift(qi):
                nv = 8 * qi + 7
                s = qi % 2
                dve.drain()
                dve.wait_ge(scored, qi + 1)
                if qi >= 2:
                    dve.wait_ge(turned, qi - 1)
                at = 415 - P * qi
                for half in range(2):
                    dve.tensor_tensor(e[:, s, half::2, 0:nv],
                                      c.ps[:, 2 * s + half, 0:256].rearrange("p (h n) -> p h n", n=32)[:, :, 0:nv],
                                      tiles[:, half::2, at:at + 16 * nv - 15:16], ALU.add)
                dve.drain()
                dve.tensor_reduce(mx[:, s, :], e[:, s, :, 0:nv], AX, ALU.max)
                dve.drain()
                dve.tensor_scalar(mx[:, s, :], mx[:, s, :], MASKED / 100, None, ALU.max)
                dve.drain()
                dve.tensor_tensor(e[:, s, :, 0:nv], e[:, s, :, 0:nv], wide(mx[:, s, :], nv), ALU.subtract).then_inc(shifted, 1)

            def scale(qi):
                nv = 8 * qi + 7
                s = qi % 2
                dve.wait_ge(exped, qi + 1)
                dve.reduce_sum(tot[:, s, :], e[:, s, :, 0:nv], AX)
                dve.drain()
                dve.tensor_scalar(tot[:, s, :], tot[:, s, :], 1e-30, None, ALU.max)
                dve.drain()
                dve.reciprocal(tot[:, s, :], tot[:, s, :])
                dve.drain()
                dve.tensor_tensor(tot[:, s, :], tot[:, s, :], n.gate[:, qi, 0:N_HEADS], ALU.mult)
                dve.drain()
                dve.tensor_tensor(e[:, s, :, 0:nv], e[:, s, :, 0:nv], wide(tot[:, s, :], nv), ALU.mult).then_inc(ready, 1)

            shift(0)
            for qi in range(TT):
                if qi + 1 < TT:
                    shift(qi + 1)
                scale(qi)

        @block.scalar
        def _(act):
            def exps(qi):
                nv = 8 * qi + 7
                act.wait_ge(shifted, qi + 1)
                act.activation(e[:, qi % 2, :, 0:nv], e[:, qi % 2, :, 0:nv], ACT.Exp,
                               scale=N_DIM ** -0.5).then_inc(exped, 1)

            exps(0)
            for qi in range(TT):
                if qi + 1 < TT:
                    exps(qi + 1)
                act.wait_ge(turned, qi + 1)
                act.activation(n.p_cmp[:, :, qi * P:(qi + 1) * P], c.ps[:, 4, :].rearrange("p (g q) -> p g q", q=P), ACT.Copy)\
                    .then_inc(laid, 1)


def nsa_attention(nc, c, n, tiles, y):
    units = [(h, qi, i) for h in range(N_HEADS) for qi in range(TT) for i in range(2)]
    U = len(units)
    PER = 2 * TT
    with Stage(nc) as st:
        neg = st.sb("neg", [P, 4, SEQ])
        prob_T = st.sb("prob_T", [P, 2, 2, TT, SEQ])
        win = st.sb("win", [P, 2, 3 * P])
        nmax, total, recip = (st.sb(x, [P, 4]) for x in ("nmax", "total", "recip"))
        win_ready, scored, biased, exped, scaled, turned, laid, outed, kept = (
            st.sem(x) for x in ("win_ready", "scored", "biased", "exped", "scaled", "turned", "laid", "outed", "kept"))
        block = st.block()
        TURN, OUT = 3, 6

        def first_key(u):
            h, qi, i = units[u]
            return 0 if i == 0 else max(0, qi - 2)

        def width(u):
            return P * (units[u][1] + 1 - first_key(u))

        @block.gpsimd
        def _(pool):
            for h in range(N_HEADS):
                if h >= 2:
                    pool.wait_ge(biased, PER * (h - 1))
                pool.tensor_tensor(win[:, h % 2, 0:P], tiles[:, h, P:2 * P], c.winmask[:, :], ALU.add)
                pool.tensor_copy(win[:, h % 2, P:3 * P], tiles[:, h, 2 * P:4 * P])
                pool.drain().then_inc(win_ready, 1)

        @block.tensor
        def _(pe):
            def score(u):
                h, qi, i = units[u]
                if u >= 3:
                    pe.wait_ge(biased, u - 2)
                b, g = 64 * (h % 2), h // GROUP
                k0 = P * first_key(u)
                pe.matmul(c.ps[:, u % 3, 0:width(u)], n.q[b:b + 64, h // 2, qi * P:(qi + 1) * P],
                          (n.k_slc, n.k_win)[i][b:b + 64, g, k0:P * (qi + 1)], start=True, stop=True).then_inc(scored, 1)

            def turn(u):
                pe.wait_ge(scaled, u + 1)
                if u >= 3:
                    pe.wait_ge(laid, u - 2)
                for j in range(width(u) // P):
                    mm = pe.transpose(c.ps[:, TURN + u % 3, j * P:(j + 1) * P], neg[:, u % 4, j * P:(j + 1) * P], c.ident[:, :])
                mm.then_inc(turned, 1)

            def out(h):
                pe.wait_ge(laid, PER * (h + 1))
                if h >= 2:
                    pe.wait_ge(kept, h - 1)
                b, g, r = 64 * (h % 2), h // GROUP, h % GROUP
                to = OUT + h % 2
                pe.matmul(c.ps[b:b + 64, to, :], n.v_cmp[32 * r:32 * r + 32, g, :], n.p_cmp[32 * r:32 * r + 32, g, :],
                          start=True, stop=False)
                for i, v in enumerate((n.v_slc, n.v_win)):
                    for j in range(TT):
                        end = SEQ if i == 0 else min(SEQ, P * (j + 3))
                        mm = pe.matmul(c.ps[b:b + 64, to, j * P:end], v[:, j, g * N_DIM:(g + 1) * N_DIM],
                                       prob_T[:, h % 2, i, j, j * P:end], start=False, stop=(i == 1 and j == TT - 1))
                mm.then_inc(outed, 1)

            for u in range(3):
                score(u)
            for u in range(U):
                if u + 3 < U:
                    score(u + 3)
                turn(u)
                if u % PER == 3 and u > PER:
                    out(u // PER - 1)
            out(N_HEADS - 1)

        @block.vector
        def _(dve):
            def bias(u):
                h, qi, i = units[u]
                w = width(u)
                dve.wait_ge(scored, u + 1)
                if u >= 4:
                    dve.wait_ge(turned, u - 3)
                if u % PER == 0:
                    dve.wait_ge(win_ready, h + 1)
                bias_of = win[:, h % 2, 3 * P - w:] if i == 1 else tiles[:, h, SEQ - w:]
                dve.tensor_tensor_reduce(neg[:, u % 4, 0:w], c.ps[:, u % 3, 0:w], bias_of, -(N_DIM ** -0.5), 3e38,
                                         ALU.add, ALU.min, nmax[:, u % 4:u % 4 + 1]).then_inc(biased, 1)

            def scale(u):
                h, qi, i = units[u]
                w, s = width(u), u % 4
                dve.wait_ge(exped, u + 1)
                dve.reciprocal(recip[:, s:s + 1], total[:, s:s + 1])
                dve.drain()
                at = N_HEADS * (i + 1) + h
                dve.tensor_scalar(neg[:, s, 0:w], neg[:, s, 0:w], recip[:, s:s + 1], n.gate[:, qi, at:at + 1],
                                  ALU.mult, ALU.mult).then_inc(scaled, 1)

            bias(0)
            bias(1)
            for u in range(U):
                scale(u)
                if u + 2 < U:
                    bias(u + 2)

        @block.scalar
        def _(act):
            def exps(u):
                s, w = u % 4, width(u)
                act.wait_ge(biased, u + 1)
                act.activation(neg[:, s, 0:w], neg[:, s, 0:w], ACT.Exp, scale=-1.0, bias=nmax[:, s:s + 1],
                               accum_out=total[:, s:s + 1]).then_inc(exped, 1)

            def lay(u):
                h, qi, i = units[u]
                act.wait_ge(turned, u + 1)
                if h >= 2 and u % PER == 0:
                    act.wait_ge(outed, h - 1)
                act.activation(prob_T[:, h % 2, i, first_key(u):qi + 1, qi * P:(qi + 1) * P],
                               c.ps[:, TURN + u % 3, 0:width(u)].rearrange("p (j q) -> p j q", q=P), ACT.Copy)\
                    .then_inc(laid, 1)

            def keep(h):
                act.wait_ge(outed, h + 1)
                b = 64 * (h % 2)
                act.activation(y[b:b + 64, h // 2, :], c.ps[b:b + 64, OUT + h % 2, :], ACT.Copy).then_inc(kept, 1)

            exps(0)
            for u in range(U):
                if u + 1 < U:
                    exps(u + 1)
                if u >= 1:
                    lay(u - 1)
                if u % PER == PER - 1 and u >= PER:
                    keep(u // PER - 1)
            lay(U - 1)
            keep(N_HEADS - 1)


class Gla:
    def __init__(self, nc, ctx):
        def sb(name, shape):
            return ctx.enter_context(nc.sbuf_tensor(f"{name}_{nc.next_id()}", shape, F32))
        self.qk = sb("gqk", [P, 8, SEQ])
        self.q, self.k = self.qk[:, 0:4, :], self.qk[:, 4:8, :]
        self.og = sb("og", [P, 8, SEQ])
        self.v = sb("gv", [P, TT, D])
        self.lr = sb("lr", [16, SEQ])
        self.wa2 = sb("wa2", [16, 512])
        self.ba = sb("ba", [P, 4])
        self.gain = sb("ggain", [P, 2])


def gla_prepare(nc, c, g):
    with Stage(nc) as st:
        x, l, b, d = (st.sb(n, [P, 4, SEQ]) for n in ("x", "l", "b", "d"))
        gated, logged, ready, b_ready, exped, k_ready, turned, q_ready = (
            st.sem(n) for n in ("gated", "logged", "ready", "b_ready", "exped", "k_ready", "turned", "q_ready"))
        block = st.block()

        def chunks(ap):
            return ap.rearrange("p h (c t) -> p (h c) t", t=G_CHUNK)

        @block.tensor
        def _(pe):
            for h in range(G_HEADS):
                mm = pe.matmul(c.ps[:, h, :], g.wa2[:, h * P:(h + 1) * P], g.lr[:, :], start=True, stop=True)
            mm.then_inc(gated, 1)
            pe.wait_ge(k_ready, 1)
            for t in range(TT):
                for h in range(G_HEADS):
                    mm = pe.transpose(c.ps[:, 4 + t, h * P:(h + 1) * P], g.k_end[:, h, t * P:(t + 1) * P], c.ident[:, :])
            mm.then_inc(turned, 1)

        @block.scalar
        def _(act):
            act.wait_ge(gated, 1)
            for h in range(G_HEADS):
                act.activation(x[:, h, :], c.ps[:, h, :], ACT.Identity, bias=g.ba[:, h:h + 1])
            act.drain()
            act.activation(l[:, :, :], x[:, :, :], ACT.Abs)
            act.drain()
            act.activation(l[:, :, :], l[:, :, :], ACT.Exp, scale=-1.0)
            act.drain()
            act.activation(l[:, :, :], l[:, :, :], ACT.Ln, bias=c.one[:, :])
            act.drain().then_inc(logged, 1)
            act.wait_ge(b_ready, 1)
            act.activation(x[:, :, :], b[:, :, :], ACT.Exp, scale=1.0 / 16)
            act.activation(l[:, :, :], b[:, :, :], ACT.Exp, scale=-1.0 / 16)
            act.activation(g.decay[:, :, :].rearrange("p h c -> p (h c)"), chunks(b[:, :, :])[:, :, G_CHUNK - 1], ACT.Exp,
                           scale=1.0 / 16)
            act.activation(d[:, :, :], d[:, :, :], ACT.Exp, scale=1.0 / 16)
            act.drain().then_inc(exped, 1)
            act.wait_ge(turned, 1)
            act.activation(g.k_end_t[:, :, :, :].rearrange("p t h d -> p t (h d)"), c.ps[:, 4:8, :], ACT.Copy)

        @block.vector
        def _(dve):
            dve.wait_ge(logged, 1)
            dve.scalar_tensor_tensor(out=x[:, :, :], in0=x[:, :, :], scalar=0.0, in1=l[:, :, :], op0=ALU.min, op1=ALU.subtract)
            dve.drain()
            for h in range(G_HEADS):
                dve.tensor_tensor_scan(b[:, h, :], c.scanone[:, :], x[:, h, :], 0.0, ALU.mult, ALU.add)
            dve.drain()
            last = chunks(b[:, :, :])[:, :, G_CHUNK - 1:G_CHUNK].to_broadcast([P, 4 * G_CHUNKS, G_CHUNK])
            dve.tensor_tensor(chunks(d[:, :, :]), last, chunks(b[:, :, :]), ALU.subtract)
            dve.drain().then_inc(b_ready, 1)
            dve.wait_ge(exped, 1)
            dve.tensor_tensor(g.k_end[:, :, :], g.k[:, :, :], d[:, :, :], ALU.mult).then_inc(k_ready, 1)
            dve.tensor_tensor(g.k[:, :, :], g.k[:, :, :], l[:, :, :], ALU.mult)
            dve.scalar_tensor_tensor(out=g.q[:, :, :], in0=g.q[:, :, :], scalar=P ** -0.5, in1=x[:, :, :],
                                     op0=ALU.mult, op1=ALU.mult)


def gla_scan(nc, c, g, o_T):
    with Stage(nc) as st:
        att = st.sb("att", [P, TT, G_HEADS, P])
        state = st.sb("state", [P, 2, G_HEADS, G_DV])
        scored, masked, updated, stepped, read, outed, kept = (
            st.sem(n) for n in ("scored", "masked", "updated", "stepped", "read", "outed", "kept"))
        block = st.block()

        def product_for_state(k, h):
            return c.ps[:, 4 + 2 * (k % 2) + h // 2, (h % 2) * G_DV:(h % 2 + 1) * G_DV]

        @block.tensor
        def _(pe):
            def scores(t):
                if t >= 1:
                    pe.wait_ge(masked, t)
                for h in range(G_HEADS):
                    mm = pe.matmul(c.ps[:, 2, h * P:(h + 1) * P], g.k[:, h, t * P:(t + 1) * P], g.q[:, h, t * P:(t + 1) * P],
                                   start=True, stop=True)
                mm.then_inc(scored, 1)

            def update(k):
                if k >= 2:
                    pe.wait_ge(stepped, k - 1)
                t, b = k // 4, G_CHUNK * (k % 4)
                for h in range(G_HEADS):
                    mm = pe.matmul(product_for_state(k, h), g.k_end_t[b:b + 32, t, h, :],
                                   g.v[b:b + 32, t, h * G_DV:(h + 1) * G_DV], start=True, stop=True)
                mm.then_inc(updated, 1)

            scores(0)
            update(0)
            for t in range(TT):
                pe.wait_ge(masked, t + 1)
                if t >= 1:
                    pe.wait_ge(kept, t)
                for h in range(G_HEADS):
                    for e in range(2):
                        n = 2 * h + e
                        pe.matmul(c.ps[:, n // 4, (n % 4) * P:(n % 4 + 1) * P], g.v[:, t, h * G_DV + e * P:h * G_DV + (e + 1) * P],
                                  att[:, t, h, :], start=(n % 4 == 0), stop=False, skip_group_check=True)
                if t + 1 < TT:
                    scores(t + 1)
                for s in range(4):
                    k = 4 * t + s
                    if k + 2 < G_CHUNKS:
                        update(k + 1)
                    if k >= 1:
                        pe.wait_ge(stepped, k)
                        for h in range(G_HEADS):
                            for e in range(2):
                                n = 2 * h + e
                                at = (n % 4) * P + s * G_CHUNK
                                mm = pe.matmul(c.ps[:, n // 4, at:at + G_CHUNK], state[:, k % 2, h, e * P:(e + 1) * P],
                                               g.q[:, h, k * G_CHUNK:(k + 1) * G_CHUNK], start=False, stop=(s == 3),
                                               skip_group_check=True)
                        mm.then_inc(read, 1)
                    if s == 3:
                        mm = pe.drain().then_inc(outed, 1)

        @block.vector
        def _(dve):
            def mask(t):
                dve.wait_ge(scored, t + 1)
                dve.tensor_tensor(att[:, t, :, :], c.ps[:, 2, :].rearrange("p (h t) -> p h t", t=P),
                                  c.chunkmask[:, :].rearrange("p (o t) -> p o t", o=1).to_broadcast([P, G_HEADS, P]), ALU.mult)\
                    .then_inc(masked, 1)

            mask(0)
            for k in range(G_CHUNKS - 1):
                if k % 4 == 0 and k // 4 + 1 < TT:
                    mask(k // 4 + 1)
                dve.wait_ge(updated, k + 1)
                if k >= 2:
                    dve.wait_ge(read, k - 1)
                dve.drain()
                for h in range(G_HEADS):
                    new = product_for_state(k, h)
                    if k == 0:
                        ins = dve.tensor_copy(state[:, 1, h, :], new)
                    else:
                        ins = dve.scalar_tensor_tensor(out=state[:, (k + 1) % 2, h, :], in0=state[:, k % 2, h, :],
                                                       scalar=g.decay[:, h, k:k + 1], in1=new, op0=ALU.mult, op1=ALU.add)
                ins.then_inc(stepped, 1)

        @block.scalar
        def _(act):
            for t in range(TT):
                act.wait_ge(outed, t + 1)
                act.activation(o_T[:, :, t * P:(t + 1) * P], c.ps[:, 0:2, :].rearrange("p b (n q) -> p (b n) q", q=P), ACT.Copy)\
                    .then_inc(kept, 1)


def gla_finish(nc, c, g, o_T, y):
    with Stage(nc) as st:
        sq = st.sb("sq", [P, 8, SEQ])
        rstd = st.sb("rstd", [P, 4, SEQ])
        squared, summed, rooted, opened, gated = (st.sem(n) for n in ("squared", "summed", "rooted", "opened", "gated"))
        block = st.block()

        @block.scalar
        def _(act):
            for h in range(G_HEADS):
                act.activation(sq[:, 2 * h:2 * h + 2, :], o_T[:, 2 * h:2 * h + 2, :], ACT.Square).then_inc(squared, 1)
            act.activation(g.og[:, :, :], g.og[:, :, :], ACT.Silu).then_inc(opened, 1)
            for h in range(G_HEADS):
                act.wait_ge(summed, h + 1)
                act.activation(rstd[:, h, :], c.ps[:, h, :], ACT.Sqrt, scale=1.0 / G_DV, bias=c.eps[:, :]).then_inc(rooted, 1)

        @block.tensor
        def _(pe):
            for h in range(G_HEADS):
                pe.wait_ge(squared, h + 1)
                for e in range(2):
                    mm = pe.matmul(c.ps[:, h, :], c.ones[:, :], sq[:, 2 * h + e, :], start=(e == 0), stop=(e == 1))
                mm.then_inc(summed, 1)

        @block.gpsimd
        def _(pool):
            pool.wait_ge(opened, 1)
            for h in range(G_HEADS):
                at = slice(2 * h, 2 * h + 2)
                pool.tensor_tensor(g.og[:, at, :], g.og[:, at, :], o_T[:, at, :], ALU.mult).then_inc(gated, 1)

        @block.vector
        def _(dve):
            for h in range(G_HEADS):
                dve.wait_ge(rooted, h + 1)
                dve.reciprocal(rstd[:, h, :], rstd[:, h, :])
                dve.drain()
                dve.wait_ge(gated, h + 1)
                for k in (2 * h, 2 * h + 1):
                    dve.scalar_tensor_tensor(out=y[:, k, :], in0=g.og[:, k, :], scalar=g.gain[:, k % 2:k % 2 + 1],
                                             in1=rstd[:, h, :], op0=ALU.mult, op1=ALU.mult)


def second_block(nc, c, W, scratch):
    w_in = W["w_in"]
    with ExitStack() as ctx:
        def sb(name, shape, to=ctx):
            return to.enter_context(nc.sbuf_tensor(f"{name}_{nc.next_id()}", shape, F32))
        y = sb("y", [P, KD, SEQ])

        def branch(i, first):
            gated_stage(nc, c, w_in[:, MERGE + i * D:MERGE + (i + 1) * D], W["w_branch"][i], KD, ACT.Sigmoid,
                        y=y, merged=merged, accumulate=not first)

        with ExitStack() as work:
            n = Nsa(nc, work)
            with ExitStack() as early:
                kw = sb("kw", [P, 2, SEQ], early)
                at = NSA_KV
                project(nc, c, w_in, [(NSA_Q, 12, n.qk[:, 0:12, :]), (at + 512, 2, n.qk[:, 12:14, :]), (at + 1024, 2, kw[:, :, :])],
                        [], [(at + 768, 2 * P, n.v_slc[:, :, :]), (at + 1280, 2 * P, n.v_win[:, :, :]),
                             (NSA_GATE, 3 * N_HEADS, n.gate[:, :, :])], gain=W["norm_g"][0])
                with Stage(nc) as together:
                    compress(nc, c, n, n.qk[:, 8:12, :], y, W["cmp_pos"], W["cmp_w1"], W["cmp_w2"], together)
                    spread_keys(nc, c, n, kw, together)
            tiles = sb("tiles", [P, N_HEADS, SEQ], work)
            bias_tiles(nc, c, scratch, N_HEADS, tiles, N_DIM ** 0.5)
            compressed_scores(nc, c, n, tiles)
            nsa_attention(nc, c, n, tiles, y)
        merged = sb("merged", [P, KD, SEQ])
        branch(1, True)
        with ExitStack() as work:
            xg = sb("xg", [P, 16, SEQ], work)
            q, loads = lru_params(nc, work, W)
            project(nc, c, w_in, [(LRU_X, 16, xg[:, :, :])], [], [], loads)
            lru_mixer(nc, c, q, W["lru_w_gates"], xg[:, 0:8, :], xg[:, 8:16, :], y)
        branch(0, False)
        with ExitStack() as work:
            g = Gla(nc, work)
            params = [(g.wa2[:, :], W["gla_wa2"]), (g.ba[:, :], W["gla_ba"].rearrange("(k p) -> p k", p=P)),
                      (g.gain[:, :], W["gla_norm"].rearrange("(k p) -> p k", p=P))]
            project(nc, c, w_in, [(GLA_Q, 8, g.qk[:, :, :]), (GLA_OG, 8, g.og[:, :, :])], [(GLA_LR, 16, g.lr[:, :])],
                    [(GLA_V + 2 * P * i, 2 * P, g.v[:, :, 2 * P * i:2 * P * (i + 1)]) for i in range(4)], params)
            g.k_end, g.k_end_t = sb("k_end", [P, 4, SEQ], work), sb("k_end_t", [P, TT, 4, P], work)
            g.decay = sb("decay", [P, 4, G_CHUNKS], work)
            gla_prepare(nc, c, g)
            gla_scan(nc, c, g, y)
            gla_finish(nc, c, g, y, y)
        branch(2, False)
        mixed = sb("mixed", [P, KD, SEQ])
        project_out(nc, c, W["w_out"], merged, mixed, False)
        add_norm(nc, c, W["norm_g"][1], mixed)
    with ExitStack() as ctx:
        fed = ctx.enter_context(nc.sbuf_tensor("fed", [P, 4, KD, P], F32))
        ffn(nc, c, W["norm_g"][2], W["w_ffn_in"][:, 0:FF], W["w_ffn_in"][:, FF:2 * FF], W["w_ffn_out"], 1.0, raw=fed)
        add_norm(nc, c, W["norm_g"][3], feature_major(fed))




FIRST = ["ffn1_norm_w", "ffn1_w_gate", "ffn1_w_up", "ffn1_w_down", "mix_norm_w", "w_in", "mlstm_gate_bias",
         "mlstm_norm_w", "ssm_conv_w", "ssm_conv_b", "ssm_dt_bias", "ssm_A_log", "ssm_D", "ssm_norm_w",
         "diff_q_norm_w", "diff_k_norm_w", "diff_lambda", "diff_subln_w", "w_out", "ffn2_norm_w", "ffn2_w_gate",
         "ffn2_w_up", "ffn2_w_down"]


def lambda_init(nc, c, layer, now):
    with Stage(nc) as st:
        block = st.block()

        @block.vector
        def _(dve):
            for l in range(LAYERS):
                dve.memset(c.lam_init[:, l:l + 1], 0.8 - 0.6 * float(np.exp(-0.3 * l)))
            dve.drain()
            dve.tensor_copy(now[:, :], c.lam_init[:, bass.ds(layer, 1)])


def program(nc, A, out):
    scratch = nc.dram_tensor("bias_scratch", [DF_HEADS + N_HEADS, BACK + SEQ], F32, kind="Internal").ap()
    with ExitStack() as ctx:
        c = Shared(nc, ctx)
        consts(nc, c)
        with Stage(nc) as together:
            bias_rows(nc, c, A["rel_bias"], DF_HEADS, scratch[0:DF_HEADS], together)
            bias_rows(nc, c, A["rel_table_2"], N_HEADS, scratch[DF_HEADS:], together)
            load_x(nc, c, A["x"], together)
        with ExitStack() as first:
            now = first.enter_context(nc.sbuf_tensor("lam_init_now", [P, 1], F32))
            with nc.Fori(0, LAYERS) as layer:
                L = {name: A[name][layer] for name in FIRST}
                ffn(nc, c, L["ffn1_norm_w"], L["ffn1_w_gate"], L["ffn1_w_up"], L["ffn1_w_down"], 0.5)
                lambda_init(nc, c, layer, now)
                first_mixer(nc, c, L, L["mix_norm_w"], L["w_in"], L["w_out"], scratch[0:DF_HEADS], now[:, 0:1])
                ffn(nc, c, L["ffn2_norm_w"], L["ffn2_w_gate"], L["ffn2_w_up"], L["ffn2_w_down"], 0.5)
        W = {name[:-2]: (ap if name == "rel_table_2" else ap[0]) for name, ap in A.items() if name.endswith("_2")}
        second_block(nc, c, W, scratch[DF_HEADS:])
        store_x(nc, c, out)


_INS = ["x", "ffn1_norm_w", "ffn1_w_gate", "ffn1_w_up", "ffn1_w_down", "mix_norm_w", "w_in", "mlstm_gate_bias",
        "mlstm_norm_w", "ssm_conv_w", "ssm_conv_b", "ssm_dt_bias", "ssm_A_log", "ssm_D", "ssm_norm_w",
        "diff_q_norm_w", "diff_k_norm_w", "diff_lambda", "diff_subln_w", "rel_bias", "w_out", "ffn2_norm_w",
        "ffn2_w_gate", "ffn2_w_up", "ffn2_w_down", "rel_table_2", "norm_g_2", "w_in_2", "conv_w_2", "conv_b_2",
        "lru_w_gates_2", "lru_b_gates_2", "lru_lambda_2", "cmp_pos_2", "cmp_w1_2", "cmp_w2_2", "gla_wa2_2",
        "gla_ba_2", "gla_norm_2", "w_branch_2", "w_out_2", "w_ffn_in_2", "w_ffn_out_2"]
_OUTS = [((1, 512, 1024), "float32")]


def kernel(**inputs):
    import numpy as _np
    import concourse.bacc as _bacc
    from concourse import mybir as _mybir
    from concourse.bass_utils import run_bass_kernel_spmd as _run

    nc = _bacc.Bacc("TRN2", target_bir_lowering=False, num_devices=1)
    arrays, args = {}, {}
    for name in _INS:
        a = _np.ascontiguousarray(inputs[name])
        arrays[f"in_{name}_dram"] = a
        args[name] = nc.dram_tensor(f"in_{name}_dram", a.shape, _mybir.dt.from_np(a.dtype), kind="ExternalInput").ap()
    out = nc.dram_tensor("out_0_dram", _OUTS[0][0], _mybir.dt.from_np(_np.dtype(_OUTS[0][1])), kind="ExternalOutput").ap()
    program(nc, args, out)
    r = _run(nc, [arrays], core_ids=[0])
    return r.results[0]["out_0_dram"]
```
